# Optimizing a Trainium2 kernel written in Bass

```python
import math
import jax, jax.numpy as jnp
from jax import lax
import numpy as np

D_MODEL = 1024
BATCH = 1
SEQ = 256
DEPTH = 1

DN_HEADS = 8
DN_HEAD_DIM = 128
DN_WIDTH = DN_HEADS * DN_HEAD_DIM
DN_CONV = 4
DN_CHUNK = 64
MOBA_HEADS = 8
MOBA_HEAD_DIM = 128
MOBA_WIDTH = MOBA_HEADS * MOBA_HEAD_DIM
MOBA_BLOCK = 256
MOBA_TOPK = 3
MOBA_QCHUNK = 16
REL_BUCKETS = 32
REL_MAX_DIST = 2048
N_BRANCH = 2
SPLITS = (3 * DN_WIDTH, DN_WIDTH, DN_HEADS, DN_HEADS, 3 * MOBA_WIDTH, MOBA_WIDTH, N_BRANCH * D_MODEL)
D_IN_PROJ = sum(SPLITS)
NORM_EPS = 1e-6
NEG_INF = -1e30

kernel_name = 'hybrid_deltanet_moba_block'

def rms_norm(x, w):
    xf = x.astype(jnp.float32)
    y = xf * lax.rsqrt(jnp.mean(xf * xf, axis=-1, keepdims=True) + NORM_EPS)
    return (y * w.astype(jnp.float32)).astype(x.dtype)

def l2_normalize(x):
    return x * lax.rsqrt(jnp.sum(x * x, axis=-1, keepdims=True) + NORM_EPS)

def causal_depthwise_conv(x, w):
    k_width, channels = w.shape
    return lax.conv_general_dilated(
        x, w[:, None, :].astype(x.dtype), window_strides=(1,), padding=[(k_width - 1, 0)],
        dimension_numbers=('NWC', 'WIO', 'NWC'), feature_group_count=channels)

def t5_bucket(dist):
    dist = jnp.maximum(dist, 0)
    max_exact = REL_BUCKETS // 2
    d = jnp.maximum(dist, 1).astype(jnp.float32)
    large = max_exact + (jnp.log(d / max_exact) / math.log(REL_MAX_DIST / max_exact)
                         * (REL_BUCKETS - max_exact)).astype(jnp.int32)
    large = jnp.minimum(large, REL_BUCKETS - 1)
    return jnp.where(dist < max_exact, dist, large)

def gated_delta_rule(q, k, v, g, beta):
    bsz, nh, s, dk = q.shape
    dv = v.shape[-1]
    c = DN_CHUNK
    n = s // c
    q = q * dk ** -0.5
    k_beta = k * beta[..., None]
    v_beta = v * beta[..., None]
    qc = q.reshape(bsz, nh, n, c, dk)
    kc = k.reshape(bsz, nh, n, c, dk)
    kbc = k_beta.reshape(bsz, nh, n, c, dk)
    vbc = v_beta.reshape(bsz, nh, n, c, dv)
    gc = jnp.cumsum(g.reshape(bsz, nh, n, c), axis=-1)
    tri_incl = jnp.tril(jnp.ones((c, c), dtype=bool))
    tri_strict = jnp.tril(jnp.ones((c, c), dtype=bool), -1)
    gdiff = gc[..., :, None] - gc[..., None, :]
    decay = jnp.where(tri_incl, jnp.exp(jnp.where(tri_incl, gdiff, 0.0)), 0.0)
    lower = jnp.where(tri_strict, jnp.einsum('bhnid,bhnjd->bhnij', kbc, kc) * decay, 0.0)
    eye = jnp.eye(c, dtype=jnp.float32)
    t_mat = lax.linalg.triangular_solve(eye + lower, jnp.broadcast_to(eye, lower.shape),
                                        left_side=True, lower=True, unit_diagonal=True)
    u = jnp.einsum('bhnij,bhnje->bhnie', t_mat, vbc)
    w = jnp.einsum('bhnij,bhnjd->bhnid', t_mat, kbc * jnp.exp(gc)[..., None])
    attn_intra = jnp.where(tri_incl, jnp.einsum('bhnid,bhnjd->bhnij', qc, kc) * decay, 0.0)
    q_dec = qc * jnp.exp(gc)[..., None]
    g_last = gc[..., -1]
    k_dec = kc * jnp.exp(g_last[..., None] - gc)[..., None]

    def step(state, xs):
        q_i, k_i, u_i, w_i, a_i, gl_i = xs
        v_new = u_i - jnp.einsum('bhcd,bhde->bhce', w_i, state)
        o = jnp.einsum('bhcd,bhde->bhce', q_i, state) + jnp.einsum('bhij,bhje->bhie', a_i, v_new)
        state = state * jnp.exp(gl_i)[..., None, None] + jnp.einsum('bhcd,bhce->bhde', k_i, v_new)
        return state, o

    xs = tuple(jnp.moveaxis(t, 2, 0) for t in (q_dec, k_dec, u, w, attn_intra, g_last))
    state0 = jnp.zeros((bsz, nh, dk, dv), dtype=jnp.float32)
    _, o = lax.scan(step, state0, xs)
    return jnp.moveaxis(o, 0, 2).reshape(bsz, nh, s, dv)

def moba_attention(q, k, v, rel_bias):
    bsz, nh, s, dh = q.shape
    blk = MOBA_BLOCK
    s_pad = -(-s // blk) * blk
    pad = ((0, 0), (0, 0), (0, s_pad - s), (0, 0))
    q, k, v = (jnp.pad(t.astype(jnp.float32), pad) for t in (q, k, v))
    q = q * dh ** -0.5
    nb = s_pad // blk
    k_blocks = k.reshape(bsz, nh, nb, blk, dh)
    v_blocks = v.reshape(bsz, nh, nb, blk, dh)
    q_blk = jnp.arange(s_pad, dtype=jnp.int32) // blk
    past = jnp.arange(nb, dtype=jnp.int32)[None, :] < q_blk[:, None]
    gate_scores = jnp.einsum('bhsd,bhnd->bhsn', q, k_blocks.mean(axis=3))
    gate_scores = jnp.where(past, gate_scores, NEG_INF)
    topk = min(MOBA_TOPK, nb)
    _, top_idx = lax.top_k(gate_scores, topk)
    sel_valid = jnp.arange(topk, dtype=jnp.int32)[None, :] < q_blk[:, None]
    bi = jnp.arange(bsz)[:, None, None, None]
    hi = jnp.arange(nh)[None, :, None, None]
    bias_hb = rel_bias.astype(jnp.float32).T
    offs = jnp.arange(blk, dtype=jnp.int32)
    cq = MOBA_QCHUNK

    def chunk(ci):
        start = ci * cq
        qc = lax.dynamic_slice_in_dim(q, start, cq, axis=2)
        idx = lax.dynamic_slice_in_dim(top_idx, start, cq, axis=2)
        valid = lax.dynamic_slice_in_dim(sel_valid, start, cq, axis=0)
        qpos = start + jnp.arange(cq, dtype=jnp.int32)
        k_sel = k_blocks[bi, hi, idx]
        v_sel = v_blocks[bi, hi, idx]
        s_past = jnp.einsum('bhcd,bhcrkd->bhcrk', qc, k_sel)
        kpos_past = idx[..., None] * blk + offs
        s_past = s_past + bias_hb[hi[..., None], t5_bucket(qpos[:, None, None] - kpos_past)]
        s_past = jnp.where(valid[:, :, None], s_past, NEG_INF).reshape(bsz, nh, cq, topk * blk)
        own_start = (start // blk) * blk
        k_own = lax.dynamic_slice_in_dim(k, own_start, blk, axis=2)
        v_own = lax.dynamic_slice_in_dim(v, own_start, blk, axis=2)
        dist_own = qpos[:, None] - (own_start + offs)[None, :]
        s_own = jnp.einsum('bhcd,bhkd->bhck', qc, k_own) + bias_hb[:, t5_bucket(dist_own)][None]
        s_own = jnp.where(dist_own >= 0, s_own, NEG_INF)
        p = jax.nn.softmax(jnp.concatenate([s_past, s_own], axis=-1), axis=-1)
        p_past = p[..., :topk * blk].reshape(bsz, nh, cq, topk, blk)
        p_own = p[..., topk * blk:]
        return (jnp.einsum('bhcrk,bhcrkd->bhcd', p_past, v_sel)
                + jnp.einsum('bhck,bhkd->bhcd', p_own, v_own))

    out = lax.map(chunk, jnp.arange(s_pad // cq))
    out = jnp.moveaxis(out, 0, 2).reshape(bsz, nh, s_pad, dh)
    return out[:, :, :s]

def hybrid_layer(x, norm_pre_w, w_in, b_gate, conv_w, dn_a_log, dn_dt_bias, dn_onorm_w,
                 rel_bias, w_branch, w_out, norm_post_w):
    bsz, s, d = x.shape
    h = rms_norm(x, norm_pre_w)
    proj = jnp.einsum('bsd,df->bsf', h, w_in)
    cuts = []
    acc = 0
    for size in SPLITS[:-1]:
        acc += size
        cuts.append(acc)
    qkv_a, z_a, beta_a, dec_a, qkv_b, z_b, gate_logits = jnp.split(proj, cuts, axis=-1)

    qkv_a = jax.nn.silu(causal_depthwise_conv(qkv_a.astype(jnp.float32), conv_w.astype(jnp.float32)))
    qa, ka, va = jnp.split(qkv_a, 3, axis=-1)
    heads_a = lambda t: t.reshape(bsz, s, DN_HEADS, DN_HEAD_DIM).transpose(0, 2, 1, 3)
    qa = l2_normalize(heads_a(qa))
    ka = l2_normalize(heads_a(ka))
    va = heads_a(va)
    beta = jax.nn.sigmoid(beta_a.astype(jnp.float32)).transpose(0, 2, 1)
    g = (-jnp.exp(dn_a_log.astype(jnp.float32))
         * jax.nn.softplus(dec_a.astype(jnp.float32) + dn_dt_bias.astype(jnp.float32))).transpose(0, 2, 1)
    oa = gated_delta_rule(qa, ka, va, g, beta).transpose(0, 2, 1, 3)
    oa = rms_norm(oa, dn_onorm_w).reshape(bsz, s, DN_WIDTH)
    ya = (oa * jax.nn.silu(z_a.astype(jnp.float32))).astype(x.dtype)

    qb, kb, vb = jnp.split(qkv_b, 3, axis=-1)
    heads_b = lambda t: t.reshape(bsz, s, MOBA_HEADS, MOBA_HEAD_DIM).transpose(0, 2, 1, 3)
    ob = moba_attention(heads_b(qb), heads_b(kb), heads_b(vb), rel_bias)
    ob = ob.transpose(0, 2, 1, 3).reshape(bsz, s, MOBA_WIDTH)
    yb = (ob * jax.nn.silu(z_b.astype(jnp.float32))).astype(x.dtype)

    gates = jax.nn.sigmoid((gate_logits + b_gate).astype(jnp.float32)).reshape(bsz, s, N_BRANCH, d)
    pa = jnp.einsum('bsf,fd->bsd', ya, w_branch[0]).astype(jnp.float32)
    pb = jnp.einsum('bsf,fd->bsd', yb, w_branch[1]).astype(jnp.float32)
    merged = (gates[:, :, 0] * pa + gates[:, :, 1] * pb).astype(x.dtype)
    out = jnp.einsum('bsd,de->bse', merged, w_out)
    return x + rms_norm(out, norm_post_w)

def setup_inputs(seed: int = 0) -> dict:
    key = jax.random.key(seed)
    ks = jax.random.split(key, 12)
    f32 = jnp.float32
    x = jax.random.normal(ks[0], (BATCH, SEQ, D_MODEL), f32)
    norm_pre_w = 1.0 + 0.1 * jax.random.normal(ks[1], (D_MODEL,), f32)
    w_in = jax.random.normal(ks[2], (D_MODEL, D_IN_PROJ), f32) * D_MODEL ** -0.5
    b_gate = 0.1 * jax.random.normal(ks[3], (N_BRANCH * D_MODEL,), f32)
    conv_w = jax.random.normal(ks[4], (DN_CONV, 3 * DN_WIDTH), f32) * DN_CONV ** -0.5
    dn_a_log = jnp.log(jax.random.uniform(ks[5], (DN_HEADS,), f32, minval=1.0, maxval=16.0))
    dt = jnp.exp(jax.random.uniform(ks[6], (DN_HEADS,), f32, minval=math.log(1e-3), maxval=math.log(1e-1)))
    dn_dt_bias = dt + jnp.log(-jnp.expm1(-dt))
    dn_onorm_w = 1.0 + 0.1 * jax.random.normal(ks[7], (DN_HEAD_DIM,), f32)
    rel_bias = 0.5 * jax.random.normal(ks[8], (REL_BUCKETS, MOBA_HEADS), f32)
    w_branch = jax.random.normal(ks[9], (N_BRANCH, DN_WIDTH, D_MODEL), f32) * DN_WIDTH ** -0.5
    w_out = jax.random.normal(ks[10], (D_MODEL, D_MODEL), f32) * D_MODEL ** -0.5
    norm_post_w = 1.0 + 0.1 * jax.random.normal(ks[11], (D_MODEL,), f32)
    return {'x': x, 'norm_pre_w': norm_pre_w, 'w_in': w_in, 'b_gate': b_gate, 'conv_w': conv_w,
            'dn_a_log': dn_a_log, 'dn_dt_bias': dn_dt_bias, 'dn_onorm_w': dn_onorm_w,
            'rel_bias': rel_bias, 'w_branch': w_branch, 'w_out': w_out, 'norm_post_w': norm_post_w}

def reference(x, norm_pre_w, w_in, b_gate, conv_w, dn_a_log, dn_dt_bias, dn_onorm_w,
              rel_bias, w_branch, w_out, norm_post_w):
    h = x
    for _ in range(DEPTH):
        h = hybrid_layer(h, norm_pre_w, w_in, b_gate, conv_w, dn_a_log, dn_dt_bias, dn_onorm_w,
                         rel_bias, w_branch, w_out, norm_post_w)
    return h


_drawn_inputs = setup_inputs


def setup_inputs(seed=0):
    import zlib

    import numpy as np

    out = dict(_drawn_inputs(seed))
    spreads = {}
    factors = {}
    for name, (base, spread) in spreads.items():
        noise = np.random.default_rng([zlib.crc32(name.encode()), seed]).standard_normal(out[name].shape)
        drawn = base * np.exp(spread * noise) if base else spread * noise
        out[name] = __import__('jax').numpy.asarray(drawn.astype(out[name].dtype))
    for name, factor in factors.items():
        out[name] = (out[name] * factor).astype(out[name].dtype)
    return out
```

```python
from contextlib import ExitStack

import numpy as np
import concourse.bass as bass
from concourse import mybir

F32 = mybir.dt.float32
F32R = mybir.dt.float32r
ALU = mybir.AluOpType
ACT = mybir.ActivationFunctionType
AX_X = mybir.AxisListType.X

P = 128
D = 1024
SEQ = 256
NC = SEQ // P
KT = D // P
HEADS = 8
EPS = 1e-6
NEG_INF = -1e30
BUCKETS, MAX_DIST = 32, 2048
SCALE = float(P) ** -0.5
CONV = 4

SLOTS = 4
PER_HEAD = 8
GATES0 = HEADS * PER_HEAD
BRANCH0 = GATES0 + 2 * KT
OUT0 = BRANCH0 + 2 * KT
TILES = OUT0 + KT
LEAD = 2

COL_Q, COL_K, COL_V, COL_ZA = 0, D, 2 * D, 3 * D
COL_BD = 4 * D
COL_B = COL_BD + 2 * HEADS
TILE_COLS = [COL_K, COL_Q, COL_V, COL_B + D, COL_B, COL_B + 2 * D, COL_ZA, COL_B + 3 * D]
COL_GATE = COL_B + 4 * D

R_GATE, R_PRE, R_ON, ROWS = CONV * 24, CONV * 24 + 16, CONV * 24 + 24, CONV * 24 + 25

LEVELS = [2, 4, 8, 16, 32, 64]
C_ID, C_ONE, C_TRI, C_E, C_M1, C_ML = (P * i for i in (0, 1, 2, 3, 5, 6))
C_ALL = C_ML + P * len(LEVELS)
BIAS_W = 384


def shape_constants():
    i = np.arange(P)
    row, col = i[:, None], i[None, :]
    parts = [row == col, np.ones((P, P)), row <= col, row < col, row <= col, (col == row + 1) & (row % 2 == 0)]
    for b in LEVELS:
        parts.append((row // (2 * b) == col // (2 * b)) & (row // b == col // b + 1))
    consts = np.concatenate([m.astype(np.float32) for m in parts], axis=1)
    dist = 255 - np.arange(BIAS_W)
    half = BUCKETS // 2
    far = np.maximum(dist, 1).astype(np.float32)
    large = half + (np.log(far / np.float32(half)) / np.float32(np.log(MAX_DIST / half))
                    * np.float32(BUCKETS - half)).astype(np.int32)
    bucket = np.where(dist < half, np.maximum(dist, 0), np.minimum(large, BUCKETS - 1))
    onehot = np.zeros((BUCKETS + 1, BIAS_W), np.float32)
    onehot[bucket, np.arange(BIAS_W)] = 1.0
    onehot[:, dist < 0] = 0.0
    onehot[BUCKETS, dist < 0] = 1.0
    return np.ascontiguousarray(consts), onehot


def counts(value):
    return not isinstance(value, int) or value > 0


def build(nc, x, norm_pre_w, w_in, b_gate, conv_w, dn_a_log, dn_dt_bias, dn_onorm_w, rel_bias, w_branch, w_out,
          norm_post_w, consts, onehot, out):
    with ExitStack() as ctx:
        def sb(name, shape, dt=F32):
            return ctx.enter_context(nc.sbuf_tensor(name, shape, dt))

        def sem(name):
            return ctx.enter_context(nc.semaphore(name))

        bank = [ctx.enter_context(nc.psum_tensor(f"bank{i}", [P, 512], F32)) for i in range(8)]
        bA, bB, bC, bD, bE, bF = bank[2:]

        raw = sb("raw", [P, SLOTS, D])
        w_hi = sb("w_hi", [P, SLOTS, D], F32R)
        w_lo = sb("w_lo", [P, SLOTS, D], F32R)
        xin = sb("xin", [P, NC, D])
        xn = res = xin
        cst = sb("cst", [P, C_ALL])
        relb = sb("relb", [BUCKETS + 1, HEADS])
        vec = sb("vec", [P, ROWS])
        vec_half = sb("vec_half", [P, ROWS])
        wbd = sb("wbd", [P, KT, 2 * HEADS])
        alog = sb("alog", [P, HEADS])
        dtb = sb("dtb", [P, HEADS])
        h_hi = sb("h_hi", [P, KT, SEQ], F32R)
        h_lo = sb("h_lo", [P, KT, SEQ], F32R)
        bias = sb("bias", [P, HEADS, BIAS_W])
        tiny = sb("tiny", [P, 32])
        bd = sb("bd", [P, NC, 2 * HEADS])
        gt = sb("gt", [P, 10, NC, HEADS])
        tab = sb("tab", [P, 11, HEADS])
        taps = sb("taps", [P, 2, 3, CONV])
        acc = sb("acc", [P, 3, SEQ])
        tacc = sb("tacc", [P, 3, SEQ])
        act = sb("act", [P, 2, 3, SEQ])
        bT = sb("bT", [P, 2, 3, SEQ])
        tz = sb("tz", [P, 2, SEQ])
        gz = sb("gz", [P, 2, 2, SEQ])
        th = sb("th", [P, 2 * KT, SEQ])
        h32 = th[:, 0:KT, :]
        hc2 = sb("hc", [P, 2, 11])
        sq = sb("sq", [P, 2, SEQ])
        ssq = sb("ssq", [P, 4])
        rn2 = sb("rn", [P, 2, 4])
        dm = sb("dm", [P, 256])
        ex = sb("ex", [P, 256])
        e4 = sb("e4", [P, 512])
        kk = sb("kk", [P, 4, P])
        vb2 = sb("vb", [P, 2, NC, P])
        kdec2 = sb("kdec", [P, 2, P])
        kkT2 = sb("kkT", [P, 2, 4, P])
        la2 = sb("la", [P, 2, 4, P])
        u_tmp = sb("u_tmp", [P, NC, P])
        tu2 = sb("tu", [P, 2, 4, P])
        xl2 = sb("xl", [P, 2, NC, P])
        q1 = sb("q1", [P, 2, P])
        gza = sb("gza", [P, 2, SEQ])
        v0 = sb("v0", [P, P])
        s1 = sb("s1", [P, P])
        r1 = sb("r1", [P, P])
        qs = sb("qs", [P, P])
        v1 = sb("v1", [P, P])
        oo = sb("oo", [P, NC, P])
        junk = sb("junk", [P, 512])
        so = sb("so", [P, 8])
        on = sb("on", [P, NC, P])
        sc = sb("sc", [P, BIAS_W])
        mx = sb("mx", [P, 8])
        pt = sb("pt", [P, BIAS_W])
        vtok = sb("vtok", [P, NC, P])
        y32 = sb("y32", [P, 2, SEQ])
        y_hi = sb("y_hi", [P, 2, HEADS, SEQ], F32R)
        y_lo = sb("y_lo", [P, 2, HEADS, SEQ], F32R)
        m2, m32 = acc[:, 0:2, :], acc[:, 2, :]
        post = bT[:].rearrange("p a t n -> p (a t n)")[:, 0:D]
        m_hi, m_lo = h_hi, h_lo
        hot, brow, rows = sc[0:BUCKETS + 1, :], pt[0:HEADS, :], r1
        bias_rows = nc.dram_tensor("bias_rows", [HEADS, P, BIAS_W + 1], F32, kind="Internal").ap()

        ident = cst[:, C_ID:C_ID + P]
        ones = cst[:, C_ONE:C_ONE + P]
        tri = cst[:, C_TRI:C_TRI + P]

        def both(col):
            return cst[:, col:col + P].rearrange("p (a n) -> p a n", a=1).to_broadcast([P, NC, P])

        s_T = sem("s_T")
        s_act = sem("s_act")
        s_bT = sem("s_bT")
        s_bd = sem("s_bd")
        s_bd_p = sem("s_bd_p")
        s_bd_w = sem("s_bd_w")
        s_bias_p = sem("s_bias_p")
        s_brow = sem("s_brow")
        s_cst = sem("s_cst")
        s_d_p = sem("s_d_p")
        s_dm = sem("s_dm")
        s_e4 = sem("s_e4")
        s_ex = sem("s_ex")
        s_f = sem("s_f")
        s_g = sem("s_g")
        s_ga = sem("s_ga")
        s_gate_th = sem("s_gate_th")
        s_gb = sem("s_gb")
        s_gc = sem("s_gc")
        s_gc_p = sem("s_gc_p")
        s_gv = sem("s_gv")
        s_gz = sem("s_gz")
        s_h32 = sem("s_h32")
        s_hT = sem("s_hT")
        s_h_hi = sem("s_h_hi")
        s_h_lo = sem("s_h_lo")
        s_hc = sem("s_hc")
        s_hi = sem("s_hi")
        s_hot = sem("s_hot")
        s_keep = sem("s_keep")
        s_kk = sem("s_kk")
        s_kkT = sem("s_kkT")
        s_ks_p = sem("s_ks_p")
        s_kt_p = sem("s_kt_p")
        s_kv = sem("s_kv")
        s_la = sem("s_la")
        s_la_p = sem("s_la_p")
        s_lo = sem("s_lo")
        s_loaded = sem("s_loaded")
        s_m2 = sem("s_m2")
        s_m32 = sem("s_m32")
        s_m_hi = sem("s_m_hi")
        s_m_lo = sem("s_m_lo")
        s_mx = sem("s_mx")
        s_nmx = sem("s_nmx")
        s_o0 = sem("s_o0")
        s_o0_p = sem("s_o0_p")
        s_o1 = sem("s_o1")
        s_o1_p = sem("s_o1_p")
        s_o_f = sem("s_o_f")
        s_o_n = sem("s_o_n")
        s_o_p = sem("s_o_p")
        s_o_r = sem("s_o_r")
        s_o_sq = sem("s_o_sq")
        s_o_t = sem("s_o_t")
        s_on = sem("s_on")
        s_ot_p = sem("s_ot_p")
        s_out = sem("s_out")
        s_pexp = sem("s_pexp")
        s_pn = sem("s_pn")
        s_post = sem("s_post")
        s_pre_c = sem("s_pre_c")
        s_pre_r = sem("s_pre_r")
        s_pre_sq = sem("s_pre_sq")
        s_pre_x = sem("s_pre_x")
        s_pt = sem("s_pt")
        s_pt_p = sem("s_pt_p")
        s_pv_p = sem("s_pv_p")
        s_qs = sem("s_qs")
        s_qs_p = sem("s_qs_p")
        s_r1 = sem("s_r1")
        s_relb = sem("s_relb")
        s_rn = sem("s_rn")
        s_rows = sem("s_rows")
        s_rsum = sem("s_rsum")
        s_s1 = sem("s_s1")
        s_s1_p = sem("s_s1_p")
        s_sc = sem("s_sc")
        s_sc_p = sem("s_sc_p")
        s_small = sem("s_small")
        s_so = sem("s_so")
        s_sq = sem("s_sq")
        s_ssq = sem("s_ssq")
        s_ssq_p = sem("s_ssq_p")
        s_stored = sem("s_stored")
        s_tab = sem("s_tab")
        s_tanh = sem("s_tanh")
        s_tap = sem("s_tap")
        s_tap0 = sem("s_tap0")
        s_taps = sem("s_taps")
        s_tile = sem("s_tile")
        s_tt_p = sem("s_tt_p")
        s_tu = sem("s_tu")
        s_tz = sem("s_tz")
        s_u2 = sem("s_u2")
        s_v0 = sem("s_v0")
        s_v0_p = sem("s_v0_p")
        s_v1 = sem("s_v1")
        s_v1_p = sem("s_v1_p")
        s_vb = sem("s_vb")
        s_vec = sem("s_vec")
        s_vec_p = sem("s_vec_p")
        s_vt_p = sem("s_vt_p")
        s_vtok = sem("s_vtok")
        s_x = sem("s_x")
        s_x_in = sem("s_x_in")
        s_x_p = sem("s_x_p")
        s_ya32 = sem("s_ya32")
        s_yb32 = sem("s_yb32")
        s_yhi_a = sem("s_yhi_a")
        s_yhi_b = sem("s_yhi_b")
        s_ylo_a = sem("s_ylo_a")
        s_ylo_b = sem("s_ylo_b")
        s_raw = [sem(f"s_raw{i}") for i in range(SLOTS)]
        block = ctx.enter_context(nc.Block())

        def one(a):
            return a.rearrange("p (a n) -> p a n", a=1)

        @block.sync
        def _(sp):
            sp.dma_start(xin[:], x[0].rearrange("(c p) d -> p c d", p=P)).then_inc(s_x_in, 16)
            sp.dma_start(cst[:], consts).then_inc(s_cst, 16)
            sp.dma_start(rows[0:R_GATE, :], conv_w.rearrange("k (t p) -> (k t) p", p=P)).then_inc(s_rows, 16)
            sp.dma_start(rows[R_GATE:R_PRE, :], b_gate.rearrange("(t p) -> t p", p=P)).then_inc(s_rows, 16)
            sp.dma_start(rows[R_PRE:R_ON, :], norm_pre_w.rearrange("(t p) -> t p", p=P)).then_inc(s_rows, 16)
            sp.dma_start(rows[R_ON:ROWS, :], dn_onorm_w.rearrange("(t p) -> t p", p=P)).then_inc(s_rows, 16)

            def load(n, src):
                if load.slot % 2 == 0:
                    if counts(2 * (n - SLOTS + 2)):
                        sp.wait_ge(s_lo, 2 * (n - SLOTS + 2))
                return sp.dma_start(raw[:, load.slot, :].rearrange("p (k n) -> p k n", k=src.shape[1]), src)

            def load_at(n, t, src):
                load.slot = t % SLOTS
                load(n, src).then_inc(s_raw[t % SLOTS], 16)

            def w_tile(col):
                return w_in[:, bass.ds(col, P)].rearrange("(k p) n -> p k n", p=P)

            def head_loads(h, tiles):
                for t in tiles:
                    load_at(h * PER_HEAD + t, t, w_tile(h * P + TILE_COLS[t]))

            head_loads(0, range(SLOTS))
            sp.dma_start(wbd[:], w_in[:, COL_BD:COL_B].rearrange("(k p) n -> p k n", p=P)).then_inc(s_bd_w, 16)
            sp.dma_start(alog[:], dn_a_log.rearrange("(a n) -> a n", a=1).to_broadcast([P, HEADS])).then_inc(s_small, 16)
            sp.dma_start(dtb[:], dn_dt_bias.rearrange("(a n) -> a n", a=1).to_broadcast([P, HEADS])).then_inc(s_small, 16)
            sp.dma_start(hot, onehot).then_inc(s_hot, 16)
            sp.dma_start(relb[0:BUCKETS, :], rel_bias).then_inc(s_hot, 16)
            head_loads(0, range(SLOTS, PER_HEAD))
            with sp.Fori(1, HEADS) as h:
                head_loads(h, range(PER_HEAD))
            with sp.Fori(0, 2) as i:
                for t in range(PER_HEAD):
                    load_at(GATES0 + i * PER_HEAD + t, t, w_tile(COL_GATE + (i * PER_HEAD + t) * P))
            sp.wait_ge(s_ylo_b, HEADS + 1)
            sp.dma_start(post, norm_post_w.rearrange("(a n) -> a n", a=1).to_broadcast([P, D])).then_inc(s_post, 16)
            with sp.Fori(0, KT // 2) as i:
                for t in range(4):
                    load_at(BRANCH0 + i * 4 + t, t, w_branch[t % 2][:, bass.ds((i * 2 + t // 2) * P, P)]
                            .rearrange("(k p) n -> p k n", p=P))
            for k in range(KT):
                load_at(OUT0 + k, OUT0 + k, w_out[k * P:(k + 1) * P, :].rearrange("p (k n) -> p k n", k=1))
            for c in range(NC):
                load_at(TILES + c, TILES + c, x[0, c * P:(c + 1) * P, :].rearrange("p (k n) -> p k n", k=1))
            for c in range(NC):
                sp.wait_ge(s_o_f, c + 1)
                sp.dma_start(out[0, c * P:(c + 1) * P, :], res[:, c, :]).then_inc(s_out, 16)
            sp.wait_ge(s_out, 16 * NC)

        @block.gpsimd
        def _(pool):
            pool.memset(relb[BUCKETS:BUCKETS + 1, :], NEG_INF).then_inc(s_relb, 1)
            pool.wait_ge(s_relb, 1)
            pool.memset(tiny[:, 8:12], -0.5).then_inc(s_pre_r, 1)
            pool.wait_ge(s_pre_r, 1)
            pool.memset(tiny[:, 12:14], EPS * P).then_inc(s_pre_c, 1)
            pool.wait_ge(s_pre_c, 1)
            pool.wait_ge(s_pre_sq, 2)
            pool.tensor_scalar(tiny[:, 0:2], tiny[:, 0:2], 1.0 / D, EPS, ALU.mult, ALU.add).then_inc(s_pre_r, 1)
            pool.wait_ge(s_pre_r, 2)
            pool.tensor_tensor(tiny[:, 2:4], tiny[:, 0:2], tiny[:, 8:10], ALU.pow).then_inc(s_pre_r, 1)
            pool.wait_ge(s_pre_r, 3)
            pool.wait_ge(s_brow, 1)
            pool.dma_start(bias_rows[:, :, 0:BIAS_W],
                           brow.rearrange("h (a n) -> h a n", a=1).to_broadcast([HEADS, P, BIAS_W])).then_inc(s_stored, 16)
            pool.wait_ge(s_stored, 16)
            for c0, c1, at in ((0, 256, 0), (128, 256, 256)):
                src = bass.AP(bias_rows.tensor, P - 1 + c0, [[BIAS_W, P], [P * (BIAS_W + 1), HEADS], [1, c1 - c0]])
                pool.dma_start(bias[:, :, at:at + c1 - c0], src).then_inc(s_loaded, 16)

            def front(h, p):
                if isinstance(h, int) and h == 0:
                    pool.wait_ge(s_vec, 1)
                src = vec[:, 0:R_GATE].rearrange("p (k t h) -> p t k h", k=CONV, h=HEADS)[:, :, :, bass.ds(h, 1)]
                pool.tensor_copy(taps[:, p, :, :].rearrange("p t (k a) -> p t k a", a=1), src).then_inc(s_taps, 1)
                pool.wait_ge(s_taps, h + 1)

            def stage_a(g, p):
                hc, rn = hc2[:, p], rn2[:, p]
                if counts(g):
                    pool.wait_ge(s_ylo_a, g)
                pool.tensor_copy(hc.rearrange("p (k a) -> p k a", a=1), tab[:, :, bass.ds(g, 1)]).then_inc(s_hc, 1)
                pool.wait_ge(s_hc, g + 1)
                pool.wait_ge(s_ssq, g + 1)
                pool.tensor_tensor(rn, ssq[:], tiny[:, 8:12], ALU.pow).then_inc(s_rn, 1)
                pool.wait_ge(s_rn, g + 1)
                pool.wait_ge(s_ex, g + 1)
                for j in range(2):
                    pool.tensor_tensor(e4[:, 256 * j:256 * j + 256].rearrange("p (c n) -> p c n", c=NC),
                                       ex[:].rearrange("p (c n) -> p c n", c=NC), both(C_E + P * j),
                                       ALU.mult).then_inc(s_e4, 1)
                    pool.wait_ge(s_e4, 2 * g + j + 1)

            def stage_b(g, p):
                rn = rn2[:, p]
                pool.wait_ge(s_so, 2 * g + 2)
                pool.tensor_tensor(so[:, 2:4], so[:, 0:2], rn[:, 2:4], ALU.mult).then_inc(s_f, 1)
                pool.wait_ge(s_f, 5 * g + 1)
                pool.tensor_tensor(so[:, 4:6], so[:, 2:4], rn[:, 2:4], ALU.mult).then_inc(s_f, 1)
                pool.wait_ge(s_f, 5 * g + 2)
                pool.tensor_tensor(so[:, 2:4], so[:, 4:6], tiny[:, 12:14], ALU.add).then_inc(s_f, 1)
                pool.wait_ge(s_f, 5 * g + 3)
                pool.tensor_tensor(so[:, 4:6], so[:, 2:4], tiny[:, 8:10], ALU.pow).then_inc(s_f, 1)
                pool.wait_ge(s_f, 5 * g + 4)
                pool.tensor_tensor(so[:, 6:8], so[:, 4:6], rn[:, 2:4], ALU.mult).then_inc(s_f, 1)
                pool.wait_ge(s_f, 5 * g + 5)

            front(0, 0)
            pool.wait_ge(s_tab, 3)
            front(1, 1)
            stage_a(0, 0)
            with pool.Fori(2, HEADS - 1, 2) as h:
                front(h, 0)
                stage_a(h - 1, 1)
                stage_b(h - 2, 0)
                front(h + 1, 1)
                stage_a(h, 0)
                stage_b(h - 1, 1)
            stage_a(HEADS - 1, 1)
            stage_b(HEADS - 2, 0)
            stage_b(HEADS - 1, 1)
            for c in range(NC):
                pool.wait_ge(s_o_sq, 2 * c + 2)
                pool.tensor_tensor(tiny[:, 24 + c:25 + c], tiny[:, 16 + 2 * c:17 + 2 * c],
                                   tiny[:, 17 + 2 * c:18 + 2 * c], ALU.add).then_inc(s_o_t, 1)
                pool.wait_ge(s_o_t, 3 * c + 1)
                pool.tensor_scalar(tiny[:, 26 + c:27 + c], tiny[:, 24 + c:25 + c], 0.25 / D, EPS, ALU.mult,
                                   ALU.add).then_inc(s_o_t, 1)
                pool.wait_ge(s_o_t, 3 * c + 2)
                pool.tensor_tensor(tiny[:, 28 + c:29 + c], tiny[:, 26 + c:27 + c], tiny[:, 8:9],
                                   ALU.pow).then_inc(s_o_t, 1)
                pool.wait_ge(s_o_t, 3 * c + 3)
                pool.tensor_scalar(tiny[:, 30 + c:31 + c], tiny[:, 28 + c:29 + c], 0.5, 0.0, ALU.mult,
                                   ALU.add).then_inc(s_o_r, 1)
                pool.wait_ge(s_o_r, c + 1)

        @block.scalar
        def _(sa):
            ac = nc.scalar.activation

            def split_hi(n, t):
                sa.wait_ge(s_raw[t % SLOTS], 16 * (n // SLOTS + 1) if isinstance(n, int) else split_hi.turn)
                if counts(n - SLOTS + 1):
                    sa.wait_ge(s_tile, n - SLOTS + 1)
                nc.scalar.copy(w_hi[:, t % SLOTS, :], raw[:, t % SLOTS, :]).then_inc(s_hi, 1)

            def lead(h, t):
                split_hi.turn = 16 * (h * (PER_HEAD // SLOTS) + (t + LEAD) // SLOTS + 1)
                split_hi(h * PER_HEAD + t + LEAD, t + LEAD)

            sa.wait_ge(s_x_in, 16)
            for c in range(NC):
                ac(bias[:].rearrange("p h n -> p (h n)")[:, 0:D], xin[:, c, :], ACT.Square, accum_out=tiny[:, c:c + 1]).then_inc(s_pre_sq, 1)
                sa.wait_ge(s_pre_sq, c + 1)
            sa.wait_ge(s_pre_r, 3)
            for c in range(NC):
                ac(xn[:, c, :], xin[:, c, :], ACT.Copy, scale=tiny[:, 2 + c:3 + c]).then_inc(s_pre_x, 1)
            split_hi(0, 0)
            split_hi(1, 1)
            sa.wait_ge(s_h32, KT)
            ac(h_hi[:], h32, ACT.Copy).then_inc(s_h_hi, 1)
            sa.wait_ge(s_bd, 1)
            ac(gt[:, 0], bd[:, :, 0:HEADS], ACT.Tanh, scale=0.5).then_inc(s_ga, 1)
            sa.wait_ge(s_gv, 2)
            ac(gt[:, 2], gt[:, 1], ACT.Abs).then_inc(s_ga, 1)
            sa.wait_ge(s_ga, 2)
            ac(gt[:, 3], gt[:, 2], ACT.Exp, scale=-1.0).then_inc(s_ga, 1)
            sa.wait_ge(s_small, 32)
            ac(tiny[:, 16:24], alog[:], ACT.Exp).then_inc(s_ga, 1)
            sa.wait_ge(s_gv, 3)
            ac(gt[:, 5], gt[:, 4], ACT.Ln).then_inc(s_ga, 1)

            def front(h, p, t):
                ps = bank[t % 2][:, 0:SEQ]
                sa.wait_ge(s_tile, h * PER_HEAD + t + 1)
                if t < 3:
                    w = (1, 0, 2)[t]
                    if t == 0:
                        sa.wait_ge(s_taps, h + 1)
                        if counts(h):
                            sa.wait_ge(s_act, h)
                    ac(acc[:, t, :], ps, ACT.Copy, scale=taps[:, p, w, CONV - 1:CONV]).then_inc(s_tap0, 1)
                    if t == 2:
                        sa.wait_ge(s_tap, 9 * h + 9)
                        ac(tacc[:], acc[:], ACT.Tanh, scale=0.5).then_inc(s_tanh, 1)
                elif t < 6:
                    if t == 3:
                        if counts(h):
                            sa.wait_ge(s_ylo_b, h)
                    nc.scalar.copy(bT[:, p, t - 3, :], ps).then_inc(s_bT, 1)
                    if t == 4:
                        sa.wait_ge(s_act, h + 1)
                        if counts(h):
                            sa.wait_ge(s_ssq_p, h)
                        ac(sq[:], act[:, p, 0:2, :], ACT.Square).then_inc(s_sq, 1)
                else:
                    if counts(2 * (h - 1) + t - 5):
                        sa.wait_ge(s_gz, 2 * (h - 1) + t - 5)
                    ac(tz[:, t - 6, :], ps, ACT.Tanh, scale=0.5).then_inc(s_tz, 1)

            def gate_front(i, t):
                sa.wait_ge(s_tile, GATES0 + i * PER_HEAD + t + 1)
                g = i * PER_HEAD + t
                ac(th[:, g, :], bank[t % 2][:, 0:SEQ], ACT.Tanh, scale=0.5,
                   bias=vec_half[:, R_GATE + g:R_GATE + g + 1]).then_inc(s_gate_th, 1)

            def stage_a(g, p, s):
                hc, vb, kdec, kkT, tu = hc2[:, p], vb2[:, p], kdec2[:, p], kkT2[:, p], tu2[:, p]
                if s == 0:
                    if counts(g):
                        sa.wait_ge(s_ylo_a, g)
                    sa.wait_ge(s_gz, 2 * g + 1)
                    nc.scalar.copy(q1[:, p, :], act[:, p, 1, P:2 * P]).then_inc(s_keep, 1)
                    nc.scalar.copy(gza[:, p, :], gz[:, p, 0, :]).then_inc(s_keep, 1)
                    sa.wait_ge(s_dm, 2 * g + 2)
                    ac(ex[:], dm[:], ACT.Exp).then_inc(s_ex, 1)
                elif s == 1:
                    sa.wait_ge(s_vt_p, g + 1)
                    nc.scalar.copy(vtok[:], bB[:, 0:256].rearrange("p (c n) -> p c n", c=NC)).then_inc(s_vtok, 1)
                    sa.wait_ge(s_kk, 4 * g + 2)
                    for c in range(NC):
                        ac(vb[:, c, :], bA[:, 256 + P * c:384 + P * c], ACT.Copy, scale=hc[:, 2 + c:3 + c]) \
                            .then_inc(s_vb, 1)
                    ac(kdec, kk[:, 0, :], ACT.Copy, scale=hc[:, 8:9]).then_inc(s_vb, 1)
                elif s == 2:
                    sa.wait_ge(s_kt_p, g + 1)
                    nc.scalar.copy(kkT, bB[:].rearrange("p (c n) -> p c n", c=4)).then_inc(s_kkT, 1)
                    sa.wait_ge(s_nmx, g + 1)
                    ac(sc[:, 0:256], sc[:, 0:256], ACT.Exp, bias=mx[:, 2:3], accum_out=mx[:, 4:5]).then_inc(s_pexp, 1)
                    ac(sc[:, 256:384], sc[:, 256:384], ACT.Exp, bias=mx[:, 3:4],
                       accum_out=mx[:, 5:6]).then_inc(s_pexp, 1)
                elif s == 4:
                    sa.wait_ge(s_tt_p, g + 1)
                    nc.scalar.copy(tu[:, 0:2, :], bB[:, 0:256].rearrange("p (c n) -> p c n", c=NC)).then_inc(s_T, 1)
                    sa.wait_ge(s_pt_p, g + 1)
                    nc.scalar.copy(pt[:], bC[:, 0:BIAS_W]).then_inc(s_pt, 1)
                elif s == 6:
                    sa.wait_ge(s_yb32, g + 1)
                    nc.scalar.copy(y_hi[:, 1, bass.ds(g, 1), :], one(y32[:, 1, :])).then_inc(s_yhi_b, 1)

            def stage_b(g, p, s):
                hc = hc2[:, p]
                if s == 5:
                    sa.wait_ge(s_v0_p, g + 1)
                    nc.scalar.copy(v0[:], bD[:, 0:P]).then_inc(s_v0, 1)
                elif s == 6:
                    sa.wait_ge(s_s1_p, g + 1)
                    nc.scalar.copy(s1[:], bE[:, 0:P]).then_inc(s_s1, 1)
                elif s == 7:
                    sa.wait_ge(s_qs_p, g + 1)
                    ac(qs[:], bD[:, P:2 * P], ACT.Copy, scale=hc[:, 7:8]).then_inc(s_qs, 1)
                    sa.wait_ge(s_o0, g + 1)
                    ac(junk[:, 0:P], oo[:, 0, :], ACT.Square, scale=P ** -0.5, accum_out=so[:, 0:1]).then_inc(s_so, 1)
                elif s == 8:
                    sa.wait_ge(s_v1_p, g + 1)
                    nc.scalar.copy(v1[:], bE[:, 0:P]).then_inc(s_v1, 1)
                elif s == 9:
                    sa.wait_ge(s_o1, g + 1)
                    ac(junk[:, P:2 * P], oo[:, 1, :], ACT.Square, scale=P ** -0.5,
                       accum_out=so[:, 1:2]).then_inc(s_so, 1)
                elif s == 10:
                    sa.wait_ge(s_f, 5 * g + 5)
                    for c in range(NC):
                        ac(on[:, c, :], oo[:, c, :], ACT.Copy, scale=so[:, 6 + c:7 + c]).then_inc(s_on, 1)
                elif s == 11:
                    sa.wait_ge(s_ya32, g + 1)
                    nc.scalar.copy(y_hi[:, 0, bass.ds(g, 1), :], one(y32[:, 0, :])).then_inc(s_yhi_a, 1)

            def iteration(h, p, stages):
                for t in range(PER_HEAD):
                    for s in range(3 * t, 3 * t + 3):
                        if s % 2 == 0 and stages >= 1:
                            stage_a(h - 1, 1 - p, s // 2)
                        elif s % 2 and stages == 2:
                            stage_b(h - 2, p, s // 2)
                        if s % 3 == 0 and t >= 1:
                            front(h, p, t - 1)
                        if s % 3 == 1:
                            lead(h, t)
                front(h, p, PER_HEAD - 1)

            def decays():
                sa.wait_ge(s_gc, 2)
                ac(tab[:, 7, :], tab[:, 5, :], ACT.Exp).then_inc(s_tab, 1)
                ac(tab[:, 8, :], gt[:, 9, 0], ACT.Exp).then_inc(s_tab, 1)

            iteration(0, 0, 0)
            decays()
            iteration(1, 1, 1)
            with sa.Fori(2, HEADS - 1, 2) as h:
                iteration(h, 0, 2)
                iteration(h + 1, 1, 2)
            for i in range(2):
                for t in range(PER_HEAD):
                    for s in range(3 * t, 3 * t + 3):
                        if s % 2 == 0 and i == 0:
                            stage_a(HEADS - 1, 1, s // 2)
                        elif s % 2:
                            stage_b(HEADS - 2 + i, i, s // 2)
                        if s % 3 == 0 and t >= 1:
                            gate_front(i, t - 1)
                        if s % 3 == 1:
                            lead(HEADS + i, t)
                gate_front(i, PER_HEAD - 1)

            sa.sem_inc(s_m_hi, 1)
            with sa.Fori(0, KT // 2) as i:
                for t in range(4):
                    n = BRANCH0 + i * 4 + t + LEAD
                    split_hi.turn = 16 * (BRANCH0 // SLOTS + i + (t + LEAD) // SLOTS + 1)
                    split_hi(n, t + LEAD)
                    if t % 2:
                        d = i * 2 + t // 2
                        sa.wait_ge(s_m32, d + 2)
                        nc.scalar.copy(m_hi[:, bass.ds(d, 1), :], m32.rearrange("p (a n) -> p a n", a=1)).then_inc(s_m_hi, 1)
            for k in range(KT - LEAD):
                split_hi(OUT0 + k + LEAD, k + LEAD)
            for c in range(NC):
                sa.wait_ge(s_o_p, c + 1)
                for e in range(2):
                    ac(junk[:, 0:512], bank[2 + 2 * c + e][:], ACT.Square,
                       accum_out=tiny[:, 16 + 2 * c + e:17 + 2 * c + e]).then_inc(s_o_sq, 1)
                    sa.wait_ge(s_o_sq, 2 * c + e + 1)

        @block.vector
        def _(ve):
            v = nc.vector

            def split_lo(n, t, part):
                ve.wait_ge(s_hi, n + 1)
                if part == 0:
                    if counts(n - SLOTS + 1):
                        ve.wait_ge(s_tile, n - SLOTS + 1)
                half = slice(part * (D // 2), (part + 1) * (D // 2))
                v.tensor_tensor(w_lo[:, t % SLOTS, half], raw[:, t % SLOTS, half],
                                w_hi[:, t % SLOTS, half].bitcast(F32), ALU.subtract).then_inc(s_lo, 1)

            def lead(h, t, part):
                split_lo(h * PER_HEAD + t + LEAD, t + LEAD, part)

            ve.wait_ge(s_vec_p, 1)
            v.tensor_copy(vec[:], bank[7][:, 0:ROWS]).then_inc(s_vec, 1)
            ve.wait_ge(s_vec, 1)
            v.tensor_scalar(vec_half[:], vec[:], 0.5, None, ALU.mult).then_inc(s_vec, 1)
            for k in range(KT):
                ve.wait_ge(s_hT, k + 1)
                v.tensor_scalar(h32[:, k, :], bank[k][:, 0:SEQ], vec[:, R_PRE + k:R_PRE + k + 1], None,
                                ALU.mult).then_inc(s_h32, 1)
            for n in range(LEAD):
                for part in range(2):
                    split_lo(n, n, part)
            ve.wait_ge(s_h_hi, 1)
            v.tensor_tensor(h_lo[:], h32, h_hi[:].bitcast(F32), ALU.subtract).then_inc(s_h_lo, 1)
            ve.wait_ge(s_bias_p, 1)
            v.tensor_copy(brow, bank[3][0:HEADS, 0:BIAS_W]).then_inc(s_brow, 1)
            ve.wait_ge(s_bd_p, 1)
            v.tensor_copy(bd[:], bank[2][:, 0:2 * NC * HEADS].rearrange("p (c n) -> p c n", c=NC)).then_inc(s_bd, 1)
            ve.wait_ge(s_bd, 1)
            ve.wait_ge(s_small, 32)
            for c in range(NC):
                v.tensor_tensor(gt[:, 1, c], bd[:, c, HEADS:], dtb[:], ALU.add).then_inc(s_gv, 1)
            ve.wait_ge(s_ga, 3)
            v.tensor_scalar(gt[:, 4], gt[:, 3], 1.0, None, ALU.add).then_inc(s_gv, 1)
            step = [3]

            def gate_step(ins):
                step[0] += 1
                ins.then_inc(s_gv, 1)
                ve.wait_ge(s_gv, step[0])

            ve.wait_ge(s_ga, 5)
            ve.wait_ge(s_gv, 3)
            gate_step(v.tensor_scalar(gt[:, 6], gt[:, 4], -1.0, None, ALU.add))
            gate_step(v.tensor_scalar(gt[:, 7], gt[:, 6], 0.0, None, ALU.is_equal))
            gate_step(v.tensor_tensor(gt[:, 6], gt[:, 6], gt[:, 7], ALU.add))
            gate_step(v.tensor_tensor(gt[:, 5], gt[:, 5], gt[:, 7], ALU.add))
            gate_step(v.reciprocal(gt[:, 6], gt[:, 6]))
            gate_step(v.tensor_tensor(gt[:, 5], gt[:, 5], gt[:, 3], ALU.mult))
            gate_step(v.tensor_tensor(gt[:, 5], gt[:, 5], gt[:, 6], ALU.mult))
            gate_step(v.scalar_tensor_tensor(out=gt[:, 8], in0=gt[:, 1], scalar=0.0, in1=gt[:, 5], op0=ALU.max, op1=ALU.add))
            for c in range(NC):
                gate_step(v.scalar_tensor_tensor(out=tab[:, 9 + c, :], in0=gt[:, 8, c], scalar=-1.0,
                                                 in1=tiny[:, 16:24], op0=ALU.mult, op1=ALU.mult))
            gate_step(v.tensor_scalar(tab[:, 0:2, :], gt[:, 0], 0.5, 0.5, ALU.mult, ALU.add))
            gate_step(v.tensor_scalar(tab[:, 2:4, :], gt[:, 0], 0.25, 0.25, ALU.mult, ALU.add))
            v.tensor_copy(gt[:, 9, 1], gt[:, 8, 1]).then_inc(s_g, 1)

            def decays():
                ve.wait_ge(s_gc_p, 1)
                v.tensor_copy(tab[:, 4:6, :], bC[:, 0:16].rearrange("p (c n) -> p c n", c=NC)).then_inc(s_gc, 1)
                ve.wait_ge(s_gc, 1)
                v.tensor_tensor(gt[:, 9, 0], bC[:, 16:24], tab[:, 4, :], ALU.subtract).then_inc(s_gc, 1)
                ve.wait_ge(s_tab, 2)
                v.tensor_scalar(tab[:, 6, :], tab[:, 7, :], -1.0, None, ALU.mult).then_inc(s_tab, 1)
                ve.wait_ge(s_loaded, 32)
                ve.sem_inc(s_ylo_a, 1)
                ve.sem_inc(s_ylo_b, 1)

            def front(h, p, t):
                ps = bank[t % 2]
                if t < 3:
                    w = (1, 0, 2)[t]
                    ve.wait_ge(s_tap0, 3 * h + t + 1)
                    for i in range(1, CONV):
                        if i > 1:
                            ve.wait_ge(s_tap, 9 * h + 3 * t + i - 1)
                        v.scalar_tensor_tensor(out=acc[:, t, i:], in0=ps[:, 0:SEQ - i],
                                               scalar=taps[:, p, w, CONV - 1 - i:CONV - i], in1=acc[:, t, i:],
                                               op0=ALU.mult, op1=ALU.add).then_inc(s_tap, 1)
                elif t == 3:
                    ve.wait_ge(s_tanh, h + 1)
                    if counts(h - 1):
                        ve.wait_ge(s_la_p, h - 1)
                        ve.wait_ge(s_keep, 2 * (h - 1))
                    v.scalar_tensor_tensor(out=act[:, p], in0=tacc[:], scalar=1.0, in1=acc[:], op0=ALU.add,
                                           op1=ALU.mult).then_inc(s_act, 1)
                elif t >= 6:
                    ve.wait_ge(s_tz, 2 * h + t - 5)
                    v.scalar_tensor_tensor(out=gz[:, p, t - 6, :], in0=tz[:, t - 6, :], scalar=1.0, in1=ps[:, 0:SEQ],
                                           op0=ALU.add, op1=ALU.mult).then_inc(s_gz, 1)

            def stage_a(g, p, s):
                hc, rn, la, tu, xl = hc2[:, p], rn2[:, p], la2[:, p], tu2[:, p], xl2[:, p]
                if s == 0:
                    ve.wait_ge(s_gb, g + 1)
                    for c in range(NC):
                        v.tensor_scalar(dm[:, P * c:P * c + P], bB[:, P * c:P * c + P], hc[:, 4 + c:5 + c], 0.0,
                                        ALU.subtract, ALU.min).then_inc(s_dm, 1)
                    ve.wait_ge(s_ssq_p, g + 1)
                    v.tensor_scalar(ssq[:], bC[:, 0:4], 4 * EPS, None, ALU.add).then_inc(s_ssq, 1)
                elif s == 1:
                    ve.wait_ge(s_rn, g + 1)
                    ve.wait_ge(s_kv, g + 1)
                    for c in range(NC):
                        v.tensor_scalar(kk[:, c, :], bA[:, P * c:P * c + P], rn[:, c:c + 1], None,
                                        ALU.mult).then_inc(s_kk, 1)
                    ve.wait_ge(s_kk, 4 * g + 2)
                    for c in range(NC):
                        v.tensor_scalar(kk[:, 2 + c, :], kk[:, c, :], hc[:, c:c + 1], None,
                                        ALU.mult).then_inc(s_kk, 1)
                    ve.wait_ge(s_sc_p, g + 1)
                    v.scalar_tensor_tensor(out=sc[:], in0=bC[:, 0:BIAS_W], scalar=SCALE,
                                           in1=bias[:, bass.ds(g, 1), :].rearrange("p a n -> p (a n)"),
                                           op0=ALU.mult, op1=ALU.add).then_inc(s_sc, 1)
                    ve.wait_ge(s_sc, g + 1)
                    v.tensor_reduce(mx[:, 0:1], sc[:, 0:256], AX_X, ALU.max).then_inc(s_mx, 1)
                    v.tensor_reduce(mx[:, 1:2], sc[:, 256:384], AX_X, ALU.max).then_inc(s_mx, 1)
                    ve.wait_ge(s_mx, 2 * g + 2)
                    v.tensor_scalar(mx[:, 2:4], mx[:, 0:2], -1.0, None, ALU.mult).then_inc(s_nmx, 1)
                elif s == 3:
                    ve.wait_ge(s_pexp, 2 * g + 2)
                    v.reciprocal(mx[:, 6:8], mx[:, 4:6]).then_inc(s_rsum, 1)
                    ve.wait_ge(s_la_p, g + 1)
                    ve.wait_ge(s_e4, 2 * g + 2)
                    v.tensor_tensor(la.rearrange("p c n -> p (c n)"), bA[:], e4[:], ALU.mult).then_inc(s_la, 1)
                    ve.wait_ge(s_la, g + 1)
                    v.tensor_tensor(u_tmp[:], la[:, 0:2, :], both(C_M1), ALU.mult).then_inc(s_u2, 1)
                    ve.wait_ge(s_u2, 2 * g + 1)
                    v.tensor_tensor(tu[:, 2:4, :], both(C_ID), u_tmp[:], ALU.subtract).then_inc(s_u2, 1)
                    ve.wait_ge(s_rsum, g + 1)
                    v.tensor_scalar(sc[:, 0:256], sc[:, 0:256], mx[:, 6:7], None, ALU.mult).then_inc(s_pn, 1)
                    v.tensor_scalar(sc[:, 256:384], sc[:, 256:384], mx[:, 7:8], None, ALU.mult).then_inc(s_pn, 1)
                elif s >= 5:
                    level_step(g, p, (s - 5) // 2, s % 2 == 1, bB, bC)
                    if s == 5:
                        ve.wait_ge(s_pv_p, g + 1)
                        v.scalar_tensor_tensor(out=y32[:, 1, :], in0=bA[:, 0:SEQ], scalar=0.5, in1=gz[:, p, 1, :],
                                               op0=ALU.mult, op1=ALU.mult).then_inc(s_yb32, 1)
                    if s == 7:
                        ve.wait_ge(s_yhi_b, g + 1)
                        v.tensor_tensor(y_lo[:, 1, bass.ds(g, 1), :], one(y32[:, 1, :]),
                                        y_hi[:, 1, bass.ds(g, 1), :].bitcast(F32), ALU.subtract).then_inc(s_ylo_b, 1)

            def level_step(g, p, lv, first, x_bank, d_bank):
                tu, xl = tu2[:, p], xl2[:, p]
                if first:
                    ve.wait_ge(s_x_p, 6 * g + lv + 1)
                    v.tensor_tensor(xl, x_bank[:, 0:256].rearrange("p (c n) -> p c n", c=NC), both(C_ML + P * lv),
                                    ALU.mult).then_inc(s_x, 1)
                else:
                    ve.wait_ge(s_d_p, 6 * g + lv + 1)
                    at = 0 if lv < 5 else 2
                    view = tu[:, at:4, :].rearrange("p c n -> p (c n)")
                    v.tensor_tensor(view, view, d_bank[:, P * at:512], ALU.subtract).then_inc(s_tu, 1)

            def stage_b(g, p, s):
                hc, vb = hc2[:, p], vb2[:, p]
                if s < 5:
                    level_step(g, p, 3 + (s + 1) // 2, s % 2 == 1, bD, bE)
                elif s == 6:
                    ve.wait_ge(s_o0_p, g + 1)
                    v.tensor_copy(oo[:, 0, :], bF[:, 0:P]).then_inc(s_o0, 1)
                elif s == 7:
                    ve.wait_ge(s_ks_p, g + 1)
                    v.scalar_tensor_tensor(out=r1[:], in0=bE[:, 256:384], scalar=hc[:, 6:7], in1=vb[:, 1, :],
                                           op0=ALU.mult, op1=ALU.add).then_inc(s_r1, 1)
                elif s == 9:
                    ve.wait_ge(s_o1_p, g + 1)
                    ve.wait_ge(s_qs, g + 1)
                    v.tensor_tensor(oo[:, 1, :], bF[:, P:2 * P], qs[:], ALU.add).then_inc(s_o1, 1)
                elif s == 10:
                    ve.wait_ge(s_ot_p, g + 1)
                    v.scalar_tensor_tensor(out=y32[:, 0, :], in0=bD[:, 0:SEQ], scalar=vec_half[:, R_ON:R_ON + 1],
                                           in1=gza[:, p, :], op0=ALU.mult, op1=ALU.mult).then_inc(s_ya32, 1)
                elif s == 11:
                    ve.wait_ge(s_yhi_a, g + 1)
                    v.tensor_tensor(y_lo[:, 0, bass.ds(g, 1), :], one(y32[:, 0, :]),
                                    y_hi[:, 0, bass.ds(g, 1), :].bitcast(F32), ALU.subtract).then_inc(s_ylo_a, 1)

            def iteration(h, p, stages):
                for t in range(PER_HEAD):
                    for s in range(3 * t, 3 * t + 3):
                        if s % 2 == 0 and stages >= 1:
                            stage_a(h - 1, 1 - p, s // 2)
                        elif s % 2 and stages == 2:
                            stage_b(h - 2, p, s // 2)
                        if s % 3 == 0 and t >= 1:
                            front(h, p, t - 1)
                        if s % 3 >= 1:
                            lead(h, t, s % 3 - 1)
                front(h, p, PER_HEAD - 1)

            iteration(0, 0, 0)
            decays()
            iteration(1, 1, 1)
            with ve.Fori(2, HEADS - 1, 2) as h:
                iteration(h, 0, 2)
                iteration(h + 1, 1, 2)
            for i in range(2):
                for t in range(PER_HEAD):
                    for s in range(3 * t, 3 * t + 3):
                        if s % 2 == 0 and i == 0:
                            stage_a(HEADS - 1, 1, s // 2)
                        elif s % 2:
                            stage_b(HEADS - 2 + i, i, s // 2)
                        if s % 3 >= 1:
                            lead(HEADS + i, t, s % 3 - 1)

            ve.sem_inc(s_m32, 1)
            with ve.Fori(0, KT // 2) as i:
                for t in range(4):
                    for part in range(2):
                        split_lo(BRANCH0 + i * 4 + t + LEAD, t + LEAD, part)
                    d = i * 2 + t // 2
                    ve.wait_ge(s_tile, BRANCH0 + i * 4 + t + 1)
                    if t % 2 == 0:
                        ve.wait_ge(s_m_hi, d + 1)
                    v.scalar_tensor_tensor(out=one(m2[:, t % 2, :]), in0=th[:, bass.ds((t % 2) * KT + d, 1), :], scalar=1.0,
                                           in1=one(bank[t % 2][:, 0:SEQ]), op0=ALU.add, op1=ALU.mult).then_inc(s_m2, 1)
                    if t % 2:
                        ve.wait_ge(s_m2, 2 * (d + 1))
                        v.tensor_tensor(m32, m2[:, 0, :], m2[:, 1, :], ALU.add).then_inc(s_m32, 1)
                        ve.wait_ge(s_m_hi, d + 2)
                        v.tensor_tensor(m_lo[:, bass.ds(d, 1), :], one(m32), m_hi[:, bass.ds(d, 1), :].bitcast(F32),
                                        ALU.subtract).then_inc(s_m_lo, 1)
            for k in range(KT - LEAD):
                for part in range(2):
                    split_lo(OUT0 + k + LEAD, k + LEAD, part)
            ve.wait_ge(s_post, 16)
            for c in range(NC):
                ve.wait_ge(s_o_r, c + 1)
                for e in range(2):
                    cols = slice(512 * e, 512 * e + 512)
                    v.scalar_tensor_tensor(out=res[:, c, cols], in0=bank[2 + 2 * c + e][:], scalar=tiny[:, 30 + c:31 + c],
                                           in1=post[:, cols], op0=ALU.mult, op1=ALU.mult).then_inc(s_o_n, 1)
                ve.wait_ge(s_o_n, 2 * c + 2)
                ve.wait_ge(s_raw[c], 16 * (TILES // SLOTS + 1))
                v.tensor_tensor(res[:, c, :], res[:, c, :], raw[:, c, :], ALU.add).then_inc(s_o_f, 1)

        @block.tensor
        def _(pe):
            mm = nc.tensor.matmul
            tp = nc.tensor.transpose

            pe.wait_ge(s_rows, 64)
            pe.wait_ge(s_cst, 16)
            tp(bank[7][:, 0:ROWS], rows[0:ROWS, :], ident[0:ROWS, 0:ROWS]).then_inc(s_vec_p, 1)
            for k in range(KT):
                if k == 0:
                    pe.wait_ge(s_pre_x, NC)
                if k == 7:
                    pe.wait_ge(s_vec, 1)
                for c in range(NC):
                    last = tp(bank[k][:, P * c:P * c + P], xn[:, c, P * k:P * k + P], ident)
                last.then_inc(s_hT, 1)
            pe.wait_ge(s_bd_w, 16)
            pe.wait_ge(s_h32, KT)
            for c in range(NC):
                for k in range(KT):
                    last = mm(bank[2][:, 16 * c:16 * c + 16], h32[:, k, P * c:P * c + P], wbd[:, k, :],
                              start=k == 0, stop=k == KT - 1)
            last.then_inc(s_bd_p, 1)
            pe.wait_ge(s_hot, 32)
            pe.wait_ge(s_relb, 1)
            mm(bank[3][0:HEADS, 0:BIAS_W], relb[:], hot, start=True, stop=True).then_inc(s_bias_p, 1)
            pe.wait_ge(s_h_hi, 1)
            pe.wait_ge(s_h_lo, 1)

            def third(n, t, part, right_hi, right_lo):
                ps = bank[t % 2][:, 0:SEQ]
                slot = t % SLOTS
                if part == 0:
                    pe.wait_ge(s_hi, n + 1)
                    pe.wait_ge(s_lo, 2 * n + 2)
                for i in range(8 * part, 8 * part + 8):
                    k, which = i // 3, i % 3
                    w = (w_lo if which == 2 else w_hi)[:, slot, P * k:P * k + P]
                    r = (right_lo if which == 1 else right_hi)[:, k, :]
                    last = mm(ps, w, r, start=i == 0, stop=i == 23)
                if part == 2:
                    last.then_inc(s_tile, 1)

            def bank_free(h, t):
                if t < 2:
                    if counts(2 * (h - 1) + t + 1):
                        pe.wait_ge(s_gz, 2 * (h - 1) + t + 1)
                elif t < 5:
                    pe.wait_ge(s_tap, 9 * h + 3 * (t - 1))
                else:
                    pe.wait_ge(s_bT, 3 * h + t - 4)

            def stage_a(g, p, s):
                hc, vb, kkT, la, tu = hc2[:, p], vb2[:, p], kkT2[:, p], la2[:, p], tu2[:, p]
                k_T, q_T, v_T = (act[:, p, j, :] for j in range(3))
                if s == 0:
                    pe.wait_ge(s_act, g + 1)
                    if counts(g):
                        pe.wait_ge(s_ylo_b, g + 1)
                        pe.wait_ge(s_x, 6 * g - 2)
                        pe.wait_ge(s_ylo_a, g)
                    for j, a in enumerate((k_T, v_T)):
                        for c in range(NC):
                            last = tp(bA[:, 256 * j + P * c:256 * j + P * c + P], a[:, P * c:P * c + P], ident)
                    last.then_inc(s_kv, 1)
                    pe.wait_ge(s_sq, g + 1)
                    for j in range(4):
                        last = mm(bC[:, j:j + 1], sq[:, j // 2, P * (j % 2):P * (j % 2) + P], ones[:, 0:1],
                                  start=True, stop=True)
                    last.then_inc(s_ssq_p, 1)
                    pe.wait_ge(s_hc, g + 1)
                    for c in range(NC):
                        last = mm(bB[:, P * c:P * c + P], hc[:, 9 + c:10 + c].to_broadcast([P, P]), tri,
                                  start=True, stop=True)
                    last.then_inc(s_gb, 1)
                elif s == 1:
                    pe.wait_ge(s_bT, 3 * g + 3)
                    pe.wait_ge(s_ssq, g + 1)
                    kb_T, qb_T, vb_T = (bT[:, p, j, :] for j in range(3))
                    mm(bC[:, 0:256], qb_T[:, P:2 * P], kb_T, start=True, stop=True)
                    mm(bC[:, 256:384], qb_T[:, 0:P], kb_T[:, 0:P], start=True, stop=True).then_inc(s_sc_p, 1)
                    pe.wait_ge(s_dm, 2 * g + 2)
                    for c in range(NC):
                        last = tp(bB[:, P * c:P * c + P], vb_T[:, P * c:P * c + P], ident)
                    last.then_inc(s_vt_p, 1)
                elif s == 2:
                    pe.wait_ge(s_kk, 4 * g + 4)
                    pe.wait_ge(s_vtok, g + 1)
                    for j in range(4):
                        last = tp(bB[:, P * j:P * j + P], kk[:, j, :], ident)
                    last.then_inc(s_kt_p, 1)
                elif s == 3:
                    pe.wait_ge(s_kkT, g + 1)
                    pe.wait_ge(s_vb, 3 * g + 2)
                    for c in range(NC):
                        mm(bA[:, P * c:P * c + P], kkT[:, c, :], kkT[:, 2 + c, :], start=True, stop=True)
                    for c in range(NC):
                        last = mm(bA[:, 256 + P * c:384 + P * c], kkT[:, c, :], q_T[:, P * c:P * c + P],
                                  start=True, stop=True)
                    last.then_inc(s_la_p, 1)
                elif s == 4:
                    pe.wait_ge(s_u2, 2 * g + 2)
                    for c in range(NC):
                        last = tp(bB[:, P * c:P * c + P], tu[:, 2 + c, :], ident)
                    last.then_inc(s_tt_p, 1)
                    pe.wait_ge(s_pn, 2 * g + 2)
                    tp(bC[:, 0:P], sc[:, 256:384], ident)
                    tp(bC[:, P:2 * P], sc[:, 0:P], ident)
                    tp(bC[:, 2 * P:3 * P], sc[:, P:2 * P], ident).then_inc(s_pt_p, 1)
                else:
                    if s == 5:
                        pe.wait_ge(s_T, g + 1)
                    level_step(g, p, (s - 5) // 2, s % 2 == 1, bB, bC)
                    if s == 5:
                        pe.wait_ge(s_pt, g + 1)
                        mm(bA[:, 0:256], vtok[:, 0, :], pt[:, 0:256], start=True, stop=False, skip_group_check=True)
                        mm(bA[:, P:2 * P], vtok[:, 1, :], pt[:, 256:384], start=False, stop=True,
                           skip_group_check=True).then_inc(s_pv_p, 1)

            def level_step(g, p, lv, first, x_bank, d_bank):
                la, tu, xl = la2[:, p], tu2[:, p], xl2[:, p]
                if first:
                    if lv:
                        pe.wait_ge(s_tu, 6 * g + lv)
                    for c in range(NC):
                        last = mm(x_bank[:, P * c:P * c + P], la[:, c, :], tu[:, c, :], start=True, stop=True)
                    last.then_inc(s_x_p, 1)
                else:
                    pe.wait_ge(s_x, 6 * g + lv + 1)
                    if lv < 5:
                        for c in range(NC):
                            mm(d_bank[:, P * c:P * c + P], tu[:, 2 + c, :], xl[:, c, :], start=True, stop=True)
                    for c in range(NC):
                        last = mm(d_bank[:, 256 + P * c:384 + P * c], xl[:, c, :], tu[:, 2 + c, :], start=True, stop=True)
                    last.then_inc(s_d_p, 1)

            def stage_b(g, p, s):
                vb, kdec, kkT, la, tu = vb2[:, p], kdec2[:, p], kkT2[:, p], la2[:, p], tu2[:, p]
                if s < 5:
                    if s == 0:
                        pe.wait_ge(s_ylo_a, g + 1)
                    level_step(g, p, 3 + (s + 1) // 2, s % 2 == 1, bD, bE)
                elif s == 5:
                    pe.wait_ge(s_tu, 6 * g + 6)
                    mm(bD[:, 0:P], tu[:, 2, :], vb[:, 0, :], start=True, stop=True).then_inc(s_v0_p, 1)
                elif s == 6:
                    pe.wait_ge(s_v0, g + 1)
                    mm(bE[:, 0:P], kdec, v0[:], start=True, stop=True).then_inc(s_s1_p, 1)
                    mm(bF[:, 0:P], la[:, 2, :], v0[:], start=True, stop=True).then_inc(s_o0_p, 1)
                elif s == 7:
                    pe.wait_ge(s_s1, g + 1)
                    pe.wait_ge(s_keep, 2 * g + 1)
                    mm(bE[:, 256:384], kkT[:, 3, :], s1[:], start=True, stop=True).then_inc(s_ks_p, 1)
                    mm(bD[:, P:2 * P], q1[:, p, :], s1[:], start=True, stop=True).then_inc(s_qs_p, 1)
                elif s == 8:
                    pe.wait_ge(s_r1, g + 1)
                    mm(bE[:, 0:P], tu[:, 3, :], r1[:], start=True, stop=True).then_inc(s_v1_p, 1)
                elif s == 9:
                    pe.wait_ge(s_v1, g + 1)
                    pe.wait_ge(s_o0, g + 1)
                    mm(bF[:, P:2 * P], la[:, 3, :], v1[:], start=True, stop=True).then_inc(s_o1_p, 1)
                elif s == 10:
                    pe.wait_ge(s_on, 2 * g + 2)
                    for c in range(NC):
                        last = tp(bD[:, P * c:P * c + P], on[:, c, :], ident)
                    last.then_inc(s_ot_p, 1)

            def iteration(h, p, stages):
                for t in range(PER_HEAD):
                    for s in range(3 * t, 3 * t + 3):
                        if s % 2 == 0 and stages >= 1:
                            stage_a(h - 1, 1 - p, s // 2)
                        elif s % 2 and stages == 2:
                            stage_b(h - 2, p, s // 2)
                        if s % 3 == 0:
                            bank_free(h, t)
                        third(h * PER_HEAD + t, t, s % 3, h_hi, h_lo)

            iteration(0, 0, 0)
            pe.wait_ge(s_g, 1)
            mm(bC[:, 0:16], tri, tab[:, 9:11, :], start=True, stop=True)
            mm(bC[:, 16:32], ones, tab[:, 9:11, :], start=True, stop=True).then_inc(s_gc_p, 1)
            pe.wait_ge(s_gc, 2)
            iteration(1, 1, 1)
            with pe.Fori(2, HEADS - 1, 2) as h:
                iteration(h, 0, 2)
                iteration(h + 1, 1, 2)
            for i in range(2):
                for t in range(PER_HEAD):
                    for s in range(3 * t, 3 * t + 3):
                        if s % 2 == 0 and i == 0:
                            stage_a(HEADS - 1, 1, s // 2)
                        elif s % 2:
                            stage_b(HEADS - 2 + i, i, s // 2)
                        if s % 3 == 0:
                            if i == 0 and t < 2:
                                pe.wait_ge(s_gz, 2 * (HEADS - 1) + t + 1)
                            else:
                                pe.wait_ge(s_gate_th, PER_HEAD * i + t - 1)
                        third(GATES0 + i * PER_HEAD + t, t, s % 3, h_hi, h_lo)
            pe.wait_ge(s_gate_th, 2 * KT)
            pe.wait_ge(s_ylo_a, HEADS + 1)
            pe.wait_ge(s_ylo_b, HEADS + 1)

            with pe.Fori(0, KT // 2) as i:
                for t in range(4):
                    if t >= 2:
                        pe.wait_ge(s_m2, i * 4 + t - 1)
                    else:
                        pe.wait_ge(s_m32, i * 2 + 1)
                    for part in range(3):
                        third(BRANCH0 + i * 4 + t, t, part, y_hi[:, t % 2], y_lo[:, t % 2])
            pe.wait_ge(s_m2, 2 * KT)
            for k in range(KT):
                pe.wait_ge(s_hi, OUT0 + k + 1)
                pe.wait_ge(s_lo, 2 * (OUT0 + k) + 2)
                pe.wait_ge(s_m_lo, k + 1)
                slot = (OUT0 + k) % SLOTS
                for c in range(NC):
                    for m, w in ((m_hi, w_hi), (m_hi, w_lo), (m_lo, w_hi)):
                        for e in range(2):
                            last = mm(bank[2 + 2 * c + e][:], m[:, k, P * c:P * c + P], w[:, slot, 512 * e:512 * e + 512],
                                      start=k == 0 and m is m_hi and w is w_hi, stop=k == KT - 1 and m is m_lo)
                    if k == KT - 1:
                        last.then_inc(s_o_p, 1)
                if k < KT - 1:
                    nxt = last.then_inc(s_tile, 1)


_INS = ['x', 'norm_pre_w', 'w_in', 'b_gate', 'conv_w', 'dn_a_log', 'dn_dt_bias', 'dn_onorm_w', 'rel_bias',
        'w_branch', 'w_out', 'norm_post_w']


def kernel(**inputs):
    import concourse.bacc as _bacc
    from concourse.bass_utils import run_bass_kernel_spmd as _run

    nc = _bacc.Bacc("TRN2", target_bir_lowering=False, num_devices=1)
    consts, onehot = shape_constants()
    arrays, args = {}, []
    for name, a in [(n, np.ascontiguousarray(inputs[n])) for n in _INS] + [("consts", consts), ("onehot", onehot)]:
        arrays[f"in_{name}_dram"] = a
        args.append(nc.dram_tensor(f"in_{name}_dram", a.shape, mybir.dt.from_np(a.dtype), kind="ExternalInput").ap())
    args.append(nc.dram_tensor("out_0_dram", (1, SEQ, D), F32, kind="ExternalOutput").ap())
    build(nc, *args)
    r = _run(nc, [arrays], core_ids=[0])
    return r.results[0]["out_0_dram"]
```

```python
from contextlib import ExitStack

import numpy as np
import concourse.bass as bass
from concourse import mybir

F32 = mybir.dt.float32
F32R = mybir.dt.float32r
ALU = mybir.AluOpType
ACT = mybir.ActivationFunctionType
AX_X = mybir.AxisListType.X

P = 128
D = 1024
SEQ = 256
NC = SEQ // P
KT = D // P
HEADS = 8
EPS = 1e-6
NEG_INF = -1e30
BUCKETS, MAX_DIST = 32, 2048
SCALE = float(P) ** -0.5
CONV = 4

SLOTS = 4
PER_HEAD = 8
GATES0 = HEADS * PER_HEAD
BRANCH0 = GATES0 + 2 * KT
OUT0 = BRANCH0 + 2 * KT
TILES = OUT0 + KT
LEAD = 2

COL_Q, COL_K, COL_V, COL_ZA = 0, D, 2 * D, 3 * D
COL_BD = 4 * D
COL_B = COL_BD + 2 * HEADS
TILE_COLS = [COL_K, COL_Q, COL_V, COL_B + D, COL_B, COL_B + 2 * D, COL_ZA, COL_B + 3 * D]
COL_GATE = COL_B + 4 * D

R_GATE, R_PRE, R_ON, ROWS = CONV * 24, CONV * 24 + 16, CONV * 24 + 24, CONV * 24 + 25

LEVELS = [2, 4, 8, 16, 32, 64]
C_ID, C_ONE, C_TRI, C_E, C_M1, C_ML = (P * i for i in (0, 1, 2, 3, 5, 6))
C_ALL = C_ML + P * len(LEVELS)
BIAS_W = 384


def shape_constants():
    i = np.arange(P)
    row, col = i[:, None], i[None, :]
    parts = [row == col, np.ones((P, P)), row <= col, row < col, row <= col, (col == row + 1) & (row % 2 == 0)]
    for b in LEVELS:
        parts.append((row // (2 * b) == col // (2 * b)) & (row // b == col // b + 1))
    consts = np.concatenate([m.astype(np.float32) for m in parts], axis=1)
    dist = 255 - np.arange(BIAS_W)
    half = BUCKETS // 2
    far = np.maximum(dist, 1).astype(np.float32)
    large = half + (np.log(far / np.float32(half)) / np.float32(np.log(MAX_DIST / half))
                    * np.float32(BUCKETS - half)).astype(np.int32)
    bucket = np.where(dist < half, np.maximum(dist, 0), np.minimum(large, BUCKETS - 1))
    onehot = np.zeros((BUCKETS + 1, BIAS_W), np.float32)
    onehot[bucket, np.arange(BIAS_W)] = 1.0
    onehot[:, dist < 0] = 0.0
    onehot[BUCKETS, dist < 0] = 1.0
    return np.ascontiguousarray(consts), onehot


def counts(value):
    return not isinstance(value, int) or value > 0


def build(nc, x, norm_pre_w, w_in, b_gate, conv_w, dn_a_log, dn_dt_bias, dn_onorm_w, rel_bias, w_branch, w_out,
          norm_post_w, consts, onehot, out):
    with ExitStack() as ctx:
        def sb(name, shape, dt=F32):
            return ctx.enter_context(nc.sbuf_tensor(name, shape, dt))

        def sem(name):
            return ctx.enter_context(nc.semaphore(name))

        banks = ctx.enter_context(nc.psum_tensor("banks", [P, 8 * 512], F32))
        bank = [banks[:, 512 * i:512 * i + 512] for i in range(8)]
        out_rows = [banks[:, 1024 * c + 1024:1024 * c + 2048] for c in range(NC)]
        bA, bB, bC, bD, bE, bF = bank[2:]

        raw = sb("raw", [P, SLOTS, D])
        w_hi = sb("w_hi", [P, SLOTS, D], F32R)
        w_lo = sb("w_lo", [P, SLOTS, D], F32R)
        xin = sb("xin", [P, NC, D])
        xn = res = xin
        cst = sb("cst", [P, C_ALL])
        relb = sb("relb", [BUCKETS + 1, HEADS])
        vec = sb("vec", [P, ROWS])
        vec_half = sb("vec_half", [P, ROWS])
        wbd = sb("wbd", [P, KT, 2 * HEADS])
        alog = sb("alog", [P, HEADS])
        dtb = sb("dtb", [P, HEADS])
        h_hi = sb("h_hi", [P, KT, SEQ], F32R)
        h_lo = sb("h_lo", [P, KT, SEQ], F32R)
        bias = sb("bias", [P, HEADS, BIAS_W])
        tiny = sb("tiny", [P, 32])
        bd = sb("bd", [P, NC, 2 * HEADS])
        gt = sb("gt", [P, 10, NC, HEADS])
        tab = sb("tab", [P, 11, HEADS])
        taps = sb("taps", [P, 2, 3, CONV])
        acc = sb("acc", [P, 3, SEQ])
        tacc = sb("tacc", [P, 3, SEQ])
        act = sb("act", [P, 2, 3, SEQ])
        bT = sb("bT", [P, 2, 3, SEQ])
        tz = sb("tz", [P, 2, SEQ])
        gz = sb("gz", [P, 2, 2, SEQ])
        th = sb("th", [P, 2 * KT, SEQ])
        h32 = th[:, 0:KT, :]
        hc2 = sb("hc", [P, 2, 11])
        sq = sb("sq", [P, SEQ])
        ssq = sb("ssq", [P, 6])
        rn2 = sb("rn", [P, 2, 4])
        dm = sb("dm", [P, 256])
        ex = sb("ex", [P, 256])
        e4 = sb("e4", [P, 512])
        kk = sb("kk", [P, 4, P])
        vb2 = sb("vb", [P, 2, NC, P])
        kdec2 = sb("kdec", [P, 2, P])
        kkT2 = sb("kkT", [P, 2, 4, P])
        la2 = sb("la", [P, 2, 4, P])
        u_tmp = sb("u_tmp", [P, NC, P])
        tu2 = sb("tu", [P, 2, 4, P])
        xl2 = sb("xl", [P, 2, NC, P])
        q1 = sb("q1", [P, 2, P])
        gza = sb("gza", [P, 2, SEQ])
        v0 = sb("v0", [P, P])
        s1 = sb("s1", [P, P])
        r1 = sb("r1", [P, P])
        qs = sb("qs", [P, P])
        v1 = sb("v1", [P, P])
        oo = sb("oo", [P, NC, P])
        junk = sb("junk", [P, 512])
        so = sb("so", [P, 8])
        on = sb("on", [P, NC, P])
        sc = sb("sc", [P, BIAS_W])
        mx = sb("mx", [P, 8])
        pt = sb("pt", [P, BIAS_W])
        vtok = sb("vtok", [P, NC, P])
        y32 = sb("y32", [P, 2, SEQ])
        y_hi = sb("y_hi", [P, 2, HEADS, SEQ], F32R)
        y_lo = sb("y_lo", [P, 2, HEADS, SEQ], F32R)
        m2, m32 = acc[:, 0:2, :], acc[:, 2, :]
        xl_out = th[:].rearrange("p t n -> p (t n)")[:, 0:D]
        post = bT[:].rearrange("p a t n -> p (a t n)")[:, 0:D]
        m_hi, m_lo = h_hi, h_lo
        hot, brow, rows = sc[0:BUCKETS + 1, :], pt[0:HEADS, :], r1
        bias_rows = nc.dram_tensor("bias_rows", [HEADS, P, BIAS_W + 1], F32, kind="Internal").ap()

        ident = cst[:, C_ID:C_ID + P]
        ones = cst[:, C_ONE:C_ONE + P]
        tri = cst[:, C_TRI:C_TRI + P]

        def both(col):
            return cst[:, col:col + P].rearrange("p (a n) -> p a n", a=1).to_broadcast([P, NC, P])

        s_T = sem("s_T")
        s_act = sem("s_act")
        s_bT = sem("s_bT")
        s_bd = sem("s_bd")
        s_bd_p = sem("s_bd_p")
        s_bd_w = sem("s_bd_w")
        s_bias_p = sem("s_bias_p")
        s_brow = sem("s_brow")
        s_cst = sem("s_cst")
        s_d_p = sem("s_d_p")
        s_dm = sem("s_dm")
        s_e4 = sem("s_e4")
        s_ex = sem("s_ex")
        s_f = sem("s_f")
        s_g = sem("s_g")
        s_ga = sem("s_ga")
        s_gate_th = sem("s_gate_th")
        s_gb = sem("s_gb")
        s_gc = sem("s_gc")
        s_gc_p = sem("s_gc_p")
        s_gv = sem("s_gv")
        s_gz = sem("s_gz")
        s_h32a = sem("s_h32a")
        s_h32v = sem("s_h32v")
        s_hT = sem("s_hT")
        s_h_hi = sem("s_h_hi")
        s_h_lo = sem("s_h_lo")
        s_hc = sem("s_hc")
        s_hi = sem("s_hi")
        s_hot = sem("s_hot")
        s_keep = sem("s_keep")
        s_kk = sem("s_kk")
        s_kkT = sem("s_kkT")
        s_ks_p = sem("s_ks_p")
        s_kt_p = sem("s_kt_p")
        s_kv = sem("s_kv")
        s_la = sem("s_la")
        s_la_p = sem("s_la_p")
        s_lo = sem("s_lo")
        s_loaded = sem("s_loaded")
        s_m2 = sem("s_m2")
        s_m32 = sem("s_m32")
        s_m_hi = sem("s_m_hi")
        s_m_lo = sem("s_m_lo")
        s_mx = sem("s_mx")
        s_nmx = sem("s_nmx")
        s_o0 = sem("s_o0")
        s_o0_p = sem("s_o0_p")
        s_o1 = sem("s_o1")
        s_o1_p = sem("s_o1_p")
        s_o_f = sem("s_o_f")
        s_o_p = sem("s_o_p")
        s_o_r = sem("s_o_r")
        s_o_sq = sem("s_o_sq")
        s_o_t = sem("s_o_t")
        s_on = sem("s_on")
        s_ot_p = sem("s_ot_p")
        s_out = sem("s_out")
        s_pexp = sem("s_pexp")
        s_pn = sem("s_pn")
        s_post = sem("s_post")
        s_pre_c = sem("s_pre_c")
        s_pre_r = sem("s_pre_r")
        s_pre_sq = [sem(f"s_pre_sq{c}") for c in range(NC)]
        s_pre_x = [sem(f"s_pre_x{c}") for c in range(NC)]
        s_pt = sem("s_pt")
        s_pt_p = sem("s_pt_p")
        s_pv_p = sem("s_pv_p")
        s_qs = sem("s_qs")
        s_qs_p = sem("s_qs_p")
        s_r1 = sem("s_r1")
        s_relb = sem("s_relb")
        s_rn = sem("s_rn")
        s_rows = sem("s_rows")
        s_rsum = sem("s_rsum")
        s_s1 = sem("s_s1")
        s_s1_p = sem("s_s1_p")
        s_sc = sem("s_sc")
        s_sc_p = sem("s_sc_p")
        s_small = sem("s_small")
        s_so = sem("s_so")
        s_sq = sem("s_sq")
        s_ssq = sem("s_ssq")
        s_ssq_p = sem("s_ssq_p")
        s_stored = sem("s_stored")
        s_tab = sem("s_tab")
        s_tanh = sem("s_tanh")
        s_tap = sem("s_tap")
        s_tap0 = sem("s_tap0")
        s_taps = sem("s_taps")
        s_tile = sem("s_tile")
        s_tt_p = sem("s_tt_p")
        s_tu = sem("s_tu")
        s_tz = sem("s_tz")
        s_u2 = sem("s_u2")
        s_v0 = sem("s_v0")
        s_v0_p = sem("s_v0_p")
        s_v1 = sem("s_v1")
        s_v1_p = sem("s_v1_p")
        s_vb = sem("s_vb")
        s_vec = sem("s_vec")
        s_vec_p = sem("s_vec_p")
        s_vt_p = sem("s_vt_p")
        s_vtok = sem("s_vtok")
        s_x = sem("s_x")
        s_x_in = [sem(f"s_x_in{c}") for c in range(NC)]
        s_ident = sem("s_ident")
        s_ssk = sem("s_ssk")
        s_e2 = sem("s_e2")
        s_o_w = sem("s_o_w")
        s_x_p = sem("s_x_p")
        s_ya32 = sem("s_ya32")
        s_yb32 = sem("s_yb32")
        s_yhi_a = sem("s_yhi_a")
        s_yhi_b = sem("s_yhi_b")
        s_ylo_a = sem("s_ylo_a")
        s_ylo_b = sem("s_ylo_b")
        s_raw = [sem(f"s_raw{i}") for i in range(SLOTS)]
        block = ctx.enter_context(nc.Block())

        def one(a):
            return a.rearrange("p (a n) -> p a n", a=1)

        @block.sync
        def _(sp):
            for c in range(NC):
                sp.dma_start(xin[:, c, :], x[0, c * P:(c + 1) * P, :]).then_inc(s_x_in[c], 16)
            sp.dma_start(cst[:, 0:P], consts[:, 0:P]).then_inc(s_ident, 16)
            sp.dma_start(rows[0:R_GATE, :], conv_w.rearrange("k (t p) -> (k t) p", p=P)).then_inc(s_rows, 16)
            sp.dma_start(rows[R_GATE:R_PRE, :], b_gate.rearrange("(t p) -> t p", p=P)).then_inc(s_rows, 16)
            sp.dma_start(rows[R_PRE:R_ON, :], norm_pre_w.rearrange("(t p) -> t p", p=P)).then_inc(s_rows, 16)
            sp.dma_start(rows[R_ON:ROWS, :], dn_onorm_w.rearrange("(t p) -> t p", p=P)).then_inc(s_rows, 16)

            def load(n, src):
                if load.slot % 2 == 0:
                    if counts(2 * (n - SLOTS + 2)):
                        sp.wait_ge(s_lo, 2 * (n - SLOTS + 2))
                return sp.dma_start(raw[:, load.slot, :].rearrange("p (k n) -> p k n", k=src.shape[1]), src)

            def load_at(n, t, src):
                load.slot = t % SLOTS
                load(n, src).then_inc(s_raw[t % SLOTS], 16)

            def w_tile(col):
                return w_in[:, bass.ds(col, P)].rearrange("(k p) n -> p k n", p=P)

            def head_loads(h, tiles):
                for t in tiles:
                    load_at(h * PER_HEAD + t, t, w_tile(h * P + TILE_COLS[t]))

            head_loads(0, range(2))
            sp.dma_start(cst[:, P:], consts[:, P:]).then_inc(s_cst, 16)
            sp.dma_start(wbd[:], w_in[:, COL_BD:COL_B].rearrange("(k p) n -> p k n", p=P)).then_inc(s_bd_w, 16)
            sp.dma_start(alog[:], dn_a_log.rearrange("(a n) -> a n", a=1).to_broadcast([P, HEADS])).then_inc(s_small, 16)
            sp.dma_start(dtb[:], dn_dt_bias.rearrange("(a n) -> a n", a=1).to_broadcast([P, HEADS])).then_inc(s_small, 16)
            sp.dma_start(hot, onehot).then_inc(s_hot, 16)
            sp.dma_start(relb[0:BUCKETS, :], rel_bias).then_inc(s_hot, 16)
            head_loads(0, range(2, PER_HEAD))
            with sp.Fori(1, HEADS) as h:
                head_loads(h, range(PER_HEAD))
            with sp.Fori(0, 2) as i:
                for t in range(PER_HEAD):
                    load_at(GATES0 + i * PER_HEAD + t, t, w_tile(COL_GATE + (i * PER_HEAD + t) * P))
            sp.wait_ge(s_ylo_b, HEADS + 1)
            sp.dma_start(post, norm_post_w.rearrange("(a n) -> a n", a=1).to_broadcast([P, D])).then_inc(s_post, 16)
            with sp.Fori(0, KT // 2) as i:
                for t in range(4):
                    load_at(BRANCH0 + i * 4 + t, t, w_branch[t % 2][:, bass.ds((i * 2 + t // 2) * P, P)]
                            .rearrange("(k p) n -> p k n", p=P))
            for k in range(KT):
                load_at(OUT0 + k, OUT0 + k, w_out[k * P:(k + 1) * P, :].rearrange("p (k n) -> p k n", k=1))
            for c in range(NC):
                load_at(TILES + c, TILES + c, x[0, c * P:(c + 1) * P, :].rearrange("p (k n) -> p k n", k=1))
            for c in range(NC):
                for e in range(2):
                    cols = slice(512 * e, 512 * e + 512)
                    sp.wait_ge(s_o_f, 2 * c + e + 1)
                    sp.dma_start(out[0, c * P:(c + 1) * P, cols], res[:, c, cols]).then_inc(s_out, 16)
            sp.wait_ge(s_out, 32 * NC)

        @block.gpsimd
        def _(pool):
            pool.memset(relb[BUCKETS:BUCKETS + 1, :], NEG_INF).then_inc(s_relb, 1)
            pool.wait_ge(s_relb, 1)
            pool.memset(tiny[:, 8:12], -0.5).then_inc(s_pre_r, 1)
            pool.wait_ge(s_pre_r, 1)
            pool.memset(tiny[:, 12:14], EPS * P).then_inc(s_pre_c, 1)
            pool.wait_ge(s_pre_c, 1)
            pool.memset(tiny[:, 14:16], 4 * EPS).then_inc(s_pre_c, 1)
            pool.wait_ge(s_pre_c, 2)
            for c in range(NC):
                pool.wait_ge(s_pre_sq[c], 1)
            pool.tensor_scalar(tiny[:, 0:2], tiny[:, 0:2], 1.0 / D, EPS, ALU.mult, ALU.add).then_inc(s_pre_r, 1)
            pool.wait_ge(s_pre_r, 2)
            pool.tensor_tensor(tiny[:, 2:4], tiny[:, 0:2], tiny[:, 8:10], ALU.pow).then_inc(s_pre_r, 1)
            pool.wait_ge(s_pre_r, 3)
            def front(h, p):
                if isinstance(h, int) and h == 0:
                    pool.wait_ge(s_vec, 1)
                src = vec[:, 0:R_GATE].rearrange("p (k t h) -> p t k h", k=CONV, h=HEADS)[:, :, :, bass.ds(h, 1)]
                pool.tensor_copy(taps[:, p, :, :].rearrange("p t (k a) -> p t k a", a=1), src).then_inc(s_taps, 1)
                pool.wait_ge(s_taps, h + 1)

            front(0, 0)
            pool.wait_ge(s_brow, 1)
            pool.dma_start(bias_rows[:, :, 0:BIAS_W],
                           brow.rearrange("h (a n) -> h a n", a=1).to_broadcast([HEADS, P, BIAS_W])).then_inc(s_stored, 16)
            pool.wait_ge(s_stored, 16)
            for c0, c1, at in ((0, 256, 0), (128, 256, 256)):
                src = bass.AP(bias_rows.tensor, P - 1 + c0, [[BIAS_W, P], [P * (BIAS_W + 1), HEADS], [1, c1 - c0]])
                pool.dma_start(bias[:, :, at:at + c1 - c0], src).then_inc(s_loaded, 16)

            def stage_a(g, p):
                hc, rn = hc2[:, p], rn2[:, p]
                if counts(g):
                    pool.wait_ge(s_ylo_a, g)
                pool.tensor_copy(hc.rearrange("p (k a) -> p k a", a=1), tab[:, :, bass.ds(g, 1)]).then_inc(s_hc, 1)
                pool.wait_ge(s_hc, g + 1)
                pool.wait_ge(s_ssk, 2 * g + 2)
                pool.tensor_tensor(ssq[:, 4:6], ssq[:, 0:2], tiny[:, 14:16], ALU.add).then_inc(s_rn, 1)
                pool.wait_ge(s_rn, 2 * g + 1)
                pool.tensor_tensor(rn[:, 0:2], ssq[:, 4:6], tiny[:, 8:10], ALU.pow).then_inc(s_rn, 1)
                pool.wait_ge(s_rn, 2 * g + 2)
                pool.wait_ge(s_ex, g + 1)
                for j in range(2):
                    pool.tensor_tensor(e4[:, 256 * j:256 * j + 256].rearrange("p (c n) -> p c n", c=NC),
                                       ex[:].rearrange("p (c n) -> p c n", c=NC), both(C_E + P * j),
                                       ALU.mult).then_inc(s_e4, 1)
                    pool.wait_ge(s_e4, 2 * g + j + 1)
                pool.wait_ge(s_ssq, g + 1)
                pool.tensor_tensor(rn[:, 2:4], ssq[:, 2:4], tiny[:, 12:14], ALU.mult).then_inc(s_e2, 1)
                pool.wait_ge(s_e2, g + 1)

            def stage_b(g, p):
                rn = rn2[:, p]
                pool.wait_ge(s_so, 2 * g + 2)
                pool.tensor_tensor(so[:, 2:4], so[:, 0:2], rn[:, 2:4], ALU.add).then_inc(s_f, 1)
                pool.wait_ge(s_f, 2 * g + 1)
                pool.tensor_tensor(so[:, 6:8], so[:, 2:4], tiny[:, 8:10], ALU.pow).then_inc(s_f, 1)
                pool.wait_ge(s_f, 2 * g + 2)

            pool.wait_ge(s_tab, 5)
            front(1, 1)
            stage_a(0, 0)
            with pool.Fori(2, HEADS - 1, 2) as h:
                front(h, 0)
                stage_a(h - 1, 1)
                stage_b(h - 2, 0)
                front(h + 1, 1)
                stage_a(h, 0)
                stage_b(h - 1, 1)
            stage_a(HEADS - 1, 1)
            stage_b(HEADS - 2, 0)
            stage_b(HEADS - 1, 1)
            for c in range(NC):
                pool.wait_ge(s_o_sq, c + 1)
                pool.tensor_tensor(tiny[:, 26 + c:27 + c], tiny[:, 24 + c:25 + c], tiny[:, 14:15],
                                   ALU.add).then_inc(s_o_t, 1)
                pool.wait_ge(s_o_t, c + 1)
                pool.tensor_tensor(tiny[:, 28 + c:29 + c], tiny[:, 26 + c:27 + c], tiny[:, 8:9],
                                   ALU.pow).then_inc(s_o_r, 1)
                pool.wait_ge(s_o_r, c + 1)

        @block.scalar
        def _(sa):
            ac = nc.scalar.activation

            def split_hi(n, t):
                sa.wait_ge(s_raw[t % SLOTS], 16 * (n // SLOTS + 1) if isinstance(n, int) else split_hi.turn)
                if counts(n - SLOTS + 1):
                    sa.wait_ge(s_tile, n - SLOTS + 1)
                nc.scalar.copy(w_hi[:, t % SLOTS, :], raw[:, t % SLOTS, :]).then_inc(s_hi, 1)

            def lead(h, t):
                split_hi.turn = 16 * (h * (PER_HEAD // SLOTS) + (t + LEAD) // SLOTS + 1)
                split_hi(h * PER_HEAD + t + LEAD, t + LEAD)

            sa.wait_ge(s_x_in[0], 16)
            ac(bias[:].rearrange("p h n -> p (h n)")[:, 0:D], xin[:, 0, :], ACT.Square,
               accum_out=tiny[:, 0:1]).then_inc(s_pre_sq[0], 1)
            sa.wait_ge(s_pre_r, 3)
            ac(xn[:, 0, :], xin[:, 0, :], ACT.Copy, scale=tiny[:, 2:3]).then_inc(s_pre_x[0], 1)
            sa.wait_ge(s_vec, 2)
            split_hi(0, 0)
            for k in range(1, KT, 2):
                sa.wait_ge(s_hT, k + 1)
                ac(h32[:, k, :], bank[k][:, 0:SEQ], ACT.Copy, scale=vec[:, R_PRE + k:R_PRE + k + 1]).then_inc(s_h32a, 1)
                sa.wait_ge(s_h32a, k // 2 + 1)
                sa.wait_ge(s_h32v, k // 2 + 1)
                nc.scalar.copy(h_hi[:, k - 1:k + 1, :], h32[:, k - 1:k + 1, :]).then_inc(s_h_hi, 1)
            split_hi(1, 1)

            def gates(part):
                if part == 0:
                    sa.wait_ge(s_bd, 1)
                    ac(gt[:, 0], bd[:, :, 0:HEADS], ACT.Tanh, scale=0.5).then_inc(s_ga, 1)
                    sa.wait_ge(s_gv, 2)
                    ac(gt[:, 2], gt[:, 1], ACT.Abs).then_inc(s_ga, 1)
                    sa.wait_ge(s_ga, 2)
                    ac(gt[:, 3], gt[:, 2], ACT.Exp, scale=-1.0).then_inc(s_ga, 1)
                    sa.wait_ge(s_small, 32)
                    ac(tiny[:, 16:24], alog[:], ACT.Exp).then_inc(s_ga, 1)
                elif part == 1:
                    sa.wait_ge(s_gv, 3)
                    ac(gt[:, 5], gt[:, 4], ACT.Ln).then_inc(s_ga, 1)
                else:
                    sa.wait_ge(s_gc, 2)
                    ac(tab[:, 7, :], tab[:, 5, :], ACT.Exp).then_inc(s_tab, 1)
                    ac(tab[:, 8, :], gt[:, 9, 0], ACT.Exp).then_inc(s_tab, 1)

            def front(h, p, t):
                ps = bank[t % 2][:, 0:SEQ]
                sa.wait_ge(s_tile, h * PER_HEAD + t + 1)
                if t < 3:
                    w = (1, 0, 2)[t]
                    if t == 0:
                        sa.wait_ge(s_taps, h + 1)
                        if counts(h):
                            sa.wait_ge(s_act, h)
                    ac(acc[:, t, :], ps, ACT.Copy, scale=taps[:, p, w, CONV - 1:CONV]).then_inc(s_tap0, 1)
                    if t == 2:
                        sa.wait_ge(s_tap, 9 * h + 9)
                        ac(tacc[:], acc[:], ACT.Tanh, scale=0.5).then_inc(s_tanh, 1)
                elif t < 6:
                    if t == 3:
                        if counts(h):
                            sa.wait_ge(s_ylo_b, h)
                    nc.scalar.copy(bT[:, p, t - 3, :], ps).then_inc(s_bT, 1)
                    if t == 4:
                        sa.wait_ge(s_act, h + 1)
                        if counts(h):
                            sa.wait_ge(s_ssq_p, h)
                        ac(sq[:], act[:, p, 1, :], ACT.Square).then_inc(s_sq, 1)
                else:
                    if counts(2 * (h - 1) + t - 5):
                        sa.wait_ge(s_gz, 2 * (h - 1) + t - 5)
                    ac(tz[:, t - 6, :], ps, ACT.Tanh, scale=0.5).then_inc(s_tz, 1)

            def gate_front(i, t):
                sa.wait_ge(s_tile, GATES0 + i * PER_HEAD + t + 1)
                g = i * PER_HEAD + t
                ac(th[:, g, :], bank[t % 2][:, 0:SEQ], ACT.Tanh, scale=0.5,
                   bias=vec_half[:, R_GATE + g:R_GATE + g + 1]).then_inc(s_gate_th, 1)

            def stage_a(g, p, s):
                hc, vb, kdec, kkT, tu = hc2[:, p], vb2[:, p], kdec2[:, p], kkT2[:, p], tu2[:, p]
                if s == 0:
                    sa.wait_ge(s_kv, g + 1)
                    for c in range(NC):
                        ac(junk[:, 0:P], bA[:, P * c:P * c + P], ACT.Square, accum_out=ssq[:, c:c + 1]).then_inc(s_ssk, 1)
                        sa.wait_ge(s_ssk, 2 * g + c + 1)
                    if counts(g):
                        sa.wait_ge(s_ylo_a, g)
                    sa.wait_ge(s_gz, 2 * g + 1)
                    nc.scalar.copy(q1[:, p, :], act[:, p, 1, P:2 * P]).then_inc(s_keep, 1)
                    nc.scalar.copy(gza[:, p, :], gz[:, p, 0, :]).then_inc(s_keep, 1)
                    sa.wait_ge(s_dm, 2 * g + 2)
                    ac(ex[:], dm[:], ACT.Exp).then_inc(s_ex, 1)
                elif s == 1:
                    sa.wait_ge(s_vt_p, g + 1)
                    nc.scalar.copy(vtok[:], bB[:, 0:256].rearrange("p (c n) -> p c n", c=NC)).then_inc(s_vtok, 1)
                    sa.wait_ge(s_kk, 4 * g + 2)
                    for c in range(NC):
                        ac(vb[:, c, :], bA[:, 256 + P * c:384 + P * c], ACT.Copy, scale=hc[:, 2 + c:3 + c]) \
                            .then_inc(s_vb, 1)
                    ac(kdec, kk[:, 0, :], ACT.Copy, scale=hc[:, 8:9]).then_inc(s_vb, 1)
                elif s == 2:
                    sa.wait_ge(s_kt_p, g + 1)
                    nc.scalar.copy(kkT, bB.rearrange("p (c n) -> p c n", c=4)).then_inc(s_kkT, 1)
                    sa.wait_ge(s_nmx, g + 1)
                    ac(sc[:, 0:256], sc[:, 0:256], ACT.Exp, bias=mx[:, 2:3], accum_out=mx[:, 4:5]).then_inc(s_pexp, 1)
                    ac(sc[:, 256:384], sc[:, 256:384], ACT.Exp, bias=mx[:, 3:4],
                       accum_out=mx[:, 5:6]).then_inc(s_pexp, 1)
                elif s == 4:
                    sa.wait_ge(s_tt_p, g + 1)
                    nc.scalar.copy(tu[:, 0:2, :], bB[:, 0:256].rearrange("p (c n) -> p c n", c=NC)).then_inc(s_T, 1)
                    sa.wait_ge(s_pt_p, g + 1)
                    nc.scalar.copy(pt[:], bC[:, 0:BIAS_W]).then_inc(s_pt, 1)
                elif s == 6:
                    sa.wait_ge(s_yb32, g + 1)
                    nc.scalar.copy(y_hi[:, 1, bass.ds(g, 1), :], one(y32[:, 1, :])).then_inc(s_yhi_b, 1)

            def stage_b(g, p, s):
                hc = hc2[:, p]
                if s == 5:
                    sa.wait_ge(s_v0_p, g + 1)
                    nc.scalar.copy(v0[:], bD[:, 0:P]).then_inc(s_v0, 1)
                elif s == 6:
                    sa.wait_ge(s_s1_p, g + 1)
                    nc.scalar.copy(s1[:], bE[:, 0:P]).then_inc(s_s1, 1)
                elif s == 7:
                    sa.wait_ge(s_qs_p, g + 1)
                    ac(qs[:], bD[:, P:2 * P], ACT.Copy, scale=hc[:, 7:8]).then_inc(s_qs, 1)
                    sa.wait_ge(s_o0, g + 1)
                    ac(junk[:, 0:P], oo[:, 0, :], ACT.Square, scale=P ** -0.5, accum_out=so[:, 0:1]).then_inc(s_so, 1)
                elif s == 8:
                    sa.wait_ge(s_v1_p, g + 1)
                    nc.scalar.copy(v1[:], bE[:, 0:P]).then_inc(s_v1, 1)
                elif s == 9:
                    sa.wait_ge(s_o1, g + 1)
                    ac(junk[:, P:2 * P], oo[:, 1, :], ACT.Square, scale=P ** -0.5,
                       accum_out=so[:, 1:2]).then_inc(s_so, 1)
                elif s == 10:
                    sa.wait_ge(s_f, 2 * g + 2)
                    for c in range(NC):
                        ac(on[:, c, :], oo[:, c, :], ACT.Copy, scale=so[:, 6 + c:7 + c]).then_inc(s_on, 1)
                elif s == 11:
                    sa.wait_ge(s_ya32, g + 1)
                    nc.scalar.copy(y_hi[:, 0, bass.ds(g, 1), :], one(y32[:, 0, :])).then_inc(s_yhi_a, 1)

            def iteration(h, p, stages):
                for t in range(PER_HEAD):
                    for s in range(3 * t, 3 * t + 3):
                        if s in (9, 13, 22) and stages == 0:
                            gates((9, 13, 22).index(s))
                        if s % 2 == 0 and stages >= 1:
                            stage_a(h - 1, 1 - p, s // 2)
                        elif s % 2 and stages == 2:
                            stage_b(h - 2, p, s // 2)
                        if s % 3 == 0 and t >= 1:
                            front(h, p, t - 1)
                        if s % 3 == 1:
                            lead(h, t)
                front(h, p, PER_HEAD - 1)

            iteration(0, 0, 0)
            iteration(1, 1, 1)
            with sa.Fori(2, HEADS - 1, 2) as h:
                iteration(h, 0, 2)
                iteration(h + 1, 1, 2)
            for i in range(2):
                for t in range(PER_HEAD):
                    for s in range(3 * t, 3 * t + 3):
                        if s % 2 == 0 and i == 0:
                            stage_a(HEADS - 1, 1, s // 2)
                        elif s % 2:
                            stage_b(HEADS - 2 + i, i, s // 2)
                        if s % 3 == 0 and t >= 1:
                            gate_front(i, t - 1)
                        if s % 3 == 1:
                            lead(HEADS + i, t)
                gate_front(i, PER_HEAD - 1)

            sa.sem_inc(s_m_hi, 1)
            with sa.Fori(0, KT // 2) as i:
                for t in range(4):
                    n = BRANCH0 + i * 4 + t + LEAD
                    split_hi.turn = 16 * (BRANCH0 // SLOTS + i + (t + LEAD) // SLOTS + 1)
                    split_hi(n, t + LEAD)
                    if t % 2:
                        d = i * 2 + t // 2
                        sa.wait_ge(s_m32, d + 2)
                        nc.scalar.copy(m_hi[:, bass.ds(d, 1), :], m32.rearrange("p (a n) -> p a n", a=1)).then_inc(s_m_hi, 1)
            for k in range(KT - LEAD):
                split_hi(OUT0 + k + LEAD, k + LEAD)
            for c in range(NC):
                sa.wait_ge(s_o_p, c + 1)
                ac(xl_out, out_rows[c], ACT.Square, scale=D ** -0.5, accum_out=tiny[:, 24 + c:25 + c]).then_inc(s_o_sq, 1)
                sa.wait_ge(s_o_sq, c + 1)

        @block.vector
        def _(ve):
            v = nc.vector

            def split_lo(n, t, part):
                ve.wait_ge(s_hi, n + 1)
                if part == 0:
                    if counts(n - SLOTS + 1):
                        ve.wait_ge(s_tile, n - SLOTS + 1)
                half = slice(part * (D // 2), (part + 1) * (D // 2))
                v.tensor_tensor(w_lo[:, t % SLOTS, half], raw[:, t % SLOTS, half],
                                w_hi[:, t % SLOTS, half].bitcast(F32), ALU.subtract).then_inc(s_lo, 1)

            def lead(h, t, part):
                split_lo(h * PER_HEAD + t + LEAD, t + LEAD, part)

            def input_lo(k):
                ve.wait_ge(s_h_hi, k // 2 + 1)
                v.tensor_tensor(h_lo[:, k:k + 2, :], h32[:, k:k + 2, :], h_hi[:, k:k + 2, :].bitcast(F32),
                                ALU.subtract).then_inc(s_h_lo, 1)

            ve.wait_ge(s_x_in[1], 16)
            v.tensor_tensor_reduce(bias[:].rearrange("p h n -> p (h n)")[:, D:2 * D], xin[:, 1, :], xin[:, 1, :], 1.0,
                                   0.0, ALU.mult, ALU.add, tiny[:, 1:2]).then_inc(s_pre_sq[1], 1)
            ve.wait_ge(s_pre_r, 3)
            v.tensor_scalar(xn[:, 1, :], xin[:, 1, :], tiny[:, 3:4], None, ALU.mult).then_inc(s_pre_x[1], 1)
            ve.wait_ge(s_vec_p, 1)
            v.tensor_copy(vec[:], bank[7][:, 0:ROWS]).then_inc(s_vec, 1)
            ve.wait_ge(s_vec, 1)
            v.tensor_scalar(vec_half[:], vec[:], 0.5, None, ALU.mult).then_inc(s_vec, 1)
            for k in range(0, KT, 2):
                ve.wait_ge(s_hT, k + 1)
                v.tensor_scalar(h32[:, k, :], bank[k][:, 0:SEQ], vec[:, R_PRE + k:R_PRE + k + 1], None,
                                ALU.mult).then_inc(s_h32v, 1)
                if k == 0:
                    for part in range(2):
                        split_lo(0, 0, part)
                else:
                    input_lo(k - 2)
            input_lo(KT - 2)
            for part in range(2):
                split_lo(1, 1, part)

            step = [3]

            def gate_step(ins):
                step[0] += 1
                ins.then_inc(s_gv, 1)
                ve.wait_ge(s_gv, step[0])

            def gates(part):
                if part == 0:
                    ve.wait_ge(s_bias_p, 1)
                    v.tensor_copy(brow, bank[3][0:HEADS, 0:BIAS_W]).then_inc(s_brow, 1)
                    ve.wait_ge(s_bd_p, 1)
                    v.tensor_copy(bd[:], bank[2][:, 0:2 * NC * HEADS].rearrange("p (c n) -> p c n", c=NC)).then_inc(s_bd, 1)
                    ve.wait_ge(s_bd, 1)
                    ve.wait_ge(s_small, 32)
                    for c in range(NC):
                        v.tensor_tensor(gt[:, 1, c], bd[:, c, HEADS:], dtb[:], ALU.add).then_inc(s_gv, 1)
                elif part == 1:
                    ve.wait_ge(s_ga, 3)
                    v.tensor_scalar(gt[:, 4], gt[:, 3], 1.0, None, ALU.add).then_inc(s_gv, 1)
                elif part == 2:
                    ve.wait_ge(s_ga, 5)
                    ve.wait_ge(s_gv, 3)
                    gate_step(v.tensor_scalar(gt[:, 6], gt[:, 4], -1.0, None, ALU.add))
                    gate_step(v.tensor_scalar(gt[:, 7], gt[:, 6], 0.0, None, ALU.is_equal))
                    gate_step(v.tensor_tensor(gt[:, 6], gt[:, 6], gt[:, 7], ALU.add))
                    gate_step(v.tensor_tensor(gt[:, 5], gt[:, 5], gt[:, 7], ALU.add))
                    gate_step(v.reciprocal(gt[:, 6], gt[:, 6]))
                    gate_step(v.tensor_tensor(gt[:, 5], gt[:, 5], gt[:, 3], ALU.mult))
                    gate_step(v.tensor_tensor(gt[:, 5], gt[:, 5], gt[:, 6], ALU.mult))
                    gate_step(v.scalar_tensor_tensor(out=gt[:, 8], in0=gt[:, 1], scalar=0.0, in1=gt[:, 5],
                                                     op0=ALU.max, op1=ALU.add))
                    for c in range(NC):
                        v.scalar_tensor_tensor(out=tab[:, 9 + c, :], in0=gt[:, 8, c], scalar=-1.0,
                                               in1=tiny[:, 16:24], op0=ALU.mult, op1=ALU.mult).then_inc(s_g, 1)
                    v.tensor_scalar(tab[:, 0:2, :], gt[:, 0], 0.5, 0.5, ALU.mult, ALU.add).then_inc(s_tab, 1)
                    v.tensor_scalar(tab[:, 2:4, :], gt[:, 0], 0.25, 0.25, ALU.mult, ALU.add).then_inc(s_tab, 1)
                else:
                    ve.wait_ge(s_gc_p, 1)
                    v.tensor_copy(tab[:, 4:6, :], bC[:, 0:16].rearrange("p (c n) -> p c n", c=NC)).then_inc(s_gc, 1)
                    ve.wait_ge(s_gc, 1)
                    v.tensor_tensor(gt[:, 9, 0], bC[:, 16:24], tab[:, 4, :], ALU.subtract).then_inc(s_gc, 1)

            def last_table():
                ve.wait_ge(s_tab, 4)
                v.tensor_scalar(tab[:, 6, :], tab[:, 7, :], -1.0, None, ALU.mult).then_inc(s_tab, 1)
                ve.wait_ge(s_loaded, 32)
                ve.sem_inc(s_ylo_a, 1)
                ve.sem_inc(s_ylo_b, 1)

            def front(h, p, t):
                ps = bank[t % 2]
                if t < 3:
                    w = (1, 0, 2)[t]
                    ve.wait_ge(s_tap0, 3 * h + t + 1)
                    for i in range(1, CONV):
                        if i > 1:
                            ve.wait_ge(s_tap, 9 * h + 3 * t + i - 1)
                        v.scalar_tensor_tensor(out=acc[:, t, i:], in0=ps[:, 0:SEQ - i],
                                               scalar=taps[:, p, w, CONV - 1 - i:CONV - i], in1=acc[:, t, i:],
                                               op0=ALU.mult, op1=ALU.add).then_inc(s_tap, 1)
                elif t == 3:
                    ve.wait_ge(s_tanh, h + 1)
                    if counts(h - 1):
                        ve.wait_ge(s_la_p, h - 1)
                        ve.wait_ge(s_keep, 2 * (h - 1))
                    v.scalar_tensor_tensor(out=act[:, p], in0=tacc[:], scalar=1.0, in1=acc[:], op0=ALU.add,
                                           op1=ALU.mult).then_inc(s_act, 1)
                elif t >= 6:
                    ve.wait_ge(s_tz, 2 * h + t - 5)
                    v.scalar_tensor_tensor(out=gz[:, p, t - 6, :], in0=tz[:, t - 6, :], scalar=1.0, in1=ps[:, 0:SEQ],
                                           op0=ALU.add, op1=ALU.mult).then_inc(s_gz, 1)

            def stage_a(g, p, s):
                hc, rn, la, tu, xl = hc2[:, p], rn2[:, p], la2[:, p], tu2[:, p], xl2[:, p]
                if s == 0:
                    ve.wait_ge(s_gb, g + 1)
                    for c in range(NC):
                        v.tensor_scalar(dm[:, P * c:P * c + P], bB[:, P * c:P * c + P], hc[:, 4 + c:5 + c], 0.0,
                                        ALU.subtract, ALU.min).then_inc(s_dm, 1)
                    ve.wait_ge(s_ssq_p, g + 1)
                    v.tensor_scalar(ssq[:, 2:4], bC[:, 0:2], 4 * EPS, None, ALU.add).then_inc(s_ssq, 1)
                elif s == 1:
                    ve.wait_ge(s_rn, 2 * g + 2)
                    ve.wait_ge(s_keep, 2 * g + 2)
                    for c in range(NC):
                        v.tensor_scalar(kk[:, c, :], bA[:, P * c:P * c + P], rn[:, c:c + 1], None,
                                        ALU.mult).then_inc(s_kk, 1)
                    ve.wait_ge(s_kk, 4 * g + 2)
                    for c in range(NC):
                        v.tensor_scalar(kk[:, 2 + c, :], kk[:, c, :], hc[:, c:c + 1], None,
                                        ALU.mult).then_inc(s_kk, 1)
                    ve.wait_ge(s_sc_p, g + 1)
                    v.scalar_tensor_tensor(out=sc[:], in0=bC[:, 0:BIAS_W], scalar=SCALE,
                                           in1=bias[:, bass.ds(g, 1), :].rearrange("p a n -> p (a n)"),
                                           op0=ALU.mult, op1=ALU.add).then_inc(s_sc, 1)
                    ve.wait_ge(s_sc, g + 1)
                    v.tensor_reduce(mx[:, 0:1], sc[:, 0:256], AX_X, ALU.max).then_inc(s_mx, 1)
                    v.tensor_reduce(mx[:, 1:2], sc[:, 256:384], AX_X, ALU.max).then_inc(s_mx, 1)
                    ve.wait_ge(s_mx, 2 * g + 2)
                    v.tensor_scalar(mx[:, 2:4], mx[:, 0:2], -1.0, None, ALU.mult).then_inc(s_nmx, 1)
                elif s == 3:
                    ve.wait_ge(s_pexp, 2 * g + 2)
                    v.reciprocal(mx[:, 6:8], mx[:, 4:6]).then_inc(s_rsum, 1)
                    ve.wait_ge(s_rsum, g + 1)
                    v.tensor_scalar(sc[:, 0:256], sc[:, 0:256], mx[:, 6:7], None, ALU.mult).then_inc(s_pn, 1)
                    v.tensor_scalar(sc[:, 256:384], sc[:, 256:384], mx[:, 7:8], None, ALU.mult).then_inc(s_pn, 1)
                    ve.wait_ge(s_la_p, g + 1)
                    ve.wait_ge(s_e4, 2 * g + 2)
                    flat = la.rearrange("p c n -> p (c n)")
                    v.tensor_tensor(flat[:, 0:256], bA[:, 0:256], e4[:, 0:256], ALU.mult).then_inc(s_la, 1)
                    ve.wait_ge(s_la, 2 * g + 1)
                    v.tensor_tensor(u_tmp[:], la[:, 0:2, :], both(C_M1), ALU.mult).then_inc(s_u2, 1)
                    ve.wait_ge(s_u2, 2 * g + 1)
                    v.tensor_tensor(tu[:, 2:4, :], both(C_ID), u_tmp[:], ALU.subtract).then_inc(s_u2, 1)
                    v.tensor_tensor(flat[:, 256:512], bA[:, 256:512], e4[:, 256:512], ALU.mult).then_inc(s_la, 1)
                elif s >= 5:
                    level_step(g, p, (s - 5) // 2, s % 2 == 1, bB, bC)
                    if s == 5:
                        ve.wait_ge(s_pv_p, g + 1)
                        v.scalar_tensor_tensor(out=y32[:, 1, :], in0=bA[:, 0:SEQ], scalar=0.5, in1=gz[:, p, 1, :],
                                               op0=ALU.mult, op1=ALU.mult).then_inc(s_yb32, 1)
                    if s == 7:
                        ve.wait_ge(s_yhi_b, g + 1)
                        v.tensor_tensor(y_lo[:, 1, bass.ds(g, 1), :], one(y32[:, 1, :]),
                                        y_hi[:, 1, bass.ds(g, 1), :].bitcast(F32), ALU.subtract).then_inc(s_ylo_b, 1)

            def level_step(g, p, lv, first, x_bank, d_bank):
                tu, xl = tu2[:, p], xl2[:, p]
                if first:
                    ve.wait_ge(s_x_p, 6 * g + lv + 1)
                    v.tensor_tensor(xl, x_bank[:, 0:256].rearrange("p (c n) -> p c n", c=NC), both(C_ML + P * lv),
                                    ALU.mult).then_inc(s_x, 1)
                else:
                    ve.wait_ge(s_d_p, 6 * g + lv + 1)
                    at = 0 if lv < 5 else 2
                    view = tu[:, at:4, :].rearrange("p c n -> p (c n)")
                    v.tensor_tensor(view, view, d_bank[:, P * at:512], ALU.subtract).then_inc(s_tu, 1)

            def stage_b(g, p, s):
                hc, vb = hc2[:, p], vb2[:, p]
                if s < 5:
                    level_step(g, p, 3 + (s + 1) // 2, s % 2 == 1, bD, bE)
                elif s == 6:
                    ve.wait_ge(s_o0_p, g + 1)
                    v.tensor_copy(oo[:, 0, :], bF[:, 0:P]).then_inc(s_o0, 1)
                elif s == 7:
                    ve.wait_ge(s_ks_p, g + 1)
                    v.scalar_tensor_tensor(out=r1[:], in0=bE[:, 256:384], scalar=hc[:, 6:7], in1=vb[:, 1, :],
                                           op0=ALU.mult, op1=ALU.add).then_inc(s_r1, 1)
                elif s == 9:
                    ve.wait_ge(s_o1_p, g + 1)
                    ve.wait_ge(s_qs, g + 1)
                    v.tensor_tensor(oo[:, 1, :], bF[:, P:2 * P], qs[:], ALU.add).then_inc(s_o1, 1)
                elif s == 10:
                    ve.wait_ge(s_ot_p, g + 1)
                    v.scalar_tensor_tensor(out=y32[:, 0, :], in0=bD[:, 0:SEQ], scalar=vec_half[:, R_ON:R_ON + 1],
                                           in1=gza[:, p, :], op0=ALU.mult, op1=ALU.mult).then_inc(s_ya32, 1)
                elif s == 11:
                    ve.wait_ge(s_yhi_a, g + 1)
                    v.tensor_tensor(y_lo[:, 0, bass.ds(g, 1), :], one(y32[:, 0, :]),
                                    y_hi[:, 0, bass.ds(g, 1), :].bitcast(F32), ALU.subtract).then_inc(s_ylo_a, 1)

            def iteration(h, p, stages):
                for t in range(PER_HEAD):
                    for s in range(3 * t, 3 * t + 3):
                        if s in (7, 11, 15, 20) and stages == 0:
                            gates((7, 11, 15, 20).index(s))
                        if s % 2 == 0 and stages >= 1:
                            stage_a(h - 1, 1 - p, s // 2)
                        elif s % 2 and stages == 2:
                            stage_b(h - 2, p, s // 2)
                        if s % 3 == 0 and t >= 1:
                            front(h, p, t - 1)
                        if s % 3 >= 1:
                            lead(h, t, s % 3 - 1)
                front(h, p, PER_HEAD - 1)

            iteration(0, 0, 0)
            last_table()
            iteration(1, 1, 1)
            with ve.Fori(2, HEADS - 1, 2) as h:
                iteration(h, 0, 2)
                iteration(h + 1, 1, 2)
            for i in range(2):
                for t in range(PER_HEAD):
                    for s in range(3 * t, 3 * t + 3):
                        if s % 2 == 0 and i == 0:
                            stage_a(HEADS - 1, 1, s // 2)
                        elif s % 2:
                            stage_b(HEADS - 2 + i, i, s // 2)
                        if s % 3 >= 1:
                            lead(HEADS + i, t, s % 3 - 1)

            ve.sem_inc(s_m32, 1)
            with ve.Fori(0, KT // 2) as i:
                for t in range(4):
                    for part in range(2):
                        split_lo(BRANCH0 + i * 4 + t + LEAD, t + LEAD, part)
                    d = i * 2 + t // 2
                    ve.wait_ge(s_tile, BRANCH0 + i * 4 + t + 1)
                    if t % 2 == 0:
                        ve.wait_ge(s_m_hi, d + 1)
                    v.scalar_tensor_tensor(out=one(m2[:, t % 2, :]), in0=th[:, bass.ds((t % 2) * KT + d, 1), :], scalar=1.0,
                                           in1=one(bank[t % 2][:, 0:SEQ]), op0=ALU.add, op1=ALU.mult).then_inc(s_m2, 1)
                    if t % 2:
                        ve.wait_ge(s_m2, 2 * (d + 1))
                        v.tensor_tensor(m32, m2[:, 0, :], m2[:, 1, :], ALU.add).then_inc(s_m32, 1)
                        ve.wait_ge(s_m_hi, d + 2)
                        v.tensor_tensor(m_lo[:, bass.ds(d, 1), :], one(m32), m_hi[:, bass.ds(d, 1), :].bitcast(F32),
                                        ALU.subtract).then_inc(s_m_lo, 1)
            for k in range(KT - LEAD):
                for part in range(2):
                    split_lo(OUT0 + k + LEAD, k + LEAD, part)
            ve.wait_ge(s_post, 16)
            for c in range(NC):
                ve.wait_ge(s_o_sq, c + 1)
                v.tensor_tensor(res[:, c, :], out_rows[c], post, ALU.mult).then_inc(s_o_w, 1)
                ve.wait_ge(s_o_w, c + 1)
                ve.wait_ge(s_o_r, c + 1)
                ve.wait_ge(s_raw[c], 16 * (TILES // SLOTS + 1))
                for e in range(2):
                    cols = slice(512 * e, 512 * e + 512)
                    v.scalar_tensor_tensor(out=res[:, c, cols], in0=res[:, c, cols], scalar=tiny[:, 28 + c:29 + c],
                                           in1=raw[:, c, cols], op0=ALU.mult, op1=ALU.add).then_inc(s_o_f, 1)

        @block.tensor
        def _(pe):
            mm = nc.tensor.matmul
            tp = nc.tensor.transpose

            pe.wait_ge(s_rows, 64)
            pe.wait_ge(s_ident, 16)
            tp(bank[7][:, 0:ROWS], rows[0:ROWS, :], ident[0:ROWS, 0:ROWS]).then_inc(s_vec_p, 1)
            for c in range(NC):
                pe.wait_ge(s_pre_x[c], 1)
            for k in range(KT):
                if k == 7:
                    pe.wait_ge(s_vec, 1)
                for c in range(NC):
                    last = tp(bank[k][:, P * c:P * c + P], xn[:, c, P * k:P * k + P], ident)
                last.then_inc(s_hT, 1)
            for n in range(2):
                pe.wait_ge(s_h32v if n == 0 else s_h32a, 1)

            def gates(part):
                if part == 0:
                    pe.wait_ge(s_bd_w, 16)
                    for c in range(NC):
                        for k in range(KT):
                            last = mm(bank[2][:, 16 * c:16 * c + 16], h32[:, k, P * c:P * c + P], wbd[:, k, :],
                                      start=k == 0, stop=k == KT - 1)
                    last.then_inc(s_bd_p, 1)
                    pe.wait_ge(s_hot, 32)
                    pe.wait_ge(s_relb, 1)
                    mm(bank[3][0:HEADS, 0:BIAS_W], relb[:], hot, start=True, stop=True).then_inc(s_bias_p, 1)
                else:
                    pe.wait_ge(s_g, 2)
                    pe.wait_ge(s_cst, 16)
                    mm(bC[:, 0:16], tri, tab[:, 9:11, :], start=True, stop=True)
                    mm(bC[:, 16:32], ones, tab[:, 9:11, :], start=True, stop=True).then_inc(s_gc_p, 1)

            def third(n, t, part, right_hi, right_lo, first_tile=False):
                ps = bank[t % 2][:, 0:SEQ]
                slot = t % SLOTS
                if part == 0:
                    pe.wait_ge(s_hi, n + 1)
                    pe.wait_ge(s_lo, 2 * n + 2)
                for i in range(8 * part, 8 * part + 8):
                    k, which = i // 3, i % 3
                    if first_tile and i % 6 == 0:
                        pe.wait_ge(s_h_lo, k // 2 + 1)
                    w = (w_lo if which == 2 else w_hi)[:, slot, P * k:P * k + P]
                    r = (right_lo if which == 1 else right_hi)[:, k, :]
                    last = mm(ps, w, r, start=i == 0, stop=i == 23)
                if part == 2:
                    last.then_inc(s_tile, 1)

            def bank_free(h, t):
                if t < 2:
                    if counts(2 * (h - 1) + t + 1):
                        pe.wait_ge(s_gz, 2 * (h - 1) + t + 1)
                elif t < 5:
                    pe.wait_ge(s_tap, 9 * h + 3 * (t - 1))
                else:
                    pe.wait_ge(s_bT, 3 * h + t - 4)

            def stage_a(g, p, s):
                hc, vb, kkT, la, tu = hc2[:, p], vb2[:, p], kkT2[:, p], la2[:, p], tu2[:, p]
                k_T, q_T, v_T = (act[:, p, j, :] for j in range(3))
                if s == 0:
                    pe.wait_ge(s_act, g + 1)
                    if counts(g):
                        pe.wait_ge(s_ylo_b, g + 1)
                        pe.wait_ge(s_x, 6 * g - 2)
                        pe.wait_ge(s_ylo_a, g)
                    for j, a in enumerate((k_T, v_T)):
                        for c in range(NC):
                            last = tp(bA[:, 256 * j + P * c:256 * j + P * c + P], a[:, P * c:P * c + P], ident)
                    last.then_inc(s_kv, 1)
                    pe.wait_ge(s_sq, g + 1)
                    for c in range(NC):
                        last = mm(bC[:, c:c + 1], sq[:, P * c:P * c + P], ones[:, 0:1], start=True, stop=True)
                    last.then_inc(s_ssq_p, 1)
                    pe.wait_ge(s_hc, g + 1)
                    for c in range(NC):
                        last = mm(bB[:, P * c:P * c + P], hc[:, 9 + c:10 + c].to_broadcast([P, P]), tri,
                                  start=True, stop=True)
                    last.then_inc(s_gb, 1)
                elif s == 1:
                    pe.wait_ge(s_bT, 3 * g + 3)
                    pe.wait_ge(s_ssq, g + 1)
                    kb_T, qb_T, vb_T = (bT[:, p, j, :] for j in range(3))
                    mm(bC[:, 0:256], qb_T[:, P:2 * P], kb_T, start=True, stop=True)
                    mm(bC[:, 256:384], qb_T[:, 0:P], kb_T[:, 0:P], start=True, stop=True).then_inc(s_sc_p, 1)
                    pe.wait_ge(s_dm, 2 * g + 2)
                    for c in range(NC):
                        last = tp(bB[:, P * c:P * c + P], vb_T[:, P * c:P * c + P], ident)
                    last.then_inc(s_vt_p, 1)
                elif s == 2:
                    pe.wait_ge(s_kk, 4 * g + 4)
                    pe.wait_ge(s_vtok, g + 1)
                    for j in range(4):
                        last = tp(bB[:, P * j:P * j + P], kk[:, j, :], ident)
                    last.then_inc(s_kt_p, 1)
                elif s == 3:
                    pe.wait_ge(s_kkT, g + 1)
                    pe.wait_ge(s_vb, 3 * g + 2)
                    for c in range(NC):
                        mm(bA[:, P * c:P * c + P], kkT[:, c, :], kkT[:, 2 + c, :], start=True, stop=True)
                    for c in range(NC):
                        last = mm(bA[:, 256 + P * c:384 + P * c], kkT[:, c, :], q_T[:, P * c:P * c + P],
                                  start=True, stop=True)
                    last.then_inc(s_la_p, 1)
                elif s == 4:
                    pe.wait_ge(s_u2, 2 * g + 2)
                    for c in range(NC):
                        last = tp(bB[:, P * c:P * c + P], tu[:, 2 + c, :], ident)
                    last.then_inc(s_tt_p, 1)
                    pe.wait_ge(s_pn, 2 * g + 2)
                    tp(bC[:, 0:P], sc[:, 256:384], ident)
                    tp(bC[:, P:2 * P], sc[:, 0:P], ident)
                    tp(bC[:, 2 * P:3 * P], sc[:, P:2 * P], ident).then_inc(s_pt_p, 1)
                else:
                    if s == 5:
                        pe.wait_ge(s_T, g + 1)
                    level_step(g, p, (s - 5) // 2, s % 2 == 1, bB, bC)
                    if s == 5:
                        pe.wait_ge(s_pt, g + 1)
                        mm(bA[:, 0:256], vtok[:, 0, :], pt[:, 0:256], start=True, stop=False, skip_group_check=True)
                        mm(bA[:, P:2 * P], vtok[:, 1, :], pt[:, 256:384], start=False, stop=True,
                           skip_group_check=True).then_inc(s_pv_p, 1)

            def level_step(g, p, lv, first, x_bank, d_bank):
                la, tu, xl = la2[:, p], tu2[:, p], xl2[:, p]
                if first:
                    if lv:
                        pe.wait_ge(s_tu, 6 * g + lv)
                    for c in range(NC):
                        last = mm(x_bank[:, P * c:P * c + P], la[:, c, :], tu[:, c, :], start=True, stop=True)
                    last.then_inc(s_x_p, 1)
                else:
                    pe.wait_ge(s_x, 6 * g + lv + 1)
                    if lv < 5:
                        for c in range(NC):
                            mm(d_bank[:, P * c:P * c + P], tu[:, 2 + c, :], xl[:, c, :], start=True, stop=True)
                    for c in range(NC):
                        last = mm(d_bank[:, 256 + P * c:384 + P * c], xl[:, c, :], tu[:, 2 + c, :], start=True, stop=True)
                    last.then_inc(s_d_p, 1)

            def stage_b(g, p, s):
                vb, kdec, kkT, la, tu = vb2[:, p], kdec2[:, p], kkT2[:, p], la2[:, p], tu2[:, p]
                if s < 5:
                    if s == 0:
                        pe.wait_ge(s_ylo_a, g + 1)
                    level_step(g, p, 3 + (s + 1) // 2, s % 2 == 1, bD, bE)
                elif s == 5:
                    pe.wait_ge(s_tu, 6 * g + 6)
                    mm(bD[:, 0:P], tu[:, 2, :], vb[:, 0, :], start=True, stop=True).then_inc(s_v0_p, 1)
                elif s == 6:
                    pe.wait_ge(s_v0, g + 1)
                    mm(bE[:, 0:P], kdec, v0[:], start=True, stop=True).then_inc(s_s1_p, 1)
                    mm(bF[:, 0:P], la[:, 2, :], v0[:], start=True, stop=True).then_inc(s_o0_p, 1)
                elif s == 7:
                    pe.wait_ge(s_s1, g + 1)
                    pe.wait_ge(s_keep, 2 * g + 1)
                    mm(bE[:, 256:384], kkT[:, 3, :], s1[:], start=True, stop=True).then_inc(s_ks_p, 1)
                    mm(bD[:, P:2 * P], q1[:, p, :], s1[:], start=True, stop=True).then_inc(s_qs_p, 1)
                elif s == 8:
                    pe.wait_ge(s_r1, g + 1)
                    mm(bE[:, 0:P], tu[:, 3, :], r1[:], start=True, stop=True).then_inc(s_v1_p, 1)
                elif s == 9:
                    pe.wait_ge(s_v1, g + 1)
                    pe.wait_ge(s_o0, g + 1)
                    mm(bF[:, P:2 * P], la[:, 3, :], v1[:], start=True, stop=True).then_inc(s_o1_p, 1)
                elif s == 10:
                    pe.wait_ge(s_on, 2 * g + 2)
                    for c in range(NC):
                        last = tp(bD[:, P * c:P * c + P], on[:, c, :], ident)
                    last.then_inc(s_ot_p, 1)

            def iteration(h, p, stages):
                for t in range(PER_HEAD):
                    for s in range(3 * t, 3 * t + 3):
                        if s in (6, 18) and stages == 0:
                            gates((6, 18).index(s))
                        if s % 2 == 0 and stages >= 1:
                            stage_a(h - 1, 1 - p, s // 2)
                        elif s % 2 and stages == 2:
                            stage_b(h - 2, p, s // 2)
                        if s % 3 == 0:
                            bank_free(h, t)
                        third(h * PER_HEAD + t, t, s % 3, h_hi, h_lo, first_tile=stages == 0 and t == 0)

            iteration(0, 0, 0)
            pe.wait_ge(s_gc, 2)
            iteration(1, 1, 1)
            with pe.Fori(2, HEADS - 1, 2) as h:
                iteration(h, 0, 2)
                iteration(h + 1, 1, 2)
            for i in range(2):
                for t in range(PER_HEAD):
                    for s in range(3 * t, 3 * t + 3):
                        if s % 2 == 0 and i == 0:
                            stage_a(HEADS - 1, 1, s // 2)
                        elif s % 2:
                            stage_b(HEADS - 2 + i, i, s // 2)
                        if s % 3 == 0:
                            if i == 0 and t < 2:
                                pe.wait_ge(s_gz, 2 * (HEADS - 1) + t + 1)
                            else:
                                pe.wait_ge(s_gate_th, PER_HEAD * i + t - 1)
                        third(GATES0 + i * PER_HEAD + t, t, s % 3, h_hi, h_lo)
            pe.wait_ge(s_gate_th, 2 * KT)
            pe.wait_ge(s_ylo_a, HEADS + 1)
            pe.wait_ge(s_ylo_b, HEADS + 1)

            with pe.Fori(0, KT // 2) as i:
                for t in range(4):
                    if t >= 2:
                        pe.wait_ge(s_m2, i * 4 + t - 1)
                    else:
                        pe.wait_ge(s_m32, i * 2 + 1)
                    for part in range(3):
                        third(BRANCH0 + i * 4 + t, t, part, y_hi[:, t % 2], y_lo[:, t % 2])
            pe.wait_ge(s_m2, 2 * KT)
            for k in range(KT):
                pe.wait_ge(s_hi, OUT0 + k + 1)
                pe.wait_ge(s_lo, 2 * (OUT0 + k) + 2)
                pe.wait_ge(s_m_lo, k + 1)
                slot = (OUT0 + k) % SLOTS
                for c in range(NC):
                    for m, w in ((m_hi, w_hi), (m_hi, w_lo), (m_lo, w_hi)):
                        for e in range(2):
                            last = mm(bank[2 + 2 * c + e], m[:, k, P * c:P * c + P], w[:, slot, 512 * e:512 * e + 512],
                                      start=k == 0 and m is m_hi and w is w_hi, stop=k == KT - 1 and m is m_lo)
                    if k == KT - 1:
                        last.then_inc(s_o_p, 1)
                if k < KT - 1:
                    nxt = last.then_inc(s_tile, 1)


_INS = ['x', 'norm_pre_w', 'w_in', 'b_gate', 'conv_w', 'dn_a_log', 'dn_dt_bias', 'dn_onorm_w', 'rel_bias',
        'w_branch', 'w_out', 'norm_post_w']


def kernel(**inputs):
    import concourse.bacc as _bacc
    from concourse.bass_utils import run_bass_kernel_spmd as _run

    nc = _bacc.Bacc("TRN2", target_bir_lowering=False, num_devices=1)
    consts, onehot = shape_constants()
    arrays, args = {}, []
    for name, a in [(n, np.ascontiguousarray(inputs[n])) for n in _INS] + [("consts", consts), ("onehot", onehot)]:
        arrays[f"in_{name}_dram"] = a
        args.append(nc.dram_tensor(f"in_{name}_dram", a.shape, mybir.dt.from_np(a.dtype), kind="ExternalInput").ap())
    args.append(nc.dram_tensor("out_0_dram", (1, SEQ, D), F32, kind="ExternalOutput").ap())
    build(nc, *args)
    r = _run(nc, [arrays], core_ids=[0])
    return r.results[0]["out_0_dram"]
```

```python
from contextlib import ExitStack

import numpy as np
import concourse.bass as bass
from concourse import mybir

F32 = mybir.dt.float32
F32R = mybir.dt.float32r
ALU = mybir.AluOpType
ACT = mybir.ActivationFunctionType
AX_X = mybir.AxisListType.X

P = 128
HALF = P // 2
D = 1024
SEQ = 256
NC = SEQ // P
KT = D // P
HEADS = 8
EPS = 1e-6
NEG_INF = -1e30
BUCKETS, MAX_DIST = 32, 2048
SCALE = float(P) ** -0.5
CONV = 4

SLOTS = 4
PER_HEAD = 8
GATES0 = HEADS * PER_HEAD
BRANCH0 = GATES0 + 2 * KT
OUT0 = BRANCH0 + 2 * KT
TILES = OUT0 + KT
LEAD = 2
WARM = 8
LATE = (8, 21)
TURNS = {2: (1, 3), 13: (0, 0), 17: (0, 1), 21: (0, 2)}

COL_Q, COL_K, COL_V, COL_ZA = 0, D, 2 * D, 3 * D
COL_BD = 4 * D
COL_B = COL_BD + 2 * HEADS
TILE_COLS = [COL_K, COL_Q, COL_V, COL_B + D, COL_B, COL_B + 2 * D, COL_ZA, COL_B + 3 * D]
COL_GATE = COL_B + 4 * D

R_GATE, R_PRE, R_ON, ROWS = CONV * 24, CONV * 24 + 16, CONV * 24 + 24, CONV * 24 + 25

LEVELS = [2, 4, 8, 16, 32, 64]
C_ID, C_ONE, C_TRI, C_E, C_M1, C_ML = (P * i for i in (0, 1, 2, 3, 5, 6))
C_ALL = C_ML + P * len(LEVELS)
BIAS_W = 384


def shape_constants():
    i = np.arange(P)
    row, col = i[:, None], i[None, :]
    parts = [row == col, np.ones((P, P)), row <= col, row < col, row <= col, (col == row + 1) & (row % 2 == 0)]
    for b in LEVELS:
        parts.append((row // (2 * b) == col // (2 * b)) & (row // b == col // b + 1))
    consts = np.concatenate([m.astype(np.float32) for m in parts], axis=1)
    dist = 255 - np.arange(BIAS_W)
    half = BUCKETS // 2
    far = np.maximum(dist, 1).astype(np.float32)
    large = half + (np.log(far / np.float32(half)) / np.float32(np.log(MAX_DIST / half))
                    * np.float32(BUCKETS - half)).astype(np.int32)
    bucket = np.where(dist < half, np.maximum(dist, 0), np.minimum(large, BUCKETS - 1))
    onehot = np.zeros((BUCKETS + 1, BIAS_W), np.float32)
    onehot[bucket, np.arange(BIAS_W)] = 1.0
    onehot[:, dist < 0] = 0.0
    onehot[BUCKETS, dist < 0] = 1.0
    return np.ascontiguousarray(consts), onehot


def counts(value):
    return not isinstance(value, int) or value > 0


def build(nc, x, norm_pre_w, w_in, b_gate, conv_w, dn_a_log, dn_dt_bias, dn_onorm_w, rel_bias, w_branch, w_out,
          norm_post_w, consts, onehot, out):
    with ExitStack() as ctx:
        def sb(name, shape, dt=F32):
            return ctx.enter_context(nc.sbuf_tensor(name, shape, dt))

        def sem(name):
            return ctx.enter_context(nc.semaphore(name))

        banks = ctx.enter_context(nc.psum_tensor("banks", [P, 8 * 512], F32))
        bank = [banks[:, 512 * i:512 * i + 512] for i in range(8)]
        bA, bB, bC, bD, bE, bF = bank[2:]

        raw = sb("raw", [P, SLOTS, D])
        w_hi = sb("w_hi", [P, SLOTS, D], F32R)
        w_lo = sb("w_lo", [P, SLOTS, D], F32R)
        xin = sb("xin", [P, NC, D])
        xn = res = xin
        cst = sb("cst", [P, C_ALL])
        relb = sb("relb", [BUCKETS + 1, HEADS])
        vec = sb("vec", [P, ROWS])
        vec_half = sb("vec_half", [P, ROWS])
        wbd = sb("wbd", [P, KT, 2 * HEADS])
        wbd2 = sb("wbd2", [P, KT, 4 * HEADS], F32R)
        bd_lo = sb("bd_lo", [P, NC, 2 * HEADS])
        alog = sb("alog", [P, HEADS])
        dtb = sb("dtb", [P, HEADS])
        h_hi = sb("h_hi", [P, KT, SEQ], F32R)
        h_lo = sb("h_lo", [P, KT, SEQ], F32R)
        bias = sb("bias", [P, HEADS, BIAS_W])
        tiny = sb("tiny", [P, 32])
        bd = sb("bd", [P, NC, 2 * HEADS])
        gt = sb("gt", [P, 12, NC, HEADS])
        tab = sb("tab", [P, 11, HEADS])
        taps = sb("taps", [P, 2, 3, CONV])
        acc = sb("acc", [P, 3, SEQ])
        tacc = sb("tacc", [P, 3, SEQ])
        act = sb("act", [P, 2, 3, SEQ])
        bT = sb("bT", [P, 2, 3, SEQ])
        tz = sb("tz", [P, 2, SEQ])
        gz = sb("gz", [P, 2, 2, SEQ])
        th = sb("th", [P, 2 * KT, SEQ])
        hc2 = sb("hc", [P, 2, 9])
        ssq = sb("ssq", [P, 8])
        rn2 = sb("rn", [P, 2, 4])
        dm = sb("dm", [P, 256])
        ex = sb("ex", [P, 256])
        e4 = sb("e4", [P, 512])
        kk = sb("kk", [P, NC, P])
        vb2 = sb("vb", [P, 2, NC, P])
        kdec2 = sb("kdec", [P, 2, P])
        kkT2 = sb("kkT", [P, 2, NC, P])
        la2 = sb("la", [P, 2, 4, P])
        u_tmp = sb("u_tmp", [P, NC, P])
        tu2 = sb("tu", [P, 2, 4, P])
        xl2 = sb("xl", [P, 2, NC, P])
        q1 = sb("q1", [P, 2, P])
        gza = sb("gza", [P, 2, SEQ])
        v0 = sb("v0", [P, P])
        s1 = sb("s1", [P, P])
        r1 = sb("r1", [P, P])
        qs = sb("qs", [P, P])
        v1 = sb("v1", [P, P])
        oo = sb("oo", [P, NC, P])
        junk = sb("junk", [P, 512])
        so = sb("so", [P, 8])
        on = sb("on", [P, NC, P])
        sc = sb("sc", [P, BIAS_W])
        mx = sb("mx", [P, 8])
        pt = sb("pt", [P, BIAS_W])
        vtok = sb("vtok", [P, NC, P])
        y32 = sb("y32", [P, 2, SEQ])
        y_hi = sb("y_hi", [P, 2, HEADS, SEQ], F32R)
        y_lo = sb("y_lo", [P, 2, HEADS, SEQ], F32R)
        m2, m32 = acc[:, 0:2, :], acc[:, 2, :]
        squares = th[:].rearrange("p t n -> p (t n)")[:, 0:512]
        post = bT[:].rearrange("p a t n -> p (a t n)")[:, 0:D]
        m_hi, m_lo = h_hi, h_lo
        hot, brow, rows = sc[0:BUCKETS + 1, :], pt[0:HEADS, :], r1
        bd_T = e4[0:4 * HEADS, 0:SEQ]
        bias_rows = nc.dram_tensor("bias_rows", [HEADS, P, BIAS_W + 1], F32, kind="Internal").ap()

        ident = cst[:, C_ID:C_ID + P]
        ones = cst[:, C_ONE:C_ONE + P]
        tri = cst[:, C_TRI:C_TRI + P]

        def both(col):
            return cst[:, col:col + P].rearrange("p (a n) -> p a n", a=1).to_broadcast([P, NC, P])

        s_T = sem("s_T")
        s_act = sem("s_act")
        s_bT = sem("s_bT")
        s_bd = sem("s_bd")
        s_bd_p = sem("s_bd_p")
        s_bd_w = sem("s_bd_w")
        s_bd_m = sem("s_bd_m")
        s_bd_t = sem("s_bd_t")
        s_bd_hi = sem("s_bd_hi")
        s_bd_c = sem("s_bd_c")
        s_bd_s = sem("s_bd_s")
        s_beta = sem("s_beta")
        s_bias_p = sem("s_bias_p")
        s_brow = sem("s_brow")
        s_cst = sem("s_cst")
        s_d_p = sem("s_d_p")
        s_dm = sem("s_dm")
        s_e4 = sem("s_e4")
        s_ex = sem("s_ex")
        s_f = sem("s_f")
        s_g = sem("s_g")
        s_ga = sem("s_ga")
        s_gate_th = sem("s_gate_th")
        s_gb = sem("s_gb")
        s_gc = sem("s_gc")
        s_gc_p = sem("s_gc_p")
        s_gv = sem("s_gv")
        s_gz = sem("s_gz")
        s_hT = sem("s_hT")
        s_h_hi = sem("s_h_hi")
        s_h_lo = sem("s_h_lo")
        s_hc = sem("s_hc")
        s_hi = sem("s_hi")
        s_hot = sem("s_hot")
        s_keep = sem("s_keep")
        s_kk = sem("s_kk")
        s_kkT = sem("s_kkT")
        s_ks_p = sem("s_ks_p")
        s_kt_p = sem("s_kt_p")
        s_kv = sem("s_kv")
        s_la = sem("s_la")
        s_la_p = sem("s_la_p")
        s_lo = sem("s_lo")
        s_loaded = sem("s_loaded")
        s_m2 = sem("s_m2")
        s_m32 = sem("s_m32")
        s_m_hi = sem("s_m_hi")
        s_m_lo = sem("s_m_lo")
        s_mx = sem("s_mx")
        s_nmx = sem("s_nmx")
        s_o0 = sem("s_o0")
        s_o0_p = sem("s_o0_p")
        s_o1 = sem("s_o1")
        s_o1_p = sem("s_o1_p")
        s_o_f = sem("s_o_f")
        s_o_p = sem("s_o_p")
        s_o_r = sem("s_o_r")
        s_o_sq = sem("s_o_sq")
        s_o_t = sem("s_o_t")
        s_on = sem("s_on")
        s_ot_p = sem("s_ot_p")
        s_out = sem("s_out")
        s_pexp = sem("s_pexp")
        s_pn = sem("s_pn")
        s_post = sem("s_post")
        s_pre_c = sem("s_pre_c")
        s_pre_r = sem("s_pre_r")
        s_pre_s = sem("s_pre_s")
        s_pre_sq = [sem(f"s_pre_sq{c}") for c in range(NC)]
        s_pre_x = [sem(f"s_pre_x{c}") for c in range(NC)]
        s_pt = sem("s_pt")
        s_pt_p = sem("s_pt_p")
        s_pv_p = sem("s_pv_p")
        s_qs = sem("s_qs")
        s_qs_p = sem("s_qs_p")
        s_r1 = sem("s_r1")
        s_relb = sem("s_relb")
        s_rn = sem("s_rn")
        s_root = sem("s_root")
        s_rows = sem("s_rows")
        s_rsum = sem("s_rsum")
        s_s1 = sem("s_s1")
        s_s1_p = sem("s_s1_p")
        s_sc = sem("s_sc")
        s_sc_p = sem("s_sc_p")
        s_small = sem("s_small")
        s_so = sem("s_so")
        s_q_p = sem("s_q_p")
        s_stored = sem("s_stored")
        s_t4 = sem("s_t4")
        s_tab = sem("s_tab")
        s_tanh = sem("s_tanh")
        s_tap = sem("s_tap")
        s_tap0 = sem("s_tap0")
        s_taps = sem("s_taps")
        s_tile = sem("s_tile")
        s_tt_p = sem("s_tt_p")
        s_turn = sem("s_turn")
        s_turn_p = sem("s_turn_p")
        s_tu = sem("s_tu")
        s_tz = sem("s_tz")
        s_u2 = sem("s_u2")
        s_v0 = sem("s_v0")
        s_v0_p = sem("s_v0_p")
        s_v1 = sem("s_v1")
        s_v1_p = sem("s_v1_p")
        s_vb = sem("s_vb")
        s_vec = sem("s_vec")
        s_vec_p = sem("s_vec_p")
        s_vt_p = sem("s_vt_p")
        s_vtok = sem("s_vtok")
        s_zero = sem("s_zero")
        s_x = sem("s_x")
        s_x_in = [sem(f"s_x_in{c}") for c in range(NC)]
        s_ident = sem("s_ident")
        s_norm2 = sem("s_norm2")
        s_e2 = sem("s_e2")
        s_o_w = sem("s_o_w")
        s_x_p = sem("s_x_p")
        s_ya32 = sem("s_ya32")
        s_yb32 = sem("s_yb32")
        s_yhi_a = sem("s_yhi_a")
        s_yhi_b = sem("s_yhi_b")
        s_ylo_a = sem("s_ylo_a")
        s_ylo_b = sem("s_ylo_b")
        s_raw = [sem(f"s_raw{i}") for i in range(SLOTS)]
        block = ctx.enter_context(nc.Block())

        def turned(s, h, p):
            in_b, doubling = TURNS[s]
            return h - 1 - in_b, p if in_b else 1 - p, doubling, bD if in_b else bB

        def one(a):
            return a.rearrange("p (a n) -> p a n", a=1)

        @block.sync
        def _(sp):
            for c in range(NC):
                sp.dma_start(xin[:, c, :], x[0, c * P:(c + 1) * P, :]).then_inc(s_x_in[c], 16)
            sp.dma_start(cst[:, 0:P], consts[:, 0:P]).then_inc(s_ident, 16)
            sp.dma_start(rows[0:R_GATE, :], conv_w.rearrange("k (t p) -> (k t) p", p=P)).then_inc(s_rows, 16)
            sp.dma_start(rows[R_GATE:R_PRE, :], b_gate.rearrange("(t p) -> t p", p=P)).then_inc(s_rows, 16)
            sp.dma_start(rows[R_PRE:R_ON, :], norm_pre_w.rearrange("(t p) -> t p", p=P)).then_inc(s_rows, 16)
            sp.dma_start(rows[R_ON:ROWS, :], dn_onorm_w.rearrange("(t p) -> t p", p=P)).then_inc(s_rows, 16)

            def load(n, src):
                if load.slot % 2 == 0:
                    if counts(2 * (n - SLOTS + 2)):
                        sp.wait_ge(s_lo, 2 * (n - SLOTS + 2))
                return sp.dma_start(raw[:, load.slot, :].rearrange("p (k n) -> p k n", k=src.shape[1]), src)

            def load_at(n, t, src):
                load.slot = t % SLOTS
                load(n, src).then_inc(s_raw[t % SLOTS], 16)

            def w_tile(col):
                return w_in[:, bass.ds(col, P)].rearrange("(k p) n -> p k n", p=P)

            def head_loads(h, tiles):
                for t in tiles:
                    load_at(h * PER_HEAD + t, t, w_tile(h * P + TILE_COLS[t]))

            head_loads(0, range(2))
            sp.dma_start(cst[:, P:], consts[:, P:]).then_inc(s_cst, 16)
            sp.dma_start(wbd[:], w_in[:, COL_BD:COL_B].rearrange("(k p) n -> p k n", p=P)).then_inc(s_bd_w, 16)
            sp.dma_start(alog[:], dn_a_log.rearrange("(a n) -> a n", a=1).to_broadcast([P, HEADS])).then_inc(s_small, 16)
            sp.dma_start(dtb[:], dn_dt_bias.rearrange("(a n) -> a n", a=1).to_broadcast([P, HEADS])).then_inc(s_small, 16)
            sp.dma_start(hot, onehot).then_inc(s_hot, 16)
            sp.dma_start(relb[0:BUCKETS, :], rel_bias).then_inc(s_hot, 16)
            head_loads(0, range(2, PER_HEAD))
            with sp.Fori(1, HEADS) as h:
                head_loads(h, range(PER_HEAD))
            with sp.Fori(0, 2) as i:
                for t in range(PER_HEAD):
                    load_at(GATES0 + i * PER_HEAD + t, t, w_tile(COL_GATE + (i * PER_HEAD + t) * P))
            sp.wait_ge(s_ylo_b, HEADS + 1)
            sp.dma_start(post, norm_post_w.rearrange("(a n) -> a n", a=1).to_broadcast([P, D])).then_inc(s_post, 16)
            with sp.Fori(0, KT // 2) as i:
                for t in range(4):
                    load_at(BRANCH0 + i * 4 + t, t, w_branch[t % 2][:, bass.ds((i * 2 + t // 2) * P, P)]
                            .rearrange("(k p) n -> p k n", p=P))
            for k in range(KT):
                load_at(OUT0 + k, OUT0 + k, w_out[k * P:(k + 1) * P, :].rearrange("p (k n) -> p k n", k=1))
            for c in range(NC):
                load_at(TILES + c, TILES + c, x[0, c * P:(c + 1) * P, :].rearrange("p (k n) -> p k n", k=1))
            for c in range(NC):
                for e in range(2):
                    cols = slice(512 * e, 512 * e + 512)
                    sp.wait_ge(s_o_f, 2 * c + e + 1)
                    sp.dma_start(out[0, c * P:(c + 1) * P, cols], res[:, c, cols]).then_inc(s_out, 16)
            sp.wait_ge(s_out, 32 * NC)

        @block.gpsimd
        def _(pool):
            pool.memset(relb[BUCKETS:BUCKETS + 1, :], NEG_INF).then_inc(s_relb, 1)
            pool.wait_ge(s_relb, 1)
            pool.memset(tiny[:, 8:12], -0.5).then_inc(s_pre_r, 1)
            pool.wait_ge(s_pre_r, 1)
            pool.memset(tiny[:, 12:14], EPS * P).then_inc(s_pre_c, 1)
            pool.wait_ge(s_pre_c, 1)
            pool.memset(tiny[:, 14:16], 4 * EPS).then_inc(s_pre_c, 1)
            pool.wait_ge(s_pre_c, 2)
            pool.memset(gt[:, 10], 0.5).then_inc(s_pre_c, 1)
            pool.wait_ge(s_pre_c, 3)
            for c in range(NC):
                pool.wait_ge(s_pre_sq[c], c + 1)
                if c == 1:
                    pool.tensor_tensor(tiny[:, 1:2], tiny[:, 1:2], tiny[:, 4:5], ALU.add).then_inc(s_pre_s, 1)
                    pool.wait_ge(s_pre_s, 1)
                pool.tensor_scalar(tiny[:, c:c + 1], tiny[:, c:c + 1], 1.0 / D, EPS, ALU.mult, ALU.add).then_inc(s_pre_r, 1)
                pool.wait_ge(s_pre_r, 2 * c + 2)
                pool.tensor_tensor(tiny[:, 2 + c:3 + c], tiny[:, c:c + 1], tiny[:, 8:9], ALU.pow).then_inc(s_pre_r, 1)
                pool.wait_ge(s_pre_r, 2 * c + 3)
            def front(h, p):
                if isinstance(h, int) and h == 0:
                    pool.wait_ge(s_vec, 1)
                src = vec[:, 0:R_GATE].rearrange("p (k t h) -> p t k h", k=CONV, h=HEADS)[:, :, :, bass.ds(h, 1)]
                pool.tensor_copy(taps[:, p, :, :].rearrange("p t (k a) -> p t k a", a=1), src).then_inc(s_taps, 1)
                pool.wait_ge(s_taps, h + 1)

            front(0, 0)
            pool.wait_ge(s_hi, 1)
            pool.tensor_tensor(w_lo[:, 0, D // 2:], raw[:, 0, D // 2:], w_hi[:, 0, D // 2:].bitcast(F32),
                               ALU.subtract).then_inc(s_lo, 1)
            pool.wait_ge(s_lo, 2)
            pool.wait_ge(s_hi, 2)
            pool.tensor_tensor(w_lo[:, 1, D // 2:], raw[:, 1, D // 2:], w_hi[:, 1, D // 2:].bitcast(F32),
                               ALU.subtract).then_inc(s_lo, 1)
            pool.wait_ge(s_lo, 4)
            pool.wait_ge(s_brow, 1)
            pool.dma_start(bias_rows[:, :, 0:BIAS_W],
                           brow.rearrange("h (a n) -> h a n", a=1).to_broadcast([HEADS, P, BIAS_W])).then_inc(s_stored, 16)
            pool.wait_ge(s_stored, 16)
            for c0, c1, at in ((0, 256, 0), (128, 256, 256)):
                src = bass.AP(bias_rows.tensor, P - 1 + c0, [[BIAS_W, P], [P * (BIAS_W + 1), HEADS], [1, c1 - c0]])
                pool.dma_start(bias[:, :, at:at + c1 - c0], src).then_inc(s_loaded, 16)

            def stage_a(g, p):
                hc, rn = hc2[:, p], rn2[:, p]
                if counts(g):
                    pool.wait_ge(s_ylo_a, g)
                pool.tensor_copy(hc.rearrange("p (k a) -> p k a", a=1), tab[:, 0:9, bass.ds(g, 1)]).then_inc(s_hc, 1)
                pool.wait_ge(s_hc, g + 1)
                pool.wait_ge(s_norm2, 4 * g + 2)
                pool.tensor_tensor(ssq[:, 4:6], ssq[:, 0:2], tiny[:, 14:16], ALU.add).then_inc(s_rn, 1)
                pool.wait_ge(s_rn, 2 * g + 1)
                pool.tensor_tensor(rn[:, 0:2], ssq[:, 4:6], tiny[:, 8:10], ALU.pow).then_inc(s_rn, 1)
                pool.wait_ge(s_rn, 2 * g + 2)
                pool.wait_ge(s_ex, g + 1)
                for j in range(2):
                    pool.tensor_tensor(e4[:, 256 * j:256 * j + 256].rearrange("p (c n) -> p c n", c=NC),
                                       ex[:].rearrange("p (c n) -> p c n", c=NC), both(C_E + P * j),
                                       ALU.mult).then_inc(s_e4, 1)
                    pool.wait_ge(s_e4, 2 * g + j + 1)
                pool.wait_ge(s_norm2, 4 * g + 4)
                pool.tensor_tensor(ssq[:, 6:8], ssq[:, 2:4], tiny[:, 14:16], ALU.add).then_inc(s_e2, 1)
                pool.wait_ge(s_e2, 2 * g + 1)
                pool.tensor_tensor(rn[:, 2:4], ssq[:, 6:8], tiny[:, 12:14], ALU.mult).then_inc(s_e2, 1)
                pool.wait_ge(s_e2, 2 * g + 2)

            def stage_b(g, p):
                rn = rn2[:, p]
                pool.wait_ge(s_so, 2 * g + 2)
                pool.tensor_tensor(so[:, 2:4], so[:, 0:2], rn[:, 2:4], ALU.add).then_inc(s_f, 1)
                pool.wait_ge(s_f, 2 * g + 1)
                pool.tensor_tensor(so[:, 6:8], so[:, 2:4], tiny[:, 8:10], ALU.pow).then_inc(s_f, 1)
                pool.wait_ge(s_f, 2 * g + 2)

            pool.wait_ge(s_beta, 1)
            pool.tensor_tensor(tab[:, 0:2, :], gt[:, 11], gt[:, 10], ALU.pow).then_inc(s_root, 1)
            pool.wait_ge(s_root, 1)
            pool.tensor_tensor(tab[:, 2:4, :], tab[:, 0:2, :], gt[:, 10], ALU.mult).then_inc(s_root, 1)
            pool.wait_ge(s_root, 2)
            front(1, 1)
            pool.wait_ge(s_tab, 3)
            stage_a(0, 0)
            with pool.Fori(2, HEADS - 1, 2) as h:
                front(h, 0)
                stage_a(h - 1, 1)
                stage_b(h - 2, 0)
                front(h + 1, 1)
                stage_a(h, 0)
                stage_b(h - 1, 1)
            stage_a(HEADS - 1, 1)
            stage_b(HEADS - 2, 0)
            stage_b(HEADS - 1, 1)
            for c in range(NC):
                pool.wait_ge(s_o_sq, 2 * c + 1)
                pool.tensor_tensor(tiny[:, 28 + c:29 + c], tiny[:, 24 + 2 * c:25 + 2 * c], tiny[:, 14:15],
                                   ALU.add).then_inc(s_o_t, 1)
                pool.wait_ge(s_o_t, 2 * c + 1)
                pool.wait_ge(s_o_sq, 2 * c + 2)
                pool.tensor_tensor(tiny[:, 28 + c:29 + c], tiny[:, 28 + c:29 + c],
                                   tiny[:, 25 + 2 * c:26 + 2 * c], ALU.add).then_inc(s_o_t, 1)
                pool.wait_ge(s_o_t, 2 * c + 2)
                pool.tensor_tensor(tiny[:, 30 + c:31 + c], tiny[:, 28 + c:29 + c], tiny[:, 8:9],
                                   ALU.pow).then_inc(s_o_r, 1)
                pool.wait_ge(s_o_r, c + 1)

        @block.scalar
        def _(sa):
            ac = nc.scalar.activation

            def split_hi(n, t):
                sa.wait_ge(s_raw[t % SLOTS], 16 * (n // SLOTS + 1) if isinstance(n, int) else split_hi.turn)
                if counts(n - SLOTS + 1):
                    sa.wait_ge(s_tile, n - SLOTS + 1)
                nc.scalar.copy(w_hi[:, t % SLOTS, :], raw[:, t % SLOTS, :]).then_inc(s_hi, 1)

            def lead(h, t):
                split_hi.turn = 16 * (h * (PER_HEAD // SLOTS) + (t + LEAD) // SLOTS + 1)
                split_hi(h * PER_HEAD + t + LEAD, t + LEAD)

            sa.wait_ge(s_x_in[0], 16)
            ac(bias[:].rearrange("p h n -> p (h n)")[:, 0:D], xin[:, 0, :], ACT.Square,
               accum_out=tiny[:, 0:1]).then_inc(s_pre_sq[0], 1)
            sa.wait_ge(s_x_in[1], 16)
            ac(bias[:].rearrange("p h n -> p (h n)")[:, D:D + D // 2], xin[:, 1, 0:D // 2], ACT.Square,
               accum_out=tiny[:, 1:2]).then_inc(s_pre_sq[1], 1)
            sa.wait_ge(s_pre_r, 3)
            ac(xn[:, 0, :], xin[:, 0, :], ACT.Copy, scale=tiny[:, 2:3]).then_inc(s_pre_x[0], 1)
            sa.wait_ge(s_vec, 2)
            split_hi(0, 0)
            for k in range(KT):
                sa.wait_ge(s_hT, k + 1)
                ac(h_hi[:, k, :], bank[k][:, 0:SEQ], ACT.Copy, scale=vec[:, R_PRE + k:R_PRE + k + 1]).then_inc(s_h_hi, 1)
            split_hi(1, 1)
            sa.wait_ge(s_bd_w, 16)
            nc.scalar.copy(wbd2[:, :, 0:2 * HEADS], wbd[:]).then_inc(s_bd_hi, 1)

            def gates(part):
                if part == 0:
                    sa.wait_ge(s_bd, 1)
                    ac(gt[:, 0], bd[:, :, 0:HEADS], ACT.Tanh, scale=0.5).then_inc(s_ga, 1)
                    sa.wait_ge(s_gv, 2)
                    ac(gt[:, 2], gt[:, 1], ACT.Abs).then_inc(s_ga, 1)
                    sa.wait_ge(s_ga, 2)
                    ac(gt[:, 3], gt[:, 2], ACT.Exp, scale=-1.0).then_inc(s_ga, 1)
                    sa.wait_ge(s_small, 32)
                    ac(tiny[:, 16:24], alog[:], ACT.Exp).then_inc(s_ga, 1)
                elif part == 1:
                    sa.wait_ge(s_gv, 3)
                    ac(gt[:, 5], gt[:, 4], ACT.Ln).then_inc(s_ga, 1)
                else:
                    sa.wait_ge(s_gc, 2)
                    ac(tab[:, 7, :], tab[:, 5, :], ACT.Exp).then_inc(s_tab, 1)
                    ac(tab[:, 8, :], gt[:, 9, 0], ACT.Exp).then_inc(s_tab, 1)

            def front(h, p, t):
                ps = bank[t % 2][:, 0:SEQ]
                sa.wait_ge(s_tile, h * PER_HEAD + t + 1)
                if t < 3:
                    w = (1, 0, 2)[t]
                    if t == 0:
                        sa.wait_ge(s_taps, h + 1)
                        if counts(h):
                            sa.wait_ge(s_act, h)
                    ac(acc[:, t, :], ps, ACT.Copy, scale=taps[:, p, w, CONV - 1:CONV]).then_inc(s_tap0, 1)
                elif t < 6:
                    if t == 3:
                        if counts(h):
                            sa.wait_ge(s_ylo_b, h)
                    nc.scalar.copy(bT[:, p, t - 3, :], ps).then_inc(s_bT, 1)
                else:
                    if counts(2 * (h - 1) + t - 5):
                        sa.wait_ge(s_gz, 2 * (h - 1) + t - 5)
                    ac(tz[:, t - 6, :], ps, ACT.Tanh, scale=0.5).then_inc(s_tz, 1)

            def silu_tanh(h):
                sa.wait_ge(s_tap, 9 * h + 9)
                ac(tacc[:], acc[:], ACT.Tanh, scale=0.5).then_inc(s_tanh, 1)

            def gate_front(i, t):
                sa.wait_ge(s_tile, GATES0 + i * PER_HEAD + t + 1)
                g = i * PER_HEAD + t
                ac(th[:, g, :], bank[t % 2][:, 0:SEQ], ACT.Tanh, scale=0.5,
                   bias=vec_half[:, R_GATE + g:R_GATE + g + 1]).then_inc(s_gate_th, 1)

            def stage_a(g, p, s):
                hc, vb, kdec, kkT, tu = hc2[:, p], vb2[:, p], kdec2[:, p], kkT2[:, p], tu2[:, p]
                if s == 0:
                    sa.wait_ge(s_kv, g + 1)
                    for j in range(2 * NC):
                        if j == NC:
                            sa.wait_ge(s_q_p, g + 1)
                            if counts(g):
                                sa.wait_ge(s_e2, 2 * g)
                        ac(junk[:, 0:P], (bA if j < NC else bC)[:, P * (j % NC):P * (j % NC) + P], ACT.Square,
                           accum_out=ssq[:, j:j + 1]).then_inc(s_norm2, 1)
                        sa.wait_ge(s_norm2, 4 * g + j + 1)
                    if counts(g):
                        sa.wait_ge(s_ylo_a, g)
                    sa.wait_ge(s_gz, 2 * g + 1)
                    nc.scalar.copy(q1[:, p, :], act[:, p, 1, P:2 * P]).then_inc(s_keep, 1)
                    nc.scalar.copy(gza[:, p, :], gz[:, p, 0, :]).then_inc(s_keep, 1)
                    sa.wait_ge(s_dm, 2 * g + 2)
                    ac(ex[:], dm[:], ACT.Exp).then_inc(s_ex, 1)
                elif s == 1:
                    sa.wait_ge(s_vt_p, g + 1)
                    nc.scalar.copy(vtok[:], bB[:, 0:256].rearrange("p (c n) -> p c n", c=NC)).then_inc(s_vtok, 1)
                    sa.wait_ge(s_kk, 2 * g + 2)
                    for c in range(NC):
                        ac(vb[:, c, :], bA[:, 256 + P * c:384 + P * c], ACT.Copy, scale=hc[:, 2 + c:3 + c]) \
                            .then_inc(s_vb, 1)
                    ac(kdec, kk[:, 0, :], ACT.Copy, scale=hc[:, 8:9]).then_inc(s_vb, 1)
                elif s == 2:
                    sa.wait_ge(s_kt_p, g + 1)
                    nc.scalar.copy(kkT, bB[:, 0:256].rearrange("p (c n) -> p c n", c=NC)).then_inc(s_kkT, 1)
                    sa.wait_ge(s_nmx, g + 1)
                    ac(sc[:, 0:256], sc[:, 0:256], ACT.Exp, bias=mx[:, 2:3], accum_out=mx[:, 4:5]).then_inc(s_pexp, 1)
                    ac(sc[:, 256:384], sc[:, 256:384], ACT.Exp, bias=mx[:, 3:4],
                       accum_out=mx[:, 5:6]).then_inc(s_pexp, 1)
                elif s == 3:
                    sa.wait_ge(s_rsum, g + 1)
                    ac(sc[:, 0:256], sc[:, 0:256], ACT.Copy, scale=mx[:, 6:7]).then_inc(s_pn, 1)
                    ac(sc[:, 256:384], sc[:, 256:384], ACT.Copy, scale=mx[:, 7:8]).then_inc(s_pn, 1)
                elif s == 4:
                    sa.wait_ge(s_tt_p, g + 1)
                    nc.scalar.copy(tu[:, 0:2, :], bB[:, 0:256].rearrange("p (c n) -> p c n", c=NC)).then_inc(s_T, 1)
                    sa.wait_ge(s_pt_p, g + 1)
                    nc.scalar.copy(pt[:], bC[:, 0:BIAS_W]).then_inc(s_pt, 1)
                elif s == 6:
                    sa.wait_ge(s_yb32, g + 1)
                    nc.scalar.copy(y_hi[:, 1, bass.ds(g, 1), :], one(y32[:, 1, :])).then_inc(s_yhi_b, 1)

            def turn(g, p, lv, x_bank):
                sa.wait_ge(s_turn_p, 4 * g + lv + 1)
                nc.scalar.copy(tu2[:, p, 0:2, :], x_bank[:, 256:512].rearrange("p (c n) -> p c n", c=NC)).then_inc(s_turn, 1)

            def stage_b(g, p, s):
                hc = hc2[:, p]
                if s == 5:
                    sa.wait_ge(s_v0_p, g + 1)
                    nc.scalar.copy(v0[:], bD[:, 0:P]).then_inc(s_v0, 1)
                elif s == 6:
                    sa.wait_ge(s_s1_p, g + 1)
                    nc.scalar.copy(s1[:], bE[:, 0:P]).then_inc(s_s1, 1)
                elif s == 7:
                    sa.wait_ge(s_qs_p, g + 1)
                    ac(qs[:], bD[:, P:2 * P], ACT.Copy, scale=hc[:, 7:8]).then_inc(s_qs, 1)
                    sa.wait_ge(s_o0, g + 1)
                    ac(junk[:, 0:P], oo[:, 0, :], ACT.Square, scale=P ** -0.5, accum_out=so[:, 0:1]).then_inc(s_so, 1)
                elif s == 8:
                    sa.wait_ge(s_v1_p, g + 1)
                    nc.scalar.copy(v1[:], bE[:, 0:P]).then_inc(s_v1, 1)
                elif s == 9:
                    sa.wait_ge(s_o1, g + 1)
                    ac(junk[:, P:2 * P], oo[:, 1, :], ACT.Square, scale=P ** -0.5,
                       accum_out=so[:, 1:2]).then_inc(s_so, 1)
                elif s == 10:
                    sa.wait_ge(s_f, 2 * g + 2)
                    for c in range(NC):
                        ac(on[:, c, :], oo[:, c, :], ACT.Copy, scale=so[:, 6 + c:7 + c]).then_inc(s_on, 1)
                elif s == 11:
                    sa.wait_ge(s_ya32, g + 1)
                    nc.scalar.copy(y_hi[:, 0, bass.ds(g, 1), :], one(y32[:, 0, :])).then_inc(s_yhi_a, 1)

            def iteration(h, p, stages):
                for t in range(PER_HEAD):
                    for s in range(3 * t, 3 * t + 3):
                        if s % 3 == 1:
                            lead(h, t)
                        if s in (7, 13, 21) and stages == 0:
                            gates((7, 13, 21).index(s))
                        if s == 2 and stages == 2:
                            turn(*turned(s, h, p))
                        if s % 2 == 0 and stages >= 1:
                            stage_a(h - 1, 1 - p, s // 2)
                        elif s % 2 and stages == 2:
                            stage_b(h - 2, p, s // 2)
                        if s in TURNS and s != 2 and stages >= 1 + TURNS[s][0]:
                            turn(*turned(s, h, p))
                        if s % 3 == 0 and t >= 1:
                            front(h, p, t - 1)
                        if s == 11:
                            silu_tanh(h)
                front(h, p, PER_HEAD - 1)

            iteration(0, 0, 0)
            iteration(1, 1, 1)
            with sa.Fori(2, HEADS - 1, 2) as h:
                iteration(h, 0, 2)
                iteration(h + 1, 1, 2)
            for i in range(2):
                for t in range(PER_HEAD):
                    for s in range(3 * t, 3 * t + 3):
                        if s % 3 == 1:
                            lead(HEADS + i, t)
                        if s == 2:
                            turn(*turned(s, HEADS + i, i))
                        if s % 2 == 0 and i == 0:
                            stage_a(HEADS - 1, 1, s // 2)
                        elif s % 2:
                            stage_b(HEADS - 2 + i, i, s // 2)
                        if s in TURNS and s != 2 and (TURNS[s][0] or i == 0):
                            turn(*turned(s, HEADS + i, i))
                        if s % 3 == 0 and t >= 1:
                            gate_front(i, t - 1)
                gate_front(i, PER_HEAD - 1)

            sa.sem_inc(s_m_hi, 1)
            with sa.Fori(0, KT // 2) as i:
                for t in range(4):
                    n = BRANCH0 + i * 4 + t + LEAD
                    split_hi.turn = 16 * (BRANCH0 // SLOTS + i + (t + LEAD) // SLOTS + 1)
                    split_hi(n, t + LEAD)
                    if t % 2:
                        d = i * 2 + t // 2
                        sa.wait_ge(s_m32, d + 2)
                        nc.scalar.copy(m_hi[:, bass.ds(d, 1), :], m32.rearrange("p (a n) -> p a n", a=1)).then_inc(s_m_hi, 1)
            for k in range(KT - LEAD):
                split_hi(OUT0 + k + LEAD, k + LEAD)
            for b in range(2 * NC):
                sa.wait_ge(s_o_p, b + 1)
                ac(squares, bank[2 + b], ACT.Square, scale=D ** -0.5,
                   accum_out=tiny[:, 24 + b:25 + b]).then_inc(s_o_sq, 1)
                sa.wait_ge(s_o_sq, b + 1)

        @block.vector
        def _(ve):
            v = nc.vector

            def split_lo(n, t, part):
                ve.wait_ge(s_hi, n + 1)
                if part == 0:
                    if counts(n - SLOTS + 1):
                        ve.wait_ge(s_tile, n - SLOTS + 1)
                half = slice(part * (D // 2), (part + 1) * (D // 2))
                v.tensor_tensor(w_lo[:, t % SLOTS, half], raw[:, t % SLOTS, half],
                                w_hi[:, t % SLOTS, half].bitcast(F32), ALU.subtract).then_inc(s_lo, 1)

            def lead(h, t, part):
                split_lo(h * PER_HEAD + t + LEAD, t + LEAD, part)

            v.memset(acc[:, 0, :], 0.0).then_inc(s_zero, 1)
            ve.wait_ge(s_x_in[1], 16)
            v.tensor_tensor_reduce(bias[:].rearrange("p h n -> p (h n)")[:, D + D // 2:2 * D], xin[:, 1, D // 2:],
                                   xin[:, 1, D // 2:], 1.0, 0.0, ALU.mult, ALU.add, tiny[:, 4:5]).then_inc(s_pre_sq[1], 1)
            ve.wait_ge(s_vec_p, 1)
            v.tensor_copy(vec[:], bank[7][:, 0:ROWS]).then_inc(s_vec, 1)
            ve.wait_ge(s_vec, 1)
            v.tensor_scalar(vec_half[:], vec[:], 0.5, None, ALU.mult).then_inc(s_vec, 1)
            ve.wait_ge(s_pre_r, 5)
            v.tensor_scalar(xn[:, 1, :], xin[:, 1, :], tiny[:, 3:4], None, ALU.mult).then_inc(s_pre_x[1], 1)
            split_lo(0, 0, 0)
            for k in range(KT):
                ve.wait_ge(s_h_hi, k + 1)
                v.scalar_tensor_tensor(out=h_lo[:, k, :], in0=bank[k][:, 0:SEQ], scalar=vec[:, R_PRE + k:R_PRE + k + 1],
                                       in1=h_hi[:, k, :].bitcast(F32), op0=ALU.mult, op1=ALU.subtract).then_inc(s_h_lo, 1)
            ve.wait_ge(s_lo, 2)
            split_lo(1, 1, 0)
            ve.wait_ge(s_bd_hi, 1)
            v.tensor_tensor(wbd2[:, :, 2 * HEADS:], wbd[:], wbd2[:, :, 0:2 * HEADS].bitcast(F32),
                            ALU.subtract).then_inc(s_bd_s, 1)
            ve.wait_ge(s_lo, 4)

            step = [3]

            def gate_step(ins):
                step[0] += 1
                ins.then_inc(s_gv, 1)
                ve.wait_ge(s_gv, step[0])

            def gates(part):
                if part == 0:
                    ve.wait_ge(s_bias_p, 1)
                    v.tensor_copy(brow, bank[3][0:HEADS, 0:BIAS_W]).then_inc(s_brow, 1)
                    ve.wait_ge(s_bd_p, 1)
                    sums = bank[2][:, 0:4 * NC * HEADS].rearrange("p (c n) -> p c n", c=NC)
                    v.tensor_copy(bd_lo[:], sums[:, :, 2 * HEADS:]).then_inc(s_bd_c, 1)
                    ve.wait_ge(s_bd_c, 1)
                    v.tensor_tensor(bd[:], sums[:, :, 0:2 * HEADS], bd_lo[:], ALU.add).then_inc(s_bd, 1)
                    ve.wait_ge(s_bd, 1)
                    ve.wait_ge(s_small, 32)
                    for c in range(NC):
                        v.tensor_tensor(gt[:, 1, c], bd[:, c, HEADS:], dtb[:], ALU.add).then_inc(s_gv, 1)
                elif part == 1:
                    ve.wait_ge(s_ga, 3)
                    v.tensor_scalar(gt[:, 11], gt[:, 0], 0.5, 0.5, ALU.mult, ALU.add).then_inc(s_beta, 1)
                    v.tensor_scalar(gt[:, 4], gt[:, 3], 1.0, None, ALU.add).then_inc(s_gv, 1)
                elif part == 2:
                    ve.wait_ge(s_ga, 5)
                    ve.wait_ge(s_gv, 3)
                    gate_step(v.tensor_scalar(gt[:, 6], gt[:, 4], -1.0, None, ALU.add))
                    gate_step(v.tensor_scalar(gt[:, 7], gt[:, 6], 0.0, None, ALU.is_equal))
                    gate_step(v.tensor_tensor(gt[:, 6], gt[:, 6], gt[:, 7], ALU.add))
                    gate_step(v.tensor_tensor(gt[:, 5], gt[:, 5], gt[:, 7], ALU.add))
                    gate_step(v.reciprocal(gt[:, 6], gt[:, 6]))
                    gate_step(v.tensor_tensor(gt[:, 5], gt[:, 5], gt[:, 3], ALU.mult))
                    gate_step(v.tensor_tensor(gt[:, 5], gt[:, 5], gt[:, 6], ALU.mult))
                    gate_step(v.scalar_tensor_tensor(out=gt[:, 8], in0=gt[:, 1], scalar=0.0, in1=gt[:, 5],
                                                     op0=ALU.max, op1=ALU.add))
                    for c in range(NC):
                        v.scalar_tensor_tensor(out=tab[:, 9 + c, :], in0=gt[:, 8, c], scalar=-1.0,
                                               in1=tiny[:, 16:24], op0=ALU.mult, op1=ALU.mult).then_inc(s_g, 1)
                elif part == 3:
                    ve.wait_ge(s_gc_p, 1)
                    v.tensor_copy(tab[:, 4:6, :], bC[:, 0:16].rearrange("p (c n) -> p c n", c=NC)).then_inc(s_gc, 1)
                    ve.wait_ge(s_gc, 1)
                    v.tensor_tensor(gt[:, 9, 0], bC[:, 16:24], tab[:, 4, :], ALU.subtract).then_inc(s_gc, 1)
                else:
                    ve.wait_ge(s_tab, 2)
                    v.tensor_scalar(tab[:, 6, :], tab[:, 7, :], -1.0, None, ALU.mult).then_inc(s_tab, 1)
                    ve.wait_ge(s_loaded, 32)
                    ve.sem_inc(s_ylo_a, 1)
                    ve.sem_inc(s_ylo_b, 1)

            def front(h, p, t, part):
                ps = bank[t % 2]
                if t < 3:
                    w = (1, 0, 2)[t]
                    if part == 0:
                        ve.wait_ge(s_tap0, 3 * h + t + 1)
                    for i in ((1, 2), (3,))[part]:
                        if i > 1:
                            ve.wait_ge(s_tap, 9 * h + 3 * t + i - 1)
                        v.scalar_tensor_tensor(out=acc[:, t, i:], in0=ps[:, 0:SEQ - i],
                                               scalar=taps[:, p, w, CONV - 1 - i:CONV - i], in1=acc[:, t, i:],
                                               op0=ALU.mult, op1=ALU.add).then_inc(s_tap, 1)
                elif part == 0 and t == 3:
                    ve.wait_ge(s_tanh, h + 1)
                    if counts(h - 1):
                        ve.wait_ge(s_la_p, h - 1)
                        ve.wait_ge(s_keep, 2 * (h - 1))
                    v.scalar_tensor_tensor(out=act[:, p], in0=tacc[:], scalar=1.0, in1=acc[:], op0=ALU.add,
                                           op1=ALU.mult).then_inc(s_act, 1)
                elif part == 0 and t >= 6:
                    ve.wait_ge(s_tz, 2 * h + t - 5)
                    v.scalar_tensor_tensor(out=gz[:, p, t - 6, :], in0=tz[:, t - 6, :], scalar=1.0, in1=ps[:, 0:SEQ],
                                           op0=ALU.add, op1=ALU.mult).then_inc(s_gz, 1)

            def stage_a(g, p, s):
                hc, rn, la, tu, xl = hc2[:, p], rn2[:, p], la2[:, p], tu2[:, p], xl2[:, p]
                if s == 0:
                    ve.wait_ge(s_gb, g + 1)
                    for c in range(NC):
                        v.tensor_scalar(dm[:, P * c:P * c + P], bB[:, P * c:P * c + P], hc[:, 4 + c:5 + c], 0.0,
                                        ALU.subtract, ALU.min).then_inc(s_dm, 1)
                elif s == 1:
                    ve.wait_ge(s_rn, 2 * g + 2)
                    for c in range(NC):
                        v.tensor_scalar(kk[:, c, :], bA[:, P * c:P * c + P], rn[:, c:c + 1], hc[:, c:c + 1],
                                        ALU.mult, ALU.mult).then_inc(s_kk, 1)
                    ve.wait_ge(s_sc_p, g + 1)
                    v.scalar_tensor_tensor(out=sc[:], in0=bC[:, 0:BIAS_W], scalar=SCALE,
                                           in1=bias[:, bass.ds(g, 1), :].rearrange("p a n -> p (a n)"),
                                           op0=ALU.mult, op1=ALU.add).then_inc(s_sc, 1)
                    ve.wait_ge(s_sc, g + 1)
                    v.tensor_reduce(mx[:, 0:1], sc[:, 0:256], AX_X, ALU.max).then_inc(s_mx, 1)
                    v.tensor_reduce(mx[:, 1:2], sc[:, 256:384], AX_X, ALU.max).then_inc(s_mx, 1)
                    ve.wait_ge(s_mx, 2 * g + 2)
                    v.tensor_scalar(mx[:, 2:4], mx[:, 0:2], -1.0, None, ALU.mult).then_inc(s_nmx, 1)
                elif s == 3:
                    ve.wait_ge(s_pexp, 2 * g + 2)
                    v.reciprocal(mx[:, 6:8], mx[:, 4:6]).then_inc(s_rsum, 1)
                    ve.wait_ge(s_la_p, g + 1)
                    ve.wait_ge(s_e4, 2 * g + 2)
                    flat = la.rearrange("p c n -> p (c n)")
                    v.tensor_tensor(flat[:, 0:256], bA[:, 0:256], e4[:, 0:256], ALU.mult).then_inc(s_la, 1)
                    ve.wait_ge(s_la, 2 * g + 1)
                    v.tensor_tensor(u_tmp[:], la[:, 0:2, :], both(C_M1), ALU.mult).then_inc(s_u2, 1)
                    ve.wait_ge(s_u2, 2 * g + 1)
                    v.tensor_tensor(tu[:, 2:4, :], both(C_ID), u_tmp[:], ALU.subtract).then_inc(s_u2, 1)
                elif s == 4:
                    flat = la.rearrange("p c n -> p (c n)")
                    v.tensor_tensor(flat[:, 256:512], bA[:, 256:512], e4[:, 256:512], ALU.mult).then_inc(s_la, 1)
                elif s >= 5:
                    level_step(g, p, (s - 5) // 2, s % 2 == 1, bB, bC)
                    if s == 5:
                        ve.wait_ge(s_pv_p, g + 1)
                        v.scalar_tensor_tensor(out=y32[:, 1, :], in0=bA[:, 0:SEQ], scalar=0.5, in1=gz[:, p, 1, :],
                                               op0=ALU.mult, op1=ALU.mult).then_inc(s_yb32, 1)
                    if s == 7:
                        ve.wait_ge(s_yhi_b, g + 1)
                        v.tensor_tensor(y_lo[:, 1, bass.ds(g, 1), :], one(y32[:, 1, :]),
                                        y_hi[:, 1, bass.ds(g, 1), :].bitcast(F32), ALU.subtract).then_inc(s_ylo_b, 1)

            def level_step(g, p, lv, first, x_bank, d_bank):
                tu, xl = tu2[:, p], xl2[:, p]
                if first:
                    ve.wait_ge(s_x_p, 6 * g + lv + 1)
                    w = P if lv < 5 else HALF
                    v.tensor_tensor(xl[:, :, 0:w], x_bank[:, 0:NC * w].rearrange("p (c n) -> p c n", c=NC),
                                    both(C_ML + P * lv)[:, :, 0:w], ALU.mult).then_inc(s_x, 1)
                else:
                    ve.wait_ge(s_d_p, 6 * g + lv + 1)
                    if lv < 4:
                        view, product = tu[:, 2:4, :].rearrange("p c n -> p (c n)"), d_bank[:, 256:512]
                    elif lv == 4:
                        view = tu[0:HALF, 0:2, 0:HALF]
                        product = d_bank[0:HALF, 0:NC * HALF].rearrange("p (c n) -> p c n", c=NC)
                        v.tensor_tensor(view, view, product, ALU.subtract).then_inc(s_t4, 1)
                        view, product = tu[:, 2:4, :].rearrange("p c n -> p (c n)"), d_bank[:, 256:512]
                    else:
                        view = tu[0:HALF, 2:4, HALF:]
                        product = d_bank[0:HALF, 0:NC * HALF].rearrange("p (c n) -> p c n", c=NC)
                    v.tensor_tensor(view, view, product, ALU.subtract).then_inc(s_tu, 1)

            def stage_b(g, p, s):
                hc, vb = hc2[:, p], vb2[:, p]
                if s < 5:
                    level_step(g, p, 3 + (s + 1) // 2, s % 2 == 1, bD, bE)
                elif s == 6:
                    ve.wait_ge(s_o0_p, g + 1)
                    v.tensor_copy(oo[:, 0, :], bF[:, 0:P]).then_inc(s_o0, 1)
                elif s == 7:
                    ve.wait_ge(s_ks_p, g + 1)
                    v.scalar_tensor_tensor(out=r1[:], in0=bE[:, 256:384], scalar=hc[:, 6:7], in1=vb[:, 1, :],
                                           op0=ALU.mult, op1=ALU.add).then_inc(s_r1, 1)
                elif s == 9:
                    ve.wait_ge(s_o1_p, g + 1)
                    ve.wait_ge(s_qs, g + 1)
                    v.tensor_tensor(oo[:, 1, :], bF[:, P:2 * P], qs[:], ALU.add).then_inc(s_o1, 1)
                elif s == 10:
                    ve.wait_ge(s_ot_p, g + 1)
                    v.scalar_tensor_tensor(out=y32[:, 0, :], in0=bD[:, 0:SEQ], scalar=vec_half[:, R_ON:R_ON + 1],
                                           in1=gza[:, p, :], op0=ALU.mult, op1=ALU.mult).then_inc(s_ya32, 1)
                elif s == 11:
                    ve.wait_ge(s_yhi_a, g + 1)
                    v.tensor_tensor(y_lo[:, 0, bass.ds(g, 1), :], one(y32[:, 0, :]),
                                    y_hi[:, 0, bass.ds(g, 1), :].bitcast(F32), ALU.subtract).then_inc(s_ylo_a, 1)

            def iteration(h, p, stages):
                for t in range(PER_HEAD):
                    for s in range(3 * t, 3 * t + 3):
                        if s == 4 and stages == 0:
                            ve.wait_ge(s_bd_m, 1)
                            v.tensor_copy(bd_T, bank[2][0:4 * HEADS, 0:SEQ]).then_inc(s_bd_t, 1)
                        if s in (6, 9, 16, 21, 22) and stages == 0:
                            gates((6, 9, 16, 21, 22).index(s))
                        if s % 2 == 0 and stages >= 1:
                            stage_a(h - 1, 1 - p, s // 2)
                        elif s % 2 and stages == 2:
                            stage_b(h - 2, p, s // 2)
                        if s % 3 <= 1 and t >= 1:
                            front(h, p, t - 1, s % 3)
                        if s % 3 >= 1:
                            lead(h, t, s % 3 - 1)
                front(h, p, PER_HEAD - 1, 0)

            iteration(0, 0, 0)
            iteration(1, 1, 1)
            with ve.Fori(2, HEADS - 1, 2) as h:
                iteration(h, 0, 2)
                iteration(h + 1, 1, 2)
            for i in range(2):
                for t in range(PER_HEAD):
                    for s in range(3 * t, 3 * t + 3):
                        if s % 2 == 0 and i == 0:
                            stage_a(HEADS - 1, 1, s // 2)
                        elif s % 2:
                            stage_b(HEADS - 2 + i, i, s // 2)
                        if s % 3 >= 1:
                            lead(HEADS + i, t, s % 3 - 1)

            ve.sem_inc(s_m32, 1)
            ve.sem_inc(s_m2, 2)
            with ve.Fori(0, KT // 2) as i:
                for t in range(4):
                    for part in range(2):
                        split_lo(BRANCH0 + i * 4 + t + LEAD, t + LEAD, part)
                    d = i * 2 + t // 2
                    ve.wait_ge(s_tile, BRANCH0 + i * 4 + t + 1)
                    if t % 2 == 0:
                        ve.wait_ge(s_m_hi, d + 1)
                    v.scalar_tensor_tensor(out=one(m2[:, t % 2, :]), in0=th[:, bass.ds((t % 2) * KT + d, 1), :], scalar=1.0,
                                           in1=one(bank[t % 2][:, 0:SEQ]), op0=ALU.add, op1=ALU.mult).then_inc(s_m2, 1)
                    if t % 2:
                        ve.wait_ge(s_m2, 2 * (d + 2))
                        v.tensor_tensor(m32, m2[:, 0, :], m2[:, 1, :], ALU.add).then_inc(s_m32, 1)
                        ve.wait_ge(s_m_hi, d + 2)
                        v.tensor_tensor(m_lo[:, bass.ds(d, 1), :], one(m32), m_hi[:, bass.ds(d, 1), :].bitcast(F32),
                                        ALU.subtract).then_inc(s_m_lo, 1)
            for k in range(KT - LEAD):
                for part in range(2):
                    split_lo(OUT0 + k + LEAD, k + LEAD, part)
            ve.wait_ge(s_post, 16)
            for c in range(NC):
                for e in range(2):
                    cols = slice(512 * e, 512 * e + 512)
                    ve.wait_ge(s_o_sq, 2 * c + e + 1)
                    v.tensor_tensor(res[:, c, cols], bank[2 + 2 * c + e], post[:, cols], ALU.mult).then_inc(s_o_w, 1)
                ve.wait_ge(s_o_w, 2 * c + 2)
                ve.wait_ge(s_o_r, c + 1)
                ve.wait_ge(s_raw[c], 16 * (TILES // SLOTS + 1))
                for e in range(2):
                    cols = slice(512 * e, 512 * e + 512)
                    v.scalar_tensor_tensor(out=res[:, c, cols], in0=res[:, c, cols], scalar=tiny[:, 30 + c:31 + c],
                                           in1=raw[:, c, cols], op0=ALU.mult, op1=ALU.add).then_inc(s_o_f, 1)

        @block.tensor
        def _(pe):
            mm = nc.tensor.matmul
            tp = nc.tensor.transpose

            pe.wait_ge(s_zero, 1)
            for n in range(WARM):
                if n == WARM - 3:
                    pe.wait_ge(s_rows, 64)
                    pe.wait_ge(s_ident, 16)
                    tp(bank[7][:, 0:ROWS], rows[0:ROWS, :], ident[0:ROWS, 0:ROWS]).then_inc(s_vec_p, 1)
                mm(bank[6][:, 0:SEQ], acc[:, 0, 0:P], acc[:, 0, :], start=True, stop=True)
            for c in range(NC):
                pe.wait_ge(s_pre_x[c], 1)
            for k in range(KT):
                if k == 7:
                    pe.wait_ge(s_vec, 1)
                for c in range(NC):
                    last = tp(bank[k][:, P * c:P * c + P], xn[:, c, P * k:P * k + P], ident)
                last.then_inc(s_hT, 1)

            def gates(part):
                if part == 0:
                    pe.wait_ge(s_bd_s, 1)
                    for k in range(KT):
                        for h_part in (h_hi, h_lo):
                            last = mm(bank[2][0:4 * HEADS, 0:SEQ], wbd2[:, k, :], h_part[:, k, :],
                                      start=k == 0 and h_part is h_hi, stop=k == KT - 1 and h_part is h_lo)
                    last.then_inc(s_bd_m, 1)
                elif part == 1:
                    pe.wait_ge(s_bd_t, 1)
                    for c in range(NC):
                        last = tp(bank[2][:, 4 * HEADS * c:4 * HEADS * (c + 1)], bd_T[:, P * c:P * c + P],
                                  ident[0:4 * HEADS, 0:4 * HEADS])
                    last.then_inc(s_bd_p, 1)
                    pe.wait_ge(s_hot, 32)
                    pe.wait_ge(s_relb, 1)
                    mm(bank[3][0:HEADS, 0:BIAS_W], relb[:], hot, start=True, stop=True).then_inc(s_bias_p, 1)
                else:
                    pe.wait_ge(s_g, 2)
                    pe.wait_ge(s_cst, 16)
                    mm(bC[:, 0:16], tri, tab[:, 9:11, :], start=True, stop=True)
                    mm(bC[:, 16:32], ones, tab[:, 9:11, :], start=True, stop=True).then_inc(s_gc_p, 1)

            def third(n, t, part, right_hi, right_lo, first_tile=False):
                ps = bank[t % 2][:, 0:SEQ]
                slot = t % SLOTS
                if part == 0:
                    pe.wait_ge(s_hi, n + 1)
                    pe.wait_ge(s_lo, 2 * n + 2)
                for i in range(8 * part, 8 * part + 8):
                    k, which = i // 3, i % 3
                    if first_tile and which == 0:
                        pe.wait_ge(s_h_lo, max(k, 1) + 1)
                    w = (w_lo if which == 2 else w_hi)[:, slot, P * k:P * k + P]
                    r = (right_lo if which == 1 else right_hi)[:, k, :]
                    last = mm(ps, w, r, start=i == 0, stop=i == 23)
                if part == 2:
                    last.then_inc(s_tile, 1)

            def bank_free(h, t):
                if t < 2:
                    if counts(2 * (h - 1) + t + 1):
                        pe.wait_ge(s_gz, 2 * (h - 1) + t + 1)
                elif t < 5:
                    pe.wait_ge(s_tap, 9 * h + 3 * (t - 1))
                else:
                    pe.wait_ge(s_bT, 3 * h + t - 4)

            def stage_a(g, p, s):
                hc, vb, kkT, la, tu = hc2[:, p], vb2[:, p], kkT2[:, p], la2[:, p], tu2[:, p]
                k_T, q_T, v_T = (act[:, p, j, :] for j in range(3))
                if s == 0:
                    pe.wait_ge(s_act, g + 1)
                    if counts(g):
                        pe.wait_ge(s_ylo_b, g + 1)
                    for j, a in enumerate((k_T, v_T)):
                        for c in range(NC):
                            last = tp(bA[:, 256 * j + P * c:256 * j + P * c + P], a[:, P * c:P * c + P], ident)
                    last.then_inc(s_kv, 1)
                    for c in range(NC):
                        last = tp(bC[:, P * c:P * c + P], q_T[:, P * c:P * c + P], ident)
                    last.then_inc(s_q_p, 1)
                    pe.wait_ge(s_hc, g + 1)
                    if counts(g):
                        pe.wait_ge(s_x, 6 * g - 2)
                        pe.wait_ge(s_ylo_a, g)
                    for c in range(NC):
                        last = tp(bB[:, P * c:P * c + P], hc[:, 4 + c:5 + c].to_broadcast([P, P]), ident)
                    last.then_inc(s_gb, 1)
                elif s == 1:
                    pe.wait_ge(s_bT, 3 * g + 3)
                    pe.wait_ge(s_norm2, 4 * g + 4)
                    kb_T, qb_T, vb_T = (bT[:, p, j, :] for j in range(3))
                    mm(bC[:, 0:256], qb_T[:, P:2 * P], kb_T, start=True, stop=True)
                    mm(bC[:, 256:384], qb_T[:, 0:P], kb_T[:, 0:P], start=True, stop=True).then_inc(s_sc_p, 1)
                    pe.wait_ge(s_dm, 2 * g + 2)
                    for c in range(NC):
                        last = tp(bB[:, P * c:P * c + P], vb_T[:, P * c:P * c + P], ident)
                    last.then_inc(s_vt_p, 1)
                elif s == 2:
                    pe.wait_ge(s_kk, 2 * g + 2)
                    pe.wait_ge(s_vtok, g + 1)
                    for c in range(NC):
                        last = tp(bB[:, P * c:P * c + P], kk[:, c, :], ident)
                    last.then_inc(s_kt_p, 1)
                elif s == 3:
                    pe.wait_ge(s_kkT, g + 1)
                    pe.wait_ge(s_vb, 3 * g + 2)
                    for c in range(NC):
                        mm(bA[:, P * c:P * c + P], kkT[:, c, :], kkT[:, c, :], start=True, stop=True)
                    for c in range(NC):
                        last = mm(bA[:, 256 + P * c:384 + P * c], kkT[:, c, :], q_T[:, P * c:P * c + P],
                                  start=True, stop=True)
                    last.then_inc(s_la_p, 1)
                elif s == 4:
                    pe.wait_ge(s_u2, 2 * g + 2)
                    for c in range(NC):
                        last = tp(bB[:, P * c:P * c + P], tu[:, 2 + c, :], ident)
                    last.then_inc(s_tt_p, 1)
                    pe.wait_ge(s_pn, 2 * g + 2)
                    tp(bC[:, 0:P], sc[:, 256:384], ident)
                    tp(bC[:, P:2 * P], sc[:, 0:P], ident)
                    tp(bC[:, 2 * P:3 * P], sc[:, P:2 * P], ident).then_inc(s_pt_p, 1)
                else:
                    if s == 5:
                        pe.wait_ge(s_T, g + 1)
                    level_step(g, p, (s - 5) // 2, s % 2 == 1, bB, bC)
                    if s == 5:
                        pe.wait_ge(s_pt, g + 1)
                        pe.wait_ge(s_la, 2 * g + 2)
                        mm(bA[:, 0:256], vtok[:, 0, :], pt[:, 0:256], start=True, stop=False, skip_group_check=True)
                        mm(bA[:, P:2 * P], vtok[:, 1, :], pt[:, 256:384], start=False, stop=True,
                           skip_group_check=True).then_inc(s_pv_p, 1)

            def level_step(g, p, lv, first, x_bank, d_bank):
                la, tu, xl = la2[:, p], tu2[:, p], xl2[:, p]
                if first:
                    if lv == 5:
                        pe.wait_ge(s_t4, g + 1)
                    elif lv:
                        pe.wait_ge(s_turn, 4 * g + lv)
                    w = P if lv < 5 else HALF
                    for c in range(NC):
                        last = mm(x_bank[:, w * c:w * c + w], la[:, c, :], tu[:, c, 0:w], start=True, stop=True)
                    last.then_inc(s_x_p, 1)
                else:
                    pe.wait_ge(s_x, 6 * g + lv + 1)
                    if lv < 5:
                        for c in range(NC):
                            if lv == 4:
                                mm(d_bank[0:HALF, HALF * c:HALF * c + HALF], tu[:, 2 + c, 0:HALF], xl[:, c, 0:HALF],
                                   start=True, stop=True)
                        for c in range(NC):
                            last = mm(d_bank[:, 256 + P * c:384 + P * c], xl[:, c, :], tu[:, 2 + c, :],
                                      start=True, stop=True)
                    else:
                        for c in range(NC):
                            last = mm(d_bank[0:HALF, HALF * c:HALF * c + HALF], xl[:, c, 0:HALF], tu[:, 2 + c, HALF:],
                                      start=True, stop=True)
                    last.then_inc(s_d_p, 1)

            def turn(g, p, lv, x_bank):
                pe.wait_ge(s_tu, 6 * g + lv + 1)
                for c in range(NC):
                    last = tp(x_bank[:, 256 + P * c:384 + P * c], tu2[:, p, 2 + c, :], ident)
                last.then_inc(s_turn_p, 1)

            def stage_b(g, p, s):
                vb, kdec, kkT, la, tu = vb2[:, p], kdec2[:, p], kkT2[:, p], la2[:, p], tu2[:, p]
                if s < 5:
                    if s == 0:
                        pe.wait_ge(s_ylo_a, g + 1)
                    level_step(g, p, 3 + (s + 1) // 2, s % 2 == 1, bD, bE)
                elif s == 5:
                    pe.wait_ge(s_tu, 6 * g + 6)
                    mm(bD[:, 0:P], tu[:, 2, :], vb[:, 0, :], start=True, stop=True).then_inc(s_v0_p, 1)
                elif s == 6:
                    pe.wait_ge(s_v0, g + 1)
                    mm(bE[:, 0:P], kdec, v0[:], start=True, stop=True).then_inc(s_s1_p, 1)
                    mm(bF[:, 0:P], la[:, 2, :], v0[:], start=True, stop=True).then_inc(s_o0_p, 1)
                elif s == 7:
                    pe.wait_ge(s_s1, g + 1)
                    pe.wait_ge(s_keep, 2 * g + 1)
                    mm(bE[:, 256:384], kkT[:, 1, :], s1[:], start=True, stop=True).then_inc(s_ks_p, 1)
                    mm(bD[:, P:2 * P], q1[:, p, :], s1[:], start=True, stop=True).then_inc(s_qs_p, 1)
                elif s == 8:
                    pe.wait_ge(s_r1, g + 1)
                    mm(bE[:, 0:P], tu[:, 3, :], r1[:], start=True, stop=True).then_inc(s_v1_p, 1)
                elif s == 9:
                    pe.wait_ge(s_v1, g + 1)
                    pe.wait_ge(s_o0, g + 1)
                    mm(bF[:, P:2 * P], la[:, 3, :], v1[:], start=True, stop=True).then_inc(s_o1_p, 1)
                elif s == 10:
                    pe.wait_ge(s_on, 2 * g + 2)
                    for c in range(NC):
                        last = tp(bD[:, P * c:P * c + P], on[:, c, :], ident)
                    last.then_inc(s_ot_p, 1)

            def iteration(h, p, stages):
                for t in range(PER_HEAD):
                    for s in range(3 * t, 3 * t + 3):
                        if s in (3, 5, 21) and stages == 0:
                            gates((3, 5, 21).index(s))
                        late = s in LATE
                        if s in TURNS and stages >= 1 + TURNS[s][0]:
                            turn(*turned(s, h, p))
                        for products in (late, not late):
                            if products:
                                if s % 3 == 0:
                                    bank_free(h, t)
                                third(h * PER_HEAD + t, t, s % 3, h_hi, h_lo, first_tile=stages == 0 and t == 0)
                            elif s % 2 == 0 and stages >= 1:
                                stage_a(h - 1, 1 - p, s // 2)
                            elif s % 2 and stages == 2:
                                stage_b(h - 2, p, s // 2)

            iteration(0, 0, 0)
            pe.wait_ge(s_gc, 2)
            iteration(1, 1, 1)
            with pe.Fori(2, HEADS - 1, 2) as h:
                iteration(h, 0, 2)
                iteration(h + 1, 1, 2)
            for i in range(2):
                for t in range(PER_HEAD):
                    for s in range(3 * t, 3 * t + 3):
                        late = s in LATE
                        if s in TURNS and (TURNS[s][0] or i == 0):
                            turn(*turned(s, HEADS + i, i))
                        for products in (late, not late):
                            if products:
                                if s % 3 == 0:
                                    if i == 0 and t < 2:
                                        pe.wait_ge(s_gz, 2 * (HEADS - 1) + t + 1)
                                    else:
                                        pe.wait_ge(s_gate_th, PER_HEAD * i + t - 1)
                                third(GATES0 + i * PER_HEAD + t, t, s % 3, h_hi, h_lo)
                            elif s % 2 == 0 and i == 0:
                                stage_a(HEADS - 1, 1, s // 2)
                            elif s % 2:
                                stage_b(HEADS - 2 + i, i, s // 2)
            pe.wait_ge(s_ylo_b, HEADS + 1)

            with pe.Fori(0, KT // 2) as i:
                for t in range(4):
                    pe.wait_ge(s_m2, i * 4 + t + 1)
                    if t < 2:
                        pe.wait_ge(s_gate_th, 2 * KT - 1 + t)
                    for part in range(3):
                        if part == 2 and t == 0:
                            pe.wait_ge(s_ylo_a, HEADS + 1)
                        third(BRANCH0 + i * 4 + t, t, part, y_hi[:, t % 2], y_lo[:, t % 2])

            def out_products(k, c, e):
                for m, w in ((m_hi, w_hi), (m_hi, w_lo), (m_lo, w_hi)):
                    last = mm(bank[2 + 2 * c + e], m[:, k, P * c:P * c + P],
                              w[:, (OUT0 + k) % SLOTS, 512 * e:512 * e + 512],
                              start=k == 0 and m is m_hi and w is w_hi, stop=k == KT - 1 and m is m_lo)
                return last

            for k in range(KT - SLOTS):
                pe.wait_ge(s_hi, OUT0 + k + 1)
                pe.wait_ge(s_lo, 2 * (OUT0 + k) + 2)
                pe.wait_ge(s_m_lo, k + 1)
                for c in range(NC):
                    for e in range(2):
                        last = out_products(k, c, e)
                last.then_inc(s_tile, 1)
            for c in range(NC):
                for halves in ((range(2),) if c == 0 else ((0,), (1,))):
                    for k in range(KT - SLOTS, KT):
                        if c == 0:
                            pe.wait_ge(s_hi, OUT0 + k + 1)
                            pe.wait_ge(s_lo, 2 * (OUT0 + k) + 2)
                            pe.wait_ge(s_m_lo, k + 1)
                        for e in halves:
                            last = out_products(k, c, e)
                            if k == KT - 1:
                                last.then_inc(s_o_p, 1)


_INS = ['x', 'norm_pre_w', 'w_in', 'b_gate', 'conv_w', 'dn_a_log', 'dn_dt_bias', 'dn_onorm_w', 'rel_bias',
        'w_branch', 'w_out', 'norm_post_w']


def kernel(**inputs):
    import concourse.bacc as _bacc
    from concourse.bass_utils import run_bass_kernel_spmd as _run

    nc = _bacc.Bacc("TRN2", target_bir_lowering=False, num_devices=1)
    consts, onehot = shape_constants()
    arrays, args = {}, []
    for name, a in [(n, np.ascontiguousarray(inputs[n])) for n in _INS] + [("consts", consts), ("onehot", onehot)]:
        arrays[f"in_{name}_dram"] = a
        args.append(nc.dram_tensor(f"in_{name}_dram", a.shape, mybir.dt.from_np(a.dtype), kind="ExternalInput").ap())
    args.append(nc.dram_tensor("out_0_dram", (1, SEQ, D), F32, kind="ExternalOutput").ap())
    build(nc, *args)
    r = _run(nc, [arrays], core_ids=[0])
    return r.results[0]["out_0_dram"]
```
